# Optimizing a Trainium2 kernel written in Bass

```python
import jax, jax.numpy as jnp
from jax import lax
import numpy as np

D_MODEL = 1024
BATCH = 1
SEQ = 512
DEPTH = 1

HG_WIDTH = D_MODEL // 2
HG_HEAD_DIM = 128
HG_HEADS = HG_WIDTH // HG_HEAD_DIM
ML_WIDTH = D_MODEL - HG_WIDTH
ML_V_DIM = 128
ML_HEADS = ML_WIDTH // ML_V_DIM
ML_QK_DIM = ML_V_DIM // 2
D_MIX = HG_WIDTH + ML_WIDTH
CONV_WIDTH = 4
D_FF = 2816
CHUNK = 64
EPS = 1e-6
SPLIT_SIZES = (HG_WIDTH, HG_WIDTH, HG_WIDTH, HG_WIDTH,
               ML_HEADS * ML_QK_DIM, ML_HEADS * ML_QK_DIM,
               ML_WIDTH, ML_WIDTH,
               ML_HEADS, ML_HEADS)
D_IN = 4 * HG_WIDTH + 2 * ML_HEADS * ML_QK_DIM + 2 * ML_WIDTH + 2 * ML_HEADS


def rms_norm(x, g):
    xf = x.astype(jnp.float32)
    y = xf * lax.rsqrt(jnp.mean(xf * xf, axis=-1, keepdims=True) + EPS)
    return (y * g.astype(jnp.float32)).astype(x.dtype)

def swiglu_ffn(x, w_in, w_out):
    gate, up = jnp.split(x @ w_in, 2, axis=-1)
    return (jax.nn.silu(gate) * up) @ w_out

def split_cols(x, sizes):
    outs, start = [], 0
    for s in sizes:
        outs.append(x[..., start:start + s])
        start += s
    return outs

def causal_depthwise_conv(x, w, b):
    y = lax.conv_general_dilated(
        x, w[:, None, :].astype(x.dtype), window_strides=(1,),
        padding=[(CONV_WIDTH - 1, 0)], dimension_numbers=("NWC", "WIO", "NWC"),
        feature_group_count=x.shape[-1])
    return y + b.astype(x.dtype)

def to_chunks(x):
    B, T, H, d = x.shape
    return x.reshape(B, T // CHUNK, CHUNK, H, d).transpose(1, 0, 3, 2, 4)

def scalar_to_chunks(x):
    B, T, H = x.shape
    return x.reshape(B, T // CHUNK, CHUNK, H).transpose(1, 0, 3, 2)

def from_chunks(y):
    NC, B, H, L, d = y.shape
    return y.transpose(1, 0, 3, 2, 4).reshape(B, NC * L, H, d)

def hgrn2_chunkwise(q, k, v, log_f):
    B, T, H, dk = q.shape
    dv = v.shape[-1]
    causal = jnp.tril(jnp.ones((CHUNK, CHUNK), dtype=bool))[:, :, None]

    def step(S, inp):
        qc, kc, vc, gc = inp
        G = jnp.cumsum(gc, axis=2)
        o_inter = jnp.einsum("bhtk,bhkv->bhtv", qc * jnp.exp(G), S)
        rel = G[:, :, :, None, :] - G[:, :, None, :, :]
        decay = jnp.exp(jnp.where(causal, rel, -jnp.inf))
        scores = jnp.sum(qc[:, :, :, None, :] * kc[:, :, None, :, :] * decay, axis=-1)
        o = o_inter + jnp.einsum("bhts,bhsv->bhtv", scores, vc)
        G_end = G[:, :, -1:, :]
        S_new = jnp.exp(G_end[:, :, 0, :])[..., None] * S + jnp.einsum(
            "bhsk,bhsv->bhkv", kc * jnp.exp(G_end - G), vc)
        return S_new, o

    S0 = jnp.zeros((B, H, dk, dv), jnp.float32)
    _, o = lax.scan(step, S0, (to_chunks(q), to_chunks(k), to_chunks(v), to_chunks(log_f)))
    return from_chunks(o)

def mlstm_chunkwise(q, k, v, log_i, log_f):
    B, T, H, dqk = q.shape
    dv = v.shape[-1]
    causal = jnp.tril(jnp.ones((CHUNK, CHUNK), dtype=bool))

    def step(carry, inp):
        C, n, m = carry
        qc, kc, vc, ic, fc = inp
        b = jnp.cumsum(fc, axis=-1)
        a = b + m[..., None]
        D = jnp.where(causal, b[..., :, None] - b[..., None, :] + ic[..., None, :], -jnp.inf)
        m_t = jnp.maximum(a, jnp.max(D, axis=-1))
        inter = jnp.exp(a - m_t)
        P = jnp.einsum("bhtd,bhsd->bhts", qc, kc) * jnp.exp(D - m_t[..., None])
        num = inter[..., None] * jnp.einsum("bhtd,bhdv->bhtv", qc, C) + jnp.einsum("bhts,bhsv->bhtv", P, vc)
        den = inter * jnp.einsum("bhtd,bhd->bht", qc, n) + jnp.sum(P, axis=-1)
        h = num / jnp.maximum(jnp.abs(den), jnp.exp(-m_t))[..., None]
        m_new = m_t[..., -1]
        w = jnp.exp(b[..., -1:] - b + ic - m_new[..., None])
        keep = inter[..., -1]
        C_new = keep[..., None, None] * C + jnp.einsum("bhs,bhsd,bhsv->bhdv", w, kc, vc)
        n_new = keep[..., None] * n + jnp.einsum("bhs,bhsd->bhd", w, kc)
        return (C_new, n_new, m_new), h

    init = (jnp.zeros((B, H, dqk, dv), jnp.float32), jnp.zeros((B, H, dqk), jnp.float32),
            jnp.zeros((B, H), jnp.float32))
    _, h = lax.scan(step, init, (to_chunks(q), to_chunks(k), to_chunks(v),
                                 scalar_to_chunks(log_i), scalar_to_chunks(log_f)))
    return from_chunks(h)

def token_mixer(h, w_in, conv_w, conv_b, gate_bias, lb, hg_norm, ml_norm, w_out):
    B, T, _ = h.shape
    f32 = jnp.float32
    hq, hf, hi, hgate, mq, mk, mv, mo, mig, mfg = split_cols(h @ w_in, SPLIT_SIZES)
    hs = (B, T, HG_HEADS, HG_HEAD_DIM)
    lbh = lb.reshape(HG_HEADS, HG_HEAD_DIM)
    forget = lbh + (1.0 - lbh) * jax.nn.sigmoid(hf.astype(f32).reshape(hs))
    hg_o = hgrn2_chunkwise(jax.nn.silu(hq.astype(f32)).reshape(hs), 1.0 - forget,
                           hi.astype(f32).reshape(hs), jnp.log(forget))
    hg_o = rms_norm(hg_o, hg_norm.reshape(HG_HEADS, HG_HEAD_DIM)).reshape(B, T, HG_WIDTH)
    hg_o = hg_o * jax.nn.silu(hgate.astype(f32))
    qk = jax.nn.silu(causal_depthwise_conv(jnp.concatenate([mq, mk], axis=-1), conv_w, conv_b))
    mq, mk = jnp.split(qk.astype(f32), 2, axis=-1)
    qs = (B, T, ML_HEADS, ML_QK_DIM)
    gates = (jnp.concatenate([mig, mfg], axis=-1) + gate_bias).astype(f32)
    log_i = gates[..., :ML_HEADS]
    log_f = jax.nn.log_sigmoid(gates[..., ML_HEADS:])
    ml_o = mlstm_chunkwise(mq.reshape(qs) * (ML_QK_DIM ** -0.5), mk.reshape(qs),
                           mv.astype(f32).reshape(B, T, ML_HEADS, ML_V_DIM), log_i, log_f)
    ml_o = rms_norm(ml_o, ml_norm.reshape(ML_HEADS, ML_V_DIM)).reshape(B, T, ML_WIDTH)
    ml_o = ml_o * jax.nn.sigmoid(mo.astype(f32))
    mix = jnp.concatenate([hg_o, ml_o], axis=-1).astype(h.dtype)
    return mix @ w_out

def first_inputs(seed: int = 0) -> dict:
    key = jax.random.key(seed)
    ks = jax.random.split(key, 16)
    nrm = jax.random.normal
    gate_bias = jnp.concatenate([
        0.1 * nrm(ks[8], (DEPTH, ML_HEADS)),
        jnp.linspace(3.0, 6.0, ML_HEADS)[None, :] + 0.1 * nrm(ks[9], (DEPTH, ML_HEADS))], axis=-1)
    return {
        "x": nrm(ks[0], (BATCH, SEQ, D_MODEL), jnp.float32),
        "norm_pre": 1.0 + 0.05 * nrm(ks[1], (DEPTH, 3, D_MODEL)),
        "norm_post": 1.0 + 0.05 * nrm(ks[2], (DEPTH, 3, D_MODEL)),
        "ffn1_w_in": nrm(ks[3], (DEPTH, D_MODEL, 2 * D_FF)) * D_MODEL ** -0.5,
        "ffn1_w_out": nrm(ks[4], (DEPTH, D_FF, D_MODEL)) * D_FF ** -0.5,
        "w_mix_in": nrm(ks[5], (DEPTH, D_MODEL, D_IN)) * D_MODEL ** -0.5,
        "conv_w": nrm(ks[6], (DEPTH, CONV_WIDTH, 2 * ML_HEADS * ML_QK_DIM)) * CONV_WIDTH ** -0.5,
        "conv_b": 0.02 * nrm(ks[7], (DEPTH, 2 * ML_HEADS * ML_QK_DIM)),
        "mlstm_gate_bias": gate_bias,
        "hgrn_lb_logits": 0.5 * nrm(ks[10], (DEPTH + 1, HG_WIDTH)),
        "hgrn_norm": 1.0 + 0.05 * nrm(ks[11], (DEPTH, HG_WIDTH)),
        "mlstm_norm": 1.0 + 0.05 * nrm(ks[12], (DEPTH, ML_WIDTH)),
        "w_mix_out": nrm(ks[13], (DEPTH, D_MIX, D_MODEL)) * D_MIX ** -0.5,
        "ffn2_w_in": nrm(ks[14], (DEPTH, D_MODEL, 2 * D_FF)) * D_MODEL ** -0.5,
        "ffn2_w_out": nrm(ks[15], (DEPTH, D_FF, D_MODEL)) * D_FF ** -0.5,
    }

def first_block(x, norm_pre, norm_post, ffn1_w_in, ffn1_w_out, w_mix_in, conv_w, conv_b,
              mlstm_gate_bias, hgrn_lb_logits, hgrn_norm, mlstm_norm, w_mix_out,
              ffn2_w_in, ffn2_w_out):
    lower_bounds = jnp.cumsum(jax.nn.softmax(hgrn_lb_logits.astype(jnp.float32), axis=0), axis=0)
    for l in range(DEPTH):
        x = x + 0.5 * rms_norm(swiglu_ffn(rms_norm(x, norm_pre[l, 0]), ffn1_w_in[l], ffn1_w_out[l]),
                               norm_post[l, 0])
        mixed = token_mixer(rms_norm(x, norm_pre[l, 1]), w_mix_in[l], conv_w[l], conv_b[l],
                            mlstm_gate_bias[l], lower_bounds[l], hgrn_norm[l], mlstm_norm[l],
                            w_mix_out[l])
        x = x + rms_norm(mixed, norm_post[l, 1])
        x = x + 0.5 * rms_norm(swiglu_ffn(rms_norm(x, norm_pre[l, 2]), ffn2_w_in[l], ffn2_w_out[l]),
                               norm_post[l, 2])
    return x


DEPTH_2 = 2

MEM_LEN = 256
SGU_BLOCK = 128
A_GROUPS = 4
A_WIDTH = D_MODEL // 2
A_GROUP_DIM = A_WIDTH // A_GROUPS
POOL_WINDOWS = (2, 4, 8, 16)
B_WIDTH = D_MODEL // 2
B_GROUP_DIM = B_WIDTH // len(POOL_WINDOWS)
C_WIDTH = D_MODEL
CONV_K = 3
XATTN_HEADS = 4
XATTN_HEAD_DIM = D_MODEL // XATTN_HEADS
D_FF_2 = ((8 * D_MODEL // 3 + 127) // 128) * 128
FFN_CONV_K = 3
LN_EPS = 1e-5
DEEPNORM_ALPHA = (2 * DEPTH_2) ** 0.25
DEEPNORM_BETA = (8 * DEPTH_2) ** -0.25
N_EVEN = (DEPTH_2 + 1) // 2
N_ODD = DEPTH_2 // 2


def layer_norm(x, g, b):
    xf = x.astype(jnp.float32)
    mu = jnp.mean(xf, axis=-1, keepdims=True)
    var = jnp.mean(jnp.square(xf - mu), axis=-1, keepdims=True)
    y = (xf - mu) * lax.rsqrt(var + LN_EPS)
    return (y * g.astype(jnp.float32) + b.astype(jnp.float32)).astype(x.dtype)

def causal_dwconv(x, w):
    k, c = w.shape
    return lax.conv_general_dilated(
        x, w[:, None, :].astype(x.dtype), window_strides=(1,), padding=[(k - 1, 0)],
        dimension_numbers=('NWC', 'WIO', 'NWC'), feature_group_count=c)

def trailing_mean_minus_self(v, window):
    seq = v.shape[1]
    vf = v.astype(jnp.float32)
    cs = jnp.cumsum(vf, axis=1)
    lagged = jnp.pad(cs, ((0, 0), (window, 0), (0, 0)))[:, :seq]
    count = jnp.minimum(jnp.arange(1, seq + 1), window).astype(jnp.float32)
    mean = (cs - lagged) / count[None, :, None]
    return (mean - vf).astype(v.dtype)

def mixer_ab(x, w_in, ln_g, ln_b, w_s, b_s, pool_w, pool_scale, w_out):
    bsz, seq, _ = x.shape
    proj = x @ w_in
    uv = jax.nn.gelu(proj[..., :2 * A_WIDTH])
    u, v = uv[..., :A_WIDTH], uv[..., A_WIDTH:]
    v = layer_norm(v, ln_g, ln_b)
    chunk_id = jnp.arange(SGU_BLOCK) // CHUNK
    mask = chunk_id[None, :] <= chunk_id[:, None]
    w_m = jnp.where(mask[None], w_s, 0.0).astype(v.dtype)
    vb = v.reshape(bsz, seq // SGU_BLOCK, SGU_BLOCK, A_GROUPS, A_GROUP_DIM)
    sp = jnp.einsum('gij,bnjgc->bnigc', w_m, vb) + b_s.T[None, None, :, :, None]
    y_a = u * sp.reshape(bsz, seq, A_WIDTH)
    xb = proj[..., 2 * A_WIDTH:].reshape(bsz, seq, len(POOL_WINDOWS), B_GROUP_DIM)
    pooled = jnp.stack([trailing_mean_minus_self(xb[:, :, g], w)
                        for g, w in enumerate(POOL_WINDOWS)], axis=2)
    y_b = jnp.einsum('bsgc,gcd->bsgd', pooled, pool_w).reshape(bsz, seq, B_WIDTH) * pool_scale
    return jnp.concatenate([y_a, y_b], axis=-1) @ w_out

def mixer_c(x, w_in, conv_w, w_out):
    proj = x @ w_in
    gate_b, gate_c, h = jnp.split(proj, 3, axis=-1)
    y = gate_b * causal_dwconv(gate_c * h, conv_w)
    return y @ w_out

def cross_attend(x, mem, wq, wkv, wo):
    bsz, seq, d = x.shape
    q = (x @ wq).reshape(bsz, seq, XATTN_HEADS, XATTN_HEAD_DIM)
    kv = mem @ wkv
    k = kv[..., :d].reshape(bsz, -1, XATTN_HEADS, XATTN_HEAD_DIM)
    v = kv[..., d:].reshape(bsz, -1, XATTN_HEADS, XATTN_HEAD_DIM)
    scores = jnp.einsum('bshd,bmhd->bhsm', q.astype(jnp.float32), k.astype(jnp.float32))
    probs = jax.nn.softmax(scores * (XATTN_HEAD_DIM ** -0.5), axis=-1).astype(x.dtype)
    out = jnp.einsum('bhsm,bmhd->bshd', probs, v).reshape(bsz, seq, d)
    return out @ wo

def conv_ffn(x, w_up, conv_w, conv_b, w_down):
    up = x @ w_up
    a, g = up[..., :D_FF_2], up[..., D_FF_2:]
    g = causal_dwconv(g, conv_w) + conv_b
    return (jax.nn.gelu(g) * a) @ w_down

def _normal(k, shape, scale):
    return jax.random.normal(k, shape, jnp.float32) * scale

def second_inputs(seed: int = 0) -> dict:
    key = jax.random.key(seed)
    ks = iter(jax.random.split(key, 32))
    d = D_MODEL
    beta = DEEPNORM_BETA
    x = _normal(next(ks), (BATCH, SEQ, d), 1.0)
    mem = _normal(next(ks), (BATCH, MEM_LEN, d), 1.0)
    ab_w_in = _normal(next(ks), (N_EVEN, d, 2 * A_WIDTH + B_WIDTH), d ** -0.5)
    sgu_ln_g = 1.0 + _normal(next(ks), (N_EVEN, A_WIDTH), 0.05)
    sgu_ln_b = _normal(next(ks), (N_EVEN, A_WIDTH), 0.02)
    sgu_w = _normal(next(ks), (N_EVEN, A_GROUPS, SGU_BLOCK, SGU_BLOCK), SGU_BLOCK ** -0.5)
    sgu_b = 1.0 + _normal(next(ks), (N_EVEN, A_GROUPS, SGU_BLOCK), 0.1)
    pool_w = _normal(next(ks), (N_EVEN, len(POOL_WINDOWS), B_GROUP_DIM, B_GROUP_DIM), B_GROUP_DIM ** -0.5)
    pool_scale = 1.0 + _normal(next(ks), (N_EVEN, B_WIDTH), 0.1)
    ab_w_out = _normal(next(ks), (N_EVEN, A_WIDTH + B_WIDTH, d), (A_WIDTH + B_WIDTH) ** -0.5 * beta)
    c_w_in = _normal(next(ks), (N_ODD, d, 3 * C_WIDTH), d ** -0.5)
    c_conv_w = _normal(next(ks), (N_ODD, CONV_K, C_WIDTH), CONV_K ** -0.5)
    c_w_out = _normal(next(ks), (N_ODD, C_WIDTH, d), C_WIDTH ** -0.5 * beta)
    ln_mix_g = 1.0 + _normal(next(ks), (DEPTH_2, d), 0.05)
    ln_mix_b = _normal(next(ks), (DEPTH_2, d), 0.02)
    xa_wq = _normal(next(ks), (DEPTH_2, d, d), d ** -0.5)
    xa_wk = _normal(next(ks), (DEPTH_2, d, d), d ** -0.5)
    xa_wv = _normal(next(ks), (DEPTH_2, d, d), d ** -0.5 * beta)
    xa_wkv = jnp.concatenate([xa_wk, xa_wv], axis=-1)
    xa_wo = _normal(next(ks), (DEPTH_2, d, d), d ** -0.5 * beta)
    ln_xa_g = 1.0 + _normal(next(ks), (DEPTH_2, d), 0.05)
    ln_xa_b = _normal(next(ks), (DEPTH_2, d), 0.02)
    ffn_w_up = _normal(next(ks), (DEPTH_2, d, 2 * D_FF_2), d ** -0.5)
    ffn_conv_w = _normal(next(ks), (DEPTH_2, FFN_CONV_K, D_FF_2), FFN_CONV_K ** -0.5)
    ffn_conv_b = _normal(next(ks), (DEPTH_2, D_FF_2), 0.02)
    ffn_w_down = _normal(next(ks), (DEPTH_2, D_FF_2, d), D_FF_2 ** -0.5 * beta)
    ln_ffn_g = 1.0 + _normal(next(ks), (DEPTH_2, d), 0.05)
    ln_ffn_b = _normal(next(ks), (DEPTH_2, d), 0.02)
    return {"x": x, "mem": mem, "ab_w_in": ab_w_in, "sgu_ln_g": sgu_ln_g, "sgu_ln_b": sgu_ln_b,
            "sgu_w": sgu_w, "sgu_b": sgu_b, "pool_w": pool_w, "pool_scale": pool_scale,
            "ab_w_out": ab_w_out, "c_w_in": c_w_in, "c_conv_w": c_conv_w, "c_w_out": c_w_out,
            "ln_mix_g": ln_mix_g, "ln_mix_b": ln_mix_b, "xa_wq": xa_wq, "xa_wkv": xa_wkv,
            "xa_wo": xa_wo, "ln_xa_g": ln_xa_g, "ln_xa_b": ln_xa_b, "ffn_w_up": ffn_w_up,
            "ffn_conv_w": ffn_conv_w, "ffn_conv_b": ffn_conv_b, "ffn_w_down": ffn_w_down,
            "ln_ffn_g": ln_ffn_g, "ln_ffn_b": ln_ffn_b}

def second_block(x, mem, ab_w_in, sgu_ln_g, sgu_ln_b, sgu_w, sgu_b, pool_w, pool_scale,
              ab_w_out, c_w_in, c_conv_w, c_w_out, ln_mix_g, ln_mix_b, xa_wq, xa_wkv,
              xa_wo, ln_xa_g, ln_xa_b, ffn_w_up, ffn_conv_w, ffn_conv_b, ffn_w_down,
              ln_ffn_g, ln_ffn_b):
    alpha = DEEPNORM_ALPHA
    for layer in range(DEPTH_2):
        j = layer // 2
        if layer % 2 == 0:
            mix = mixer_ab(x, ab_w_in[j], sgu_ln_g[j], sgu_ln_b[j], sgu_w[j], sgu_b[j],
                           pool_w[j], pool_scale[j], ab_w_out[j])
        else:
            mix = mixer_c(x, c_w_in[j], c_conv_w[j], c_w_out[j])
        x = layer_norm(alpha * x + mix, ln_mix_g[layer], ln_mix_b[layer])
        x = layer_norm(alpha * x + cross_attend(x, mem, xa_wq[layer], xa_wkv[layer], xa_wo[layer]),
                       ln_xa_g[layer], ln_xa_b[layer])
        x = layer_norm(alpha * x + conv_ffn(x, ffn_w_up[layer], ffn_conv_w[layer],
                                            ffn_conv_b[layer], ffn_w_down[layer]),
                       ln_ffn_g[layer], ln_ffn_b[layer])
    return x


def setup_inputs(seed=0):
    out = dict(first_inputs(seed))
    for name, value in second_inputs(seed + 1).items():
        if name != "x":
            out[name + "_2"] = value
    return out


def reference(
    x, norm_pre, norm_post, ffn1_w_in, ffn1_w_out, w_mix_in, conv_w, conv_b, mlstm_gate_bias,
    hgrn_lb_logits, hgrn_norm, mlstm_norm, w_mix_out, ffn2_w_in, ffn2_w_out, mem_2, ab_w_in_2,
    sgu_ln_g_2, sgu_ln_b_2, sgu_w_2, sgu_b_2, pool_w_2, pool_scale_2, ab_w_out_2, c_w_in_2,
    c_conv_w_2, c_w_out_2, ln_mix_g_2, ln_mix_b_2, xa_wq_2, xa_wkv_2, xa_wo_2, ln_xa_g_2,
    ln_xa_b_2, ffn_w_up_2, ffn_conv_w_2, ffn_conv_b_2, ffn_w_down_2, ln_ffn_g_2, ln_ffn_b_2,
):
    x = first_block(
        x, norm_pre, norm_post, ffn1_w_in, ffn1_w_out, w_mix_in, conv_w, conv_b,
        mlstm_gate_bias, hgrn_lb_logits, hgrn_norm, mlstm_norm, w_mix_out, ffn2_w_in,
        ffn2_w_out,
    )
    return second_block(
        x, mem_2, ab_w_in_2, sgu_ln_g_2, sgu_ln_b_2, sgu_w_2, sgu_b_2, pool_w_2, pool_scale_2,
        ab_w_out_2, c_w_in_2, c_conv_w_2, c_w_out_2, ln_mix_g_2, ln_mix_b_2, xa_wq_2, xa_wkv_2,
        xa_wo_2, ln_xa_g_2, ln_xa_b_2, ffn_w_up_2, ffn_conv_w_2, ffn_conv_b_2, ffn_w_down_2,
        ln_ffn_g_2, ln_ffn_b_2,
    )


_drawn_inputs = setup_inputs


def setup_inputs(seed=0):
    import zlib

    import numpy as np

    out = dict(_drawn_inputs(seed))
    spreads = {}
    factors = {'conv_b': 4.13,
     'sgu_ln_g_2': 6.784,
     'sgu_ln_b_2': 24.619,
     'sgu_b_2': 3.022,
     'ffn_conv_b_2': 8.0,
     'pool_scale_2': 3.492}
    for name, (base, spread) in spreads.items():
        noise = np.random.default_rng([zlib.crc32(name.encode()), seed]).standard_normal(out[name].shape)
        drawn = base * np.exp(spread * noise) if base else spread * noise
        out[name] = __import__('jax').numpy.asarray(drawn.astype(out[name].dtype))
    for name, factor in factors.items():
        out[name] = (out[name] * factor).astype(out[name].dtype)
    return out
```

```python
import concourse.bass as bass
from concourse import mybir
from contextlib import ExitStack

P = 128
T = 512
D = 1024
KD = D // P
FF = 2816
KF = FF // P
HALF_KF = KF // 2
MEM = 256
NT = T // P
HEADS = 4
CHUNK = 128
FULL = 16 * P
DOWN = HALF_KF * P
LEVELS = (64, 32, 16, 8, 4, 2, 1)
ALPHA = (2 * 2) ** 0.25
SLOTS = 2

PHASES = [("up0", KF, 16), ("down0", 16, HALF_KF), ("mixin", 14, 16), ("mixout", 4, 16),
          ("up1", KF, 16), ("down1", 16, HALF_KF),
          ("ab", 6, 16), ("about", 4, 16), ("kv0", 8, 16), ("q0", 4, 16), ("wo0", 4, 16),
          ("up2", KF, 16), ("down2", 16, HALF_KF),
          ("cin", 12, 16), ("cout", 4, 16), ("kv1", 8, 16), ("q1", 4, 16), ("wo1", 4, 16),
          ("up3", KF, 16), ("down3", 16, HALF_KF)]
UNIT0, UNITS, UNIT_COLS, SOURCE0 = {}, {}, [], {}
_full = _down = 0
for _name, _n, _tiles in PHASES:
    UNIT0[_name], UNITS[_name] = len(UNIT_COLS), _n
    UNIT_COLS += [_tiles * P] * _n
    SOURCE0[_name] = _full if _tiles == 16 else _down
    if _tiles == 16:
        _full += _n
    else:
        _down += _n
N_UNITS = len(UNIT_COLS)

VECTORS = [("norm_pre", 24), ("norm_post", 24), ("ln_mix_g_2", 16), ("ln_mix_b_2", 16), ("ln_xa_g_2", 16),
           ("ln_xa_b_2", 16), ("ln_ffn_g_2", 16), ("ln_ffn_b_2", 16), ("conv_w", 16), ("conv_b", 4),
           ("ffn_conv_w_2", 2 * 3 * KF), ("ffn_conv_b_2", 2 * KF), ("c_conv_w_2", 24), ("pool_scale_2", 4),
           ("hgrn_norm", 4), ("mlstm_norm", 4)]
VCOL, _c = {}, 0
for _name, _n in VECTORS:
    VCOL[_name] = _c
    _c += _n
N_VEC = _c

GEN = {n: i for i, n in enumerate(["up0", "mixin", "mixout", "up1", "ab", "about", "q0", "wo0", "up2",
                                   "cin", "cout", "q1", "wo1", "up3"])}
RMS_ENDS = ["down0", "mixout", "down1"]
LN_ENDS = ["about", "wo0", "down2", "cout", "wo1", "down3"]
GAINS = {"about": ("ln_mix", 0), "wo0": ("ln_xa", 0), "down2": ("ln_ffn", 0),
         "cout": ("ln_mix", 1), "wo1": ("ln_xa", 1), "down3": ("ln_ffn", 1)}
NEXT = {"about": "q0", "wo0": "up2", "down2": "cin", "cout": "q1", "wo1": "up3", "down3": None}


def build(nc, a):
    f32, f32r, u32 = mybir.dt.float32, mybir.dt.float32r, mybir.dt.uint32
    ACT, ALU, AX = mybir.ActivationFunctionType, mybir.AluOpType, mybir.AxisListType
    V, S, G = nc.vector, nc.scalar, nc.gpsimd

    ctx = ExitStack()
    with ctx:
        KB = 1024
        BASE = 16512
        slab = ctx.enter_context(nc.sbuf_tensor("slab", [P, 53200], f32))
        made = {}

        def at(name, shape, dt, off):
            made[name] = nc.alloc_sbuf_tensor_at(name, shape, dt, offset=BASE + int(off))
            return made[name]

        x = at("x", [P, KD, T], f32, 0)
        a_hi = at("a_hi", [P, KD, T], f32r, 16 * KB)
        a_lo = at("a_lo", [P, KD, T], f32r, 32 * KB)
        y_ff = at("y_ff", [P, KD, T], f32, 16 * KB)
        raw = at("raw", [P, SLOTS, FULL], f32, 48 * KB)
        w_hi = at("w_hi", [P, SLOTS, FULL], f32r, 64 * KB)
        w_lo = at("w_lo", [P, SLOTS, FULL], f32r, 80 * KB)
        C0 = 96 * KB
        ident = at("ident", [P, P], f32, C0)
        mean_w = at("mean_w", [P, P], f32, C0 + 512)
        vec = at("vec", [P, N_VEC], f32, C0 + 1024)
        small = at("small", [P, 16], f32, C0 + 1024 + N_VEC * 4)
        eps6, eps5, one = small[:, 0:1], small[:, 1:2], small[:, 2:3]
        half_g = at("half_g", [P, 24], f32, C0 + 1088 + N_VEC * 4)
        A0 = C0 + 4 * KB - 256

        def arena(name, shape, dt, kb):
            return at(name, shape, dt, A0 + kb * KB)

        h_hi = arena("h_hi", [P, KF, T], f32r, 0)
        h_lo = arena("h_lo", [P, KF, T], f32r, 44)
        act_out = arena("act_out", [P, 2, T], f32, 88)
        h32 = arena("h32", [P, 2, T], f32, 92)
        conv_out = arena("conv_out", [P, 2, T], f32, 96)
        acc = arena("acc", [P, 2, 2, T], f32, 88)
        sq = arena("sq", [P, 2, T], f32, 96)
        mean = arena("mean", [P, T], f32, 100)
        rstd = arena("rstd", [P, T], f32, 102)
        nt = arena("nt", [P, 2, T], f32, 104)
        logf = arena("logf", [P, NT, T], f32, 0)
        kdec = arena("kdec", [P, NT, T], f32, 0)
        k_tm = arena("k_tm", [P, NT, T], f32, 8)
        v_tm = arena("v_tm", [P, NT, T], f32, 16)
        mv_tm = arena("mv_tm", [P, NT, T], f32, 24)
        scores = arena("scores", [P, HEADS, T], f32, 24)
        q_fm = arena("q_fm", [P, HEADS, T], f32, 32)
        hgate = arena("hgate", [P, HEADS, T], f32, 40)
        mgate = arena("mgate", [P, HEADS, T], f32, 48)
        mqk = arena("mqk", [P, HEADS, T], f32, 56)
        q_dec = arena("q_dec", [P, HEADS, T], f32, 64)
        Gc = arena("Gc", [P, HEADS, T], f32, 72)
        k_fm = arena("k_fm", [P, HEADS, T], f32, 80)
        lev = [arena("lev0", [P, HEADS, T], f32, 56), arena("lev1", [P, HEADS, T], f32, 88)]
        states = arena("states", [P, 3, HEADS, P], f32, 8)
        g_end = arena("g_end", [P, HEADS * NT], f32, 14)
        masks = arena("masks", [P, 8, P], u32, 96)
        tri = arena("tri", [P, 2, P], f32, 100)
        gbias = arena("gbias", [P, 2], f32, 101)
        ct = arena("ct", [P, NT, HEADS], f32, 101.25)
        mtmp = arena("mtmp", [P, 3, T], f32, 102)
        wg_raw = arena("wg_raw", [P, KD, P], f32, 64)
        wg_hi = arena("wg_hi", [P, KD, P], f32r, 68)
        wg_lo = arena("wg_lo", [P, KD, P], f32r, 72)
        rows = arena("rows", [HEADS, 2, 256 + T], f32, 76)
        row_i = arena("row_i", [HEADS, T], f32, 82)
        row_b = arena("row_b", [HEADS, T], f32, 84)
        row_t = arena("row_t", [HEADS, T], f32, 86)
        row_nm = arena("row_nm", [HEADS, T], f32, 88)
        row_em = arena("row_em", [HEADS, T], f32, 90)
        sel = arena("sel", [HEADS, HEADS, P], f32, 92)
        mp = arena("mp", [P, NT * (T + P)], f32, 64)
        lb = arena("lb", [P, 2, T], f32, 32)
        lbt = arena("lbt", [P, 2, T], f32, 36)
        sigm = arena("sigm", [P, 2, 2, MEM], f32, 94)
        y_mix = arena("y_mix", [P, KD, T], f32, 0)
        gv = arena("gv", [P, NT, T], f32, 0)
        ug = arena("ug", [P, 4, T], f32, 8)
        PAD = 16
        pool = [arena(f"pool{n}", [P, 4, PAD + T], f32, 16 + 8.5 * n) for n in range(3)]
        ab_rows = arena("ab_rows", [P, 3, T], f32, 42)
        ws_t = arena("ws_t", [P, 4, P], f32, 48)
        pool_w = arena("pool_w", [P, 4, P], f32, 50)
        inv_cnt = arena("inv_cnt", [P, 4, PAD], f32, 52)
        bn = arena("bn", [P, NT, 6], f32, 52.5)
        mv4 = arena("mv4", [P, NT, 2], f32, 53)
        rs4 = arena("rs4", [P, NT], f32, 53.5)
        cc = arena("cc", [P, 2, T], f32, 0)
        ch = arena("ch", [P, 2, T], f32, 4)
        yc = arena("yc", [P, KD, T], f32, 8)
        mem_raw = arena("mem_raw", [P, KD, MEM], f32, 56)
        mem_hi = arena("mem_hi", [P, KD, MEM], f32r, 64)
        mem_lo = arena("mem_lo", [P, KD, MEM], f32r, 72)
        k_mem = arena("k_mem", [P, KD, MEM], f32, 80)
        v_mem = arena("v_mem", [P, 2, D], f32, 0)
        q_at = arena("q_at", [P, KD, T], f32, 8)
        pe_at = arena("pe_at", [P, 2, NT, MEM], f32, 24)
        p_t = arena("p_t", [P, 2, 2, T], f32, 32)
        o32 = arena("o32", [P, 2, T], f32, 40)
        at_s = arena("at_s", [P, 2, 3, NT], f32, 44)

        bank = ctx.enter_context(nc.psum_tensor("bank", [P, 8, T], f32))

        def sem(name):
            return ctx.enter_context(nc.semaphore(name))

        w_loaded = [sem("w_loaded0"), sem("w_loaded1")]
        w_hi_done = sem("w_hi_done")
        w_split = sem("w_split")
        gemm_done = sem("gemm_done")
        banks_free = sem("banks_free")
        consts = sem("consts")
        consts_v = sem("consts_v")
        x_in = [sem(f"x_in{k}") for k in range(KD)]
        mix_in = sem("mix_in")
        mask_in = sem("mask_in")
        ab_in = sem("ab_in")
        mem_in = sem("mem_in")
        out_s = sem("out_s")
        a_hi_done = sem("a_hi_done")
        a_done = sem("a_done")
        x_act = sem("x_act")
        x_dve = sem("x_dve")
        norm_t = sem("norm_t")
        gate_done = sem("gate_done")
        conv0 = sem("conv0")
        conv_done = sem("conv_done")
        h_hi_done = sem("h_hi_done")
        h_done = sem("h_done")
        y_copied = sem("y_copied")
        sq_done = sem("sq_done")
        acc_done = sem("acc_done")
        stats = sem("stats")
        stat_a = sem("stat_a")
        stat_v = sem("stat_v")
        dve_link = sem("dve_link")
        act_link = sem("act_link")
        SIG = {n: sem(n) for n in """gate_rows_mm c_columns_mm mlstm_m_mm mlstm_scores_mm mlstm_num_mm mlstm_den_mm mlstm_em_mm
            mlstm_ms_mm cum_decay_mm keys_transposed rest_decay_mm state_add_mm level_scores_mm hgrn_out_mm
            hgrn_ms_mm attn_scores_mm probs_transposed attn_out_mm spatial_mm pool_mm mlstm_weight
            mlstm_absden mlstm_square mlstm_rms gate_w_hi lb_exp mconv_start mqk_ready
            i_row f_row_log mlstm_v exp_neg_m mlstm_gate hgrn_input logf_ready
            cum_decay keys_fm rest_decay q_decay chunk_decay level_exp hgrn_square
            hgrn_rms sgu_v sgu_u sgu_std pool_in mem_hi_done c_gate
            c_conv_start mem_kv attn_q attn_exp probs_t c_columns mlstm_arg mlstm_p
            mlstm_masked mlstm_den mlstm_h mlstm_y lb_diff gate_w_lo mconv_done
            c_row neg_m_row neg_bm_row forget_ready keys_tm keys_decayed level_diff
            level_ready scores_taken states_ready hgrn_y sgu_stats sgu_v_ready ab_ya
            pooled ab_yb mem_lo_done c_product c_y attn_max attn_o32
            attn_probs""".split()}

        def gemm_at(unit, tile=1):
            return 2 * unit + tile + 5

        def free_at(unit):
            return unit + 3

        def gen_at(name, k=KD - 1):
            return KD * GEN[name] + k + 1

        seq = ["x0", "down0", "pre_mixin", "mixout", "pre_up1", "down1"] + LN_ENDS
        SQ0, ACC0, ST0, SA0, SV0 = {}, {}, {}, {}, {}
        c = [0] * 5
        for n in seq:
            SQ0[n], ACC0[n], ST0[n], SA0[n], SV0[n] = c
            ln = n in LN_ENDS
            steps = {"x0": 8, "pre_mixin": 8, "pre_up1": 8}.get(n, 8 if n.startswith("down") else 4)
            c = [c[0] + steps, c[1] + 1 + steps * (2 if ln else 0 if n in RMS_ENDS else 1), c[2] + 1, c[3] + (3 if ln else 1),
                 c[4] + (3 if ln else 1)]
        NORM0 = {n: KD * i for i, n in enumerate(["up0", "mixin", "up1"] + [NEXT[e] or "out" for e in LN_ENDS])}
        XACT0 = {n: KD * i for i, n in enumerate(LN_ENDS)}
        XDVE0 = {n: KD * i for i, n in enumerate(RMS_ENDS)}
        F0 = {f: KF * f for f in range(4)}

        block = ctx.enter_context(nc.Block())

        @block.sync
        def _(sp):
            def stream(phase):
                u0, n, cols, s0 = UNIT0[phase], UNITS[phase], UNIT_COLS[UNIT0[phase]], SOURCE0[phase]
                src = a["w_full"] if cols == FULL else a["w_down"]
                with sp.Fori(0, n // 2) as i:
                    for s in range(SLOTS):
                        sp.wait_ge(w_split, u0 + 2 * i + (s + 1))
                        sp.dma_start(raw[:, s:s + 1, 0:cols],
                                     src[bass.ds(s0 + 2 * i + s, 1), :, :].rearrange("u p c -> p u c")
                                     ).then_inc(w_loaded[s], 16)

            sp.dma_start(vec[:, :], a["vectors"]).then_inc(consts, 16)
            sp.dma_start(ident[:, :], a["identity"]).then_inc(consts, 16)
            for phase, _, _ in PHASES:
                stream(phase)
            for k in range(KD):
                sp.wait_ge(x_act, XACT0["down3"] + k + 1)
                sp.dma_start(a["out"][:, k, :], x[:, k, :]).then_inc(out_s, 16)
            sp.wait_ge(out_s, 16 * KD)

        @block.gpsimd
        def _(gp):
            for k in range(KD):
                gp.dma_start(x[:, k, :], a["x"][:, k, :]).then_inc(x_in[k], 16)
            gp.wait_ge(a_done, gen_at("mixin"))
            for n, (dst, src) in enumerate([(wg_raw[:, :, :], a["w_gates"]), (tri[:, :, :], a["tri"]), (sel[:, :, :], a["sel"]),
                             (gbias[0:HEADS, :], a["gate_bias"]), (lbt[:, :, :], a["lb_rows"])]):
                gp.dma_start(dst, src).then_inc(mix_in, 16)
                gp.wait_ge(mix_in, 16 * (n + 1))
            gp.wait_ge(SIG["forget_ready"], 2)
            gp.dma_start(masks[:, :, :], a["masks"]).then_inc(mask_in, 16)
            gp.wait_ge(gemm_done, gemm_at(UNIT0["ab"] - 1))
            for n, (dst, src) in enumerate([(ab_rows[:, :, :], a["ab_rows"]), (ws_t[:, :, :], a["ws_t"]), (pool_w[:, :, :], a["pool_w"]),
                             (inv_cnt[:, :, :], a["inv_cnt"])]):
                gp.dma_start(dst, src).then_inc(ab_in, 16)
                gp.wait_ge(ab_in, 16 * (n + 1))
            gp.dma_start(mem_raw[:, :, :], a["mem"]).then_inc(mem_in, 16)
            gp.wait_ge(gemm_done, gemm_at(UNIT0["cin"] - 1))
            gp.dma_start(mem_raw[:, :, :], a["mem"]).then_inc(mem_in, 16)

        @block.tensor
        def _(pe):
            mm = nc.tensor.matmul
            PARTS = ((w_hi, a_hi), (w_hi, a_lo), (w_lo, a_hi))

            def feature_units(phase, wait_gen=None):
                u0, n = UNIT0[phase], UNITS[phase]

                def pair(i, first):
                    for s in range(SLOTS):
                        pe.wait_ge(w_split, u0 + 2 * i + (s + 3))
                        pe.wait_ge(banks_free, u0 + 2 * i + (s + 1))
                        for m in range(2):
                            for k in range(KD):
                                if first and s == 0 and m == 0:
                                    pe.wait_ge(a_done, gen_at(wait_gen, k))
                                for j, (w, act_in) in enumerate(PARTS):
                                    col = (m * KD + k) * P
                                    last = mm(bank[:, 2 * s + m, :], w[:, s, col:col + P], act_in[:, k, :],
                                              start=(k == 0 and j == 0), stop=(k == KD - 1 and j == 2))
                            last.then_inc(gemm_done, 1)
                pair(0, True)
                if n > 2:
                    with pe.Fori(1, n // 2) as i:
                        pair(i, False)

            def feature_slice(phase, first_unit, n, gen=None):
                for u in range(first_unit, first_unit + n):
                    s, un = u % 2, UNIT0[phase] + u
                    pe.wait_ge(w_split, un + 3)
                    pe.wait_ge(banks_free, un + 1)
                    for m in range(2):
                        for k in range(KD):
                            if gen and u == 0 and m == 0:
                                pe.wait_ge(a_done, gen_at(gen, k))
                            for j, (w, act_in) in enumerate(PARTS):
                                col = (m * KD + k) * P
                                last = mm(bank[:, 2 * s + m, :], w[:, s, col:col + P], act_in[:, k, :],
                                          start=(k == 0 and j == 0), stop=(k == KD - 1 and j == 2))
                        last.then_inc(gemm_done, 1)

            def token_slice(phase, first_unit, n, gen=None):
                for u in range(first_unit, first_unit + n):
                    s, un = u % 2, UNIT0[phase] + u
                    pe.wait_ge(w_split, un + 3)
                    pe.wait_ge(banks_free, un + 1)
                    if gen and u == 0:
                        pe.wait_ge(a_done, gen_at(gen))
                    for m in range(2):
                        for t in range(2):
                            tok = (2 * m + t) * P
                            for k in range(KD):
                                for j, (w, act_in) in enumerate(PARTS):
                                    last = mm(bank[:, 2 * s + m, t * 256:t * 256 + 256],
                                              act_in[:, k, tok:tok + P], w[:, s, k * 256:k * 256 + 256],
                                              start=(k == 0 and j == 0), stop=(k == KD - 1 and j == 2))
                        last.then_inc(gemm_done, 1)

            def down_units(phase, f):
                u0 = UNIT0[phase]
                pe.wait_ge(h_done, F0[f] + HALF_KF)
                with pe.Fori(0, KD // 2) as i:
                    for d in range(2):
                        for s in range(SLOTS):
                            pe.wait_ge(w_split, u0 + 4 * i + (2 * d + s + 3))
                            if s == 0:
                                pe.wait_ge(banks_free, u0 + 4 * i + 2 * d)
                            else:
                                pe.wait_ge(h_done, F0[f] + KF)
                            for k in range(HALF_KF):
                                for j, (w, h) in enumerate(((w_hi, h_hi), (w_hi, h_lo), (w_lo, h_hi))):
                                    last = mm(bank[:, 4 + d, :], w[:, s, k * P:(k + 1) * P],
                                              h[:, s * HALF_KF + k, :],
                                              start=(s == 0 and k == 0 and j == 0),
                                              stop=(s == 1 and k == HALF_KF - 1 and j == 2))
                            last.then_inc(gemm_done, 2)

            def norm_sums(name):
                ln = name in LN_ENDS
                if name in ("down0", "mixout", "down1"):
                    pe.wait_ge(banks_free, free_at(UNIT0[name] + UNITS[name] - 1))
                else:
                    pe.wait_ge(acc_done, ACC0[name] + 1 + (8 if name[0] != "d" and not ln else
                                                           2 * (8 if name[0] == "d" else 4)))
                for which in ((0, 1) if ln else (1,)):
                    for par in range(2):
                        last = mm(bank[:, 7 if ln and which else 6, :], mean_w[:, :], acc[:, which, par, :],
                                  start=par == 0, stop=par == 1)
                last.then_inc(stats, 1)

            def mlstm_rows():
                pe.wait_ge(SIG["gate_w_lo"], 1)
                for k in range(KD):
                    for j, (w, act_in) in enumerate(((wg_hi, a_hi), (wg_hi, a_lo), (wg_lo, a_hi))):
                        last = mm(bank[:, 4, :], w[:, k, :], act_in[:, k, :],
                                  start=(k == 0 and j == 0), stop=(k == KD - 1 and j == 2))
                last.then_inc(SIG["gate_rows_mm"], 1)

            def mlstm_columns():
                pe.wait_ge(SIG["c_row"], 1)
                for s in range(NT):
                    last = nc.tensor.transpose(bank[:, 5, 4 * s:4 * s + 4], row_t[:, s * P:(s + 1) * P],
                                               ident[0:HEADS, 0:HEADS])
                last.then_inc(SIG["c_columns_mm"], 1)

            def mlstm_head(h):
                r = 64 * (h % 2)
                q, k = mqk[r:r + 64, h // 2, :], mqk[r:r + 64, 2 + h // 2, :]
                if h == 0:
                    pe.wait_ge(SIG["neg_m_row"], 1)
                    pe.wait_ge(SIG["exp_neg_m"], 1)
                    pe.wait_ge(SIG["mqk_ready"], 4)
                    pe.wait_ge(SIG["mlstm_v"], 2)
                else:
                    pe.wait_ge(SIG["mlstm_den"], h)
                mm(bank[:, 4, :], sel[:, h, :], row_nm[:, :], start=True, stop=True).then_inc(SIG["mlstm_m_mm"], 1)
                for s in range(NT):
                    if s >= 2:
                        pe.wait_ge(SIG["mlstm_p"], 4 * h + s - 2 + 1)
                    elif h:
                        pe.wait_ge(SIG["mlstm_h"], h)
                    mm(bank[:, 5 + s % 2, s * P:T], k[:, s * P:(s + 1) * P], q[:, s * P:T],
                       start=True, stop=True).then_inc(SIG["mlstm_scores_mm"], 1)
                pe.wait_ge(SIG["mlstm_masked"], h + 1)
                for s in range(NT):
                    last = mm(bank[:, 7, s * P:T], mv_tm[:, s, h * P:(h + 1) * P], mp[:, s * T + s * P:(s + 1) * T],
                              start=(s == 0), stop=(s == NT - 1))
                last.then_inc(SIG["mlstm_num_mm"], 1)
                for s in range(NT):
                    last = mm(bank[:, 4, s * P:T], mean_w[:, :], mp[:, s * T + s * P:(s + 1) * T],
                              start=(s == 0), stop=(s == NT - 1))
                last.then_inc(SIG["mlstm_den_mm"], 1)
                mm(bank[:, 5, :], sel[:, h, :], row_em[:, :], start=True, stop=True).then_inc(SIG["mlstm_em_mm"], 1)
                pe.wait_ge(SIG["mlstm_square"], h + 1)
                mm(bank[:, 6, :], mean_w[:, :], mtmp[:, 1, :], start=True, stop=True).then_inc(SIG["mlstm_ms_mm"], 1)

            def hgrn_core():
                pe.wait_ge(SIG["logf_ready"], 1)
                pe.wait_ge(banks_free, free_at(UNIT0["mixin"] + 13))
                for h in range(HEADS):
                    for n in range(NT):
                        last = mm(bank[:, h, n * P:(n + 1) * P], logf[:, n, h * P:(h + 1) * P], tri[:, 0, :],
                                  start=True, stop=True)
                last.then_inc(SIG["cum_decay_mm"], 1)
                pe.wait_ge(SIG["keys_tm"], 1)
                for h in range(HEADS):
                    for n in range(NT):
                        last = nc.tensor.transpose(bank[:, 4 + h, n * P:(n + 1) * P],
                                                   k_tm[:, n, h * P:(h + 1) * P], ident[:, :])
                last.then_inc(SIG["keys_transposed"], 1)
                pe.wait_ge(SIG["cum_decay"], 1)
                for n in range(NT):
                    last = mm(bank[:, n, :], tri[:, 1, :], logf[:, n, :], start=True, stop=True)
                last.then_inc(SIG["rest_decay_mm"], 1)
                pe.wait_ge(SIG["keys_decayed"], 1)
                pe.wait_ge(SIG["keys_fm"], 1)
                for n in range(NT - 1):
                    for h in range(HEADS):
                        last = mm(bank[:, 4 + n, h * P:(h + 1) * P], kdec[:, n, h * P:(h + 1) * P],
                                  v_tm[:, n, h * P:(h + 1) * P], start=True, stop=True)
                last.then_inc(SIG["state_add_mm"], 1)
                pe.wait_ge(SIG["q_decay"], 1)
                for l in range(len(LEVELS) + 1):
                    if l:
                        pe.wait_ge(SIG["level_ready"], l)
                    if l >= 2:
                        pe.wait_ge(SIG["scores_taken"], l - 2 + 1)
                    if l == 1:
                        pe.wait_ge(SIG["states_ready"], 1)
                    for h in range(HEADS):
                        for n in range(NT):
                            c0 = n * P
                            lhs = k_fm if l == 0 else lev[(l - 1) % 2]
                            rhs = q_fm if l == 0 else lev[(l - 1) % 2]
                            last = mm(bank[:, 4 * (l % 2) + h, c0:c0 + P], lhs[:, h, c0:c0 + P],
                                      rhs[:, h, c0:c0 + P], start=True, stop=True)
                    last.then_inc(SIG["level_scores_mm"], 1)
                pe.wait_ge(SIG["scores_taken"], len(LEVELS) + 1)
                for h in range(HEADS):
                    for n in range(NT):
                        c0 = n * P
                        last = mm(bank[:, h, c0:c0 + P], v_tm[:, n, h * P:(h + 1) * P], scores[:, h, c0:c0 + P],
                                  start=True, stop=(n == 0))
                        if n:
                            last = mm(bank[:, h, c0:c0 + P], states[:, n - 1, h, :], q_dec[:, h, c0:c0 + P],
                                      start=False, stop=True)
                    last.then_inc(SIG["hgrn_out_mm"], 1)
                for h in range(HEADS):
                    pe.wait_ge(SIG["hgrn_square"], h + 1)
                    mm(bank[:, 4 + h, :], mean_w[:, :], lev[1][:, h, :], start=True, stop=True).then_inc(SIG["hgrn_ms_mm"], 1)

            def memory_unit(phase, u):
                s, un = u % 2, UNIT0[phase] + u
                layer = int(phase[-1])
                if u == 0:
                    pe.wait_ge(SIG["mem_lo_done"], layer + 1)
                pe.wait_ge(w_split, un + 3)
                pe.wait_ge(banks_free, un + 1)
                for m in range(2):
                    for k in range(KD):
                        for j, (w, src) in enumerate(((w_hi, mem_hi), (w_hi, mem_lo), (w_lo, mem_hi))):
                            if u < 4:
                                col = (m * KD + k) * P
                                ops = (w[:, s, col:col + P], src[:, k, :])
                            else:
                                ops = (src[:, k, m * P:(m + 1) * P], w[:, s, k * 256:k * 256 + 256])
                            last = mm(bank[:, 2 * s + m, 0:MEM], *ops,
                                      start=(k == 0 and j == 0), stop=(k == KD - 1 and j == 2))
                    last.then_inc(gemm_done, 1)

            def attention(layer):
                pe.wait_ge(banks_free, free_at(UNIT0[f"q{layer}"] + 3))
                for h in range(HEADS + 1):
                    if h < HEADS:
                        b = 2 * (h % 2)
                        if h >= 2:
                            pe.wait_ge(SIG["attn_probs"], 4 * layer + h - 2 + 1)
                        for t in range(NT):
                            for d in range(2):
                                last = mm(bank[:, b + t // 2, (t % 2) * MEM:(t % 2) * MEM + MEM],
                                          q_at[:, 2 * h + d, t * P:(t + 1) * P], k_mem[:, 2 * h + d, :],
                                          start=(d == 0), stop=(d == 1))
                        last.then_inc(SIG["attn_scores_mm"], 1)
                    if h:
                        g = h - 1
                        pe.wait_ge(SIG["attn_probs"], 4 * layer + g + 1)
                        if g:
                            pe.wait_ge(SIG["probs_t"], 4 * layer + g)
                        for m in range(2):
                            for t in range(NT):
                                last = nc.tensor.transpose(bank[:, 4 + m, t * P:(t + 1) * P],
                                                           pe_at[:, g % 2, t, m * P:(m + 1) * P], ident[:, :])
                        last.then_inc(SIG["probs_transposed"], 1)
                        pe.wait_ge(SIG["probs_t"], 4 * layer + g + 1)
                        if g:
                            pe.wait_ge(SIG["attn_o32"], 4 * layer + g)
                        for d in range(2):
                            for m in range(2):
                                last = mm(bank[:, 6 + d, :], v_mem[:, m, (2 * g + d) * P:(2 * g + d + 1) * P],
                                          p_t[:, g % 2, m, :], start=(m == 0), stop=(m == 1))
                        last.then_inc(SIG["attn_out_mm"], 1)

            def ab_core():
                pe.wait_ge(SIG["sgu_v_ready"], 1)
                for g in range(4):
                    for n in range(NT):
                        last = mm(bank[:, 4 + g, n * P:(n + 1) * P], gv[:, n, g * P:(g + 1) * P],
                                  ws_t[:, g, :], start=True, stop=True)
                last.then_inc(SIG["spatial_mm"], 1)
                pe.wait_ge(banks_free, free_at(UNIT0["ab"] + 5))
                for g in range(4):
                    pe.wait_ge(SIG["pooled"], g + 1)
                    mm(bank[:, g, :], pool_w[:, g, :], pool[2][:, g, PAD:PAD + T],
                       start=True, stop=True).then_inc(SIG["pool_mm"], 1)

            pe.wait_ge(consts_v, 1)
            pe.wait_ge(consts, 32)
            norm_sums("x0")
            feature_units("up0", "up0")
            down_units("down0", 0)
            norm_sums("down0")
            norm_sums("pre_mixin")
            feature_slice("mixin", 0, 2, "mixin")
            mlstm_rows()
            token_slice("mixin", 2, 2)
            feature_slice("mixin", 4, 2)
            mlstm_columns()
            for h in range(HEADS):
                if h < 2:
                    token_slice("mixin", 6 + 2 * h, 2)
                else:
                    feature_slice("mixin", 6 + 2 * h, 2)
                mlstm_head(h)
            hgrn_core()
            feature_units("mixout", "mixout")
            norm_sums("mixout")
            norm_sums("pre_up1")
            feature_units("up1", "up1")
            down_units("down1", 1)
            norm_sums("down1")
            token_slice("ab", 0, 2, "ab")
            feature_slice("ab", 2, 4)
            ab_core()
            pe.wait_ge(SIG["ab_yb"], 4)
            feature_units("about", "about")
            for layer in range(2):
                memory_unit(f"kv{layer}", 0)
                norm_sums(("about", "cout")[layer])
                for u in range(1, 8):
                    memory_unit(f"kv{layer}", u)
                feature_units(f"q{layer}", f"q{layer}")
                attention(layer)
                feature_units(f"wo{layer}", f"wo{layer}")
                norm_sums(f"wo{layer}")
                feature_units(f"up{2 + layer}", f"up{2 + layer}")
                down_units(f"down{2 + layer}", 2 + layer)
                norm_sums(f"down{2 + layer}")
                if layer == 0:
                    feature_units("cin", "cin")
                    feature_units("cout", "cout")

        @block.scalar
        def _(act):
            links = [0]

            def link(ins):
                links[0] += 1
                ins.then_inc(act_link, 1)
                act.wait_ge(act_link, links[0])

            def split(unit, s, cols):
                half = unit // 2 if isinstance(unit, int) else None
                act.wait_ge(w_loaded[s], 16 * (half + 1))
                act.wait_ge(gemm_done, 2 * unit + 2)
                S.activation(w_hi[:, s, 0:cols], raw[:, s, 0:cols], ACT.Copy).then_inc(w_hi_done, 1)

            def split_in(pair0, i, s, cols):
                act.wait_ge(w_loaded[s], 16 * (pair0 + i) + 16)
                act.wait_ge(gemm_done, 4 * (pair0 + i) + (2 * s + 2))
                S.activation(w_hi[:, s, 0:cols], raw[:, s, 0:cols], ACT.Copy).then_inc(w_hi_done, 1)

            def split_next(unit):
                if unit + 1 < N_UNITS:
                    split(unit + 1, (unit + 1) % 2, UNIT_COLS[unit + 1])

            def pairs(phase, post, per_pair=2):
                u0, n, cols = UNIT0[phase], UNITS[phase], UNIT_COLS[UNIT0[phase]]
                trips = n // per_pair
                if trips > 1:
                    with act.Fori(0, trips - 1) as i:
                        for j in range(per_pair):
                            q = (j + 1) // 2
                            split_in(u0 // 2 + q, i * (per_pair // 2), (j + 1) % 2, cols)
                            post(i, j)
                for j in range(per_pair):
                    split_next(u0 + n - per_pair + j)
                    post(trips - 1, j)

            def up(f):
                conv = f >= 2
                u0, n0 = UNIT0[f"up{f}"], F0[f]
                vc = VCOL["ffn_conv_w_2"] + 3 * KF * (f - 2)
                vb = VCOL["ffn_conv_b_2"] + KF * (f - 2)

                def post(i, s):
                    act.wait_ge(gemm_done, 2 * u0 + 4 * i + (2 * s + 5))
                    if conv:
                        n = 2 * i + s
                        S.activation(conv_out[:, s, :], bank[:, 2 * s, :], ACT.Identity,
                                     scale=vec[:, bass.ds(vc + 2 * KF + n, 1)],
                                     bias=vec[:, bass.ds(vb + n, 1)]).then_inc(conv0, 1)
                        act.wait_ge(conv_done, 2 * (n0 - F0[2]) + 4 * i + (2 * s + 2))
                        S.activation(act_out[:, s, :], conv_out[:, s, :],
                                     ACT.Gelu_apprx_tanh).then_inc(gate_done, 1)
                    else:
                        S.activation(act_out[:, s, :], bank[:, 2 * s, :], ACT.Silu).then_inc(gate_done, 1)
                    act.wait_ge(banks_free, u0 + 2 * i + (s + 3))
                    S.activation(h_hi[:, bass.ds(2 * i + s, 1), :], h32[:, s:s + 1, :],
                                 ACT.Copy).then_inc(h_hi_done, 1)
                pairs(f"up{f}", post)

            def end_rms(phase, y):
                u0, down = UNIT0[phase], phase[0] == "d"

                def post(i, j):
                    if down and j % 2 == 0:
                        return
                    n = 2 * i + (j // 2 if down else j)
                    act.wait_ge(gemm_done, 2 * u0 + (8 if down else 4) * i + (2 * j + 6))
                    if down:
                        src, dst, sqd = bank[:, 4 + j // 2:5 + j // 2, :], y[:, bass.ds(n, 1), :], sq[:, 0:1, :]
                    else:
                        src, dst, sqd = bank[:, 2 * j:2 * j + 2, :], y[:, bass.ds(2 * n, 2), :], sq[:, :, :]
                    S.activation(dst, src, ACT.Copy).then_inc(y_copied, 1)
                    act.wait_ge(banks_free, u0 + (4 * i + 2 * (j // 2) if down else 2 * i + j) + 2)
                    S.activation(sqd, src, ACT.Square).then_inc(sq_done, 1)
                pairs(phase, post, 4 if down else 2)

            def end_ln(phase):
                u0, down = UNIT0[phase], phase[0] == "d"

                def post(i, j):
                    if down and j % 2 == 0:
                        return
                    n = 2 * i + (j // 2 if down else j)
                    act.wait_ge(banks_free, u0 + (4 if down else 2) * i + (j + 3))
                    act.wait_ge(acc_done, ACC0[phase] + 2 * n + 1)
                    if down:
                        S.activation(sq[:, 0:1, :], x[:, bass.ds(n, 1), :], ACT.Square).then_inc(sq_done, 1)
                    else:
                        S.activation(sq[:, :, :], x[:, bass.ds(2 * n, 2), :], ACT.Square).then_inc(sq_done, 1)
                pairs(phase, post, 4 if down else 2)

            def root(name):
                act.wait_ge(stats, ST0[name] + 1)
                S.activation(rstd[:, :], bank[:, 6, :], ACT.Sqrt, bias=eps6).then_inc(stat_a, 1)

            def ln_stats(name):
                act.wait_ge(stats, ST0[name] + 1)
                S.activation(mean[:, :], bank[:, 6, :], ACT.Copy).then_inc(stat_a, 1)
                S.activation(rstd[:, :], bank[:, 6, :], ACT.Square).then_inc(stat_a, 1)
                act.wait_ge(stat_v, SV0[name] + 2)
                S.activation(rstd[:, :], rstd[:, :], ACT.Sqrt, bias=eps5).then_inc(stat_a, 1)

            def ln_tile(name, k):
                which, layer = GAINS[name]
                g0, b0 = VCOL[which + "_g_2"] + 8 * layer + k, VCOL[which + "_b_2"] + 8 * layer + k
                nxt = NEXT[name]
                act.wait_ge(norm_t, NORM0[nxt or "out"] + k + 1)
                if nxt:
                    S.activation(a_hi[:, k, :], nt[:, k % 2, :], ACT.Identity, scale=vec[:, g0:g0 + 1],
                                 bias=vec[:, b0:b0 + 1]).then_inc(a_hi_done, 1)
                S.activation(x[:, k, :], nt[:, k % 2, :], ACT.Identity, scale=vec[:, g0:g0 + 1],
                             bias=vec[:, b0:b0 + 1]).then_inc(x_act, 1)

            def squares_of_x(name, ready):
                for k in range(KD):
                    act.wait_ge(*ready(k))
                    if k:
                        act.wait_ge(acc_done, ACC0[name] + 1 + k)
                    S.activation(sq[:, 0, :], x[:, k, :], ACT.Square).then_inc(sq_done, 1)

            def normalised(gen):
                for k in range(KD):
                    act.wait_ge(norm_t, NORM0[gen] + k + 1)
                    S.activation(a_hi[:, k, :], nt[:, k % 2, :], ACT.Copy).then_inc(a_hi_done, 1)

            def mlstm_head(h):
                act.wait_ge(SIG["mlstm_m_mm"], h + 1)
                for s in range(NT):
                    act.wait_ge(SIG["mlstm_arg"], 4 * h + s + 1)
                    S.activation(mp[:, s * T + s * P:(s + 1) * T], mp[:, s * T + s * P:(s + 1) * T],
                                 ACT.Exp).then_inc(SIG["mlstm_weight"], 1)
                act.wait_ge(SIG["mlstm_den_mm"], h + 1)
                S.activation(mtmp[:, 0, :], bank[:, 4, :], ACT.Abs, scale=float(D)).then_inc(SIG["mlstm_absden"], 1)
                act.wait_ge(SIG["mlstm_h"], h + 1)
                S.activation(mtmp[:, 1, :], mtmp[:, 0, :], ACT.Square).then_inc(SIG["mlstm_square"], 1)
                act.wait_ge(SIG["mlstm_ms_mm"], h + 1)
                S.activation(mtmp[:, 2, :], bank[:, 6, :], ACT.Sqrt, scale=float(D // P),
                             bias=eps6).then_inc(SIG["mlstm_rms"], 1)

            act.wait_ge(consts_v, 1)
            split(0, 0, FULL)
            squares_of_x("x0", lambda k: (x_in[k], 16))
            root("x0")
            normalised("up0")
            up(0)
            end_rms("down0", y_ff)
            root("down0")
            squares_of_x("pre_mixin", lambda k: (x_dve, XDVE0["down0"] + k + 1))
            root("pre_mixin")
            normalised("mixin")

            mi = UNIT0["mixin"]
            act.wait_ge(mix_in, 80)
            S.activation(wg_hi[:, :, :], wg_raw[:, :, :], ACT.Copy).then_inc(SIG["gate_w_hi"], 1)
            act.wait_ge(SIG["lb_diff"], 1)
            S.activation(lb[:, 0, :], lb[:, 0, :], ACT.Exp).then_inc(SIG["lb_exp"], 1)
            S.activation(lb[:, 1, :], lb[:, 1, :], ACT.Exp).then_inc(SIG["lb_exp"], 1)
            for u in range(2):
                split_next(mi + u)
                for m in range(2):
                    t = 2 * u + m
                    act.wait_ge(gemm_done, gemm_at(mi + u, m))
                    S.activation(mqk[:, t, :], bank[:, 2 * u + m, :], ACT.Identity,
                                 scale=vec[:, VCOL["conv_w"] + 12 + t:VCOL["conv_w"] + 13 + t],
                                 bias=vec[:, VCOL["conv_b"] + t:VCOL["conv_b"] + t + 1]).then_inc(SIG["mconv_start"], 1)
            for t in range(4):
                act.wait_ge(SIG["mconv_done"], t + 1)
                S.activation(mqk[:, t, :], mqk[:, t, :], ACT.Silu).then_inc(SIG["mqk_ready"], 1)
            act.wait_ge(SIG["gate_rows_mm"], 1)
            S.activation(row_i[:, :], bank[0:HEADS, 4, :], ACT.Identity, bias=gbias[0:HEADS, 0:1]).then_inc(SIG["i_row"], 1)
            link(S.activation(row_b[:, :], bank[32:32 + HEADS, 4, :], ACT.Identity, bias=gbias[0:HEADS, 1:2]))
            link(S.activation(row_t[:, :], row_b[:, :], ACT.Abs))
            link(S.activation(row_t[:, :], row_t[:, :], ACT.Exp, scale=-1.0))
            S.activation(row_t[:, :], row_t[:, :], ACT.Ln, bias=one[0:HEADS, :]).then_inc(SIG["f_row_log"], 1)
            for u in (2, 3):
                split_next(mi + u)
                act.wait_ge(gemm_done, gemm_at(mi + u))
                S.activation(mv_tm[:, :, (u - 2) * 256:(u - 1) * 256],
                             bank[:, 2 * (u % 2):2 * (u % 2) + 2, :].rearrange("p b (t c) -> p (b t) c", t=2),
                             ACT.Copy).then_inc(SIG["mlstm_v"], 1)
            act.wait_ge(SIG["neg_bm_row"], 1)
            S.activation(row_em[:, :], row_em[:, :], ACT.Exp).then_inc(SIG["exp_neg_m"], 1)
            for u in (4, 5):
                split_next(mi + u)
                act.wait_ge(gemm_done, gemm_at(mi + u))
                S.activation(mgate[:, 2 * (u - 4):2 * (u - 4) + 2, :], bank[:, 2 * (u % 2):2 * (u % 2) + 2, :],
                             ACT.Sigmoid).then_inc(SIG["mlstm_gate"], 1)
            for h in range(HEADS):
                for j in range(2):
                    u = 6 + 2 * h + j
                    b = 2 * (u % 2)
                    split_next(mi + u)
                    act.wait_ge(gemm_done, gemm_at(mi + u))
                    four = bank[:, b:b + 2, :].rearrange("p b (t c) -> p (b t) c", t=2)
                    if h == 0:
                        if j == 1:
                            act.wait_ge(SIG["forget_ready"], 1)
                        S.activation(sigm[:, :, :, :].rearrange("p a t c -> p (a t) c"), four,
                                     ACT.Sigmoid).then_inc(SIG["hgrn_input"], 1)
                    elif h == 1:
                        S.activation(v_tm[:, :, j * 256:(j + 1) * 256], four, ACT.Copy).then_inc(SIG["hgrn_input"], 1)
                    else:
                        dst = q_fm if h == 2 else hgate
                        S.activation(dst[:, 2 * j:2 * j + 2, :], bank[:, b:b + 2, :], ACT.Silu).then_inc(SIG["hgrn_input"], 1)
                mlstm_head(h)

            act.wait_ge(SIG["keys_tm"], 1)
            S.activation(logf[:, :, :], logf[:, :, :], ACT.Ln).then_inc(SIG["logf_ready"], 1)
            act.wait_ge(SIG["cum_decay_mm"], 1)
            S.activation(Gc[:, :, :], bank[:, 0:4, :], ACT.Copy).then_inc(SIG["cum_decay"], 1)
            act.wait_ge(SIG["keys_transposed"], 1)
            S.activation(k_fm[:, :, :], bank[:, 4:8, :], ACT.Copy).then_inc(SIG["keys_fm"], 1)
            act.wait_ge(SIG["rest_decay_mm"], 1)
            S.activation(lev[0][:, :, :], bank[:, 0:4, :], ACT.Exp).then_inc(SIG["rest_decay"], 1)
            S.activation(q_dec[:, :, :], Gc[:, :, :], ACT.Exp).then_inc(SIG["q_decay"], 1)
            act.wait_ge(SIG["keys_decayed"], 1)
            S.activation(g_end[:, :], Gc[:, :, :].rearrange("p h (n c) -> p (h n) c", c=CHUNK)[:, :, CHUNK - 1],
                         ACT.Exp).then_inc(SIG["chunk_decay"], 1)
            for l in range(len(LEVELS)):
                act.wait_ge(SIG["level_diff"], l + 1)
                S.activation(lev[l % 2][:, :, :], lev[l % 2][:, :, :], ACT.Exp).then_inc(SIG["level_exp"], 1)
            for h in range(HEADS):
                act.wait_ge(SIG["hgrn_out_mm"], h + 1)
                S.activation(lev[1][:, h, :], bank[:, h, :], ACT.Square).then_inc(SIG["hgrn_square"], 1)
            for h in range(HEADS):
                act.wait_ge(SIG["hgrn_ms_mm"], h + 1)
                S.activation(lev[0][:, h, :], bank[:, 4 + h, :], ACT.Sqrt, scale=float(D // P),
                             bias=eps6).then_inc(SIG["hgrn_rms"], 1)
            for k in range(KD):
                act.wait_ge(SIG["hgrn_y"], min(k, HEADS - 1) + 1)
                src = hgate[:, k, :] if k < HEADS else mgate[:, k - HEADS, :]
                S.activation(a_hi[:, k, :], src, ACT.Copy).then_inc(a_hi_done, 1)
            end_rms("mixout", y_mix)
            root("mixout")
            squares_of_x("pre_up1", lambda k: (x_dve, XDVE0["mixout"] + k + 1))
            root("pre_up1")
            normalised("up1")
            up(1)
            end_rms("down1", y_ff)
            root("down1")
            for k in range(KD):
                act.wait_ge(x_dve, XDVE0["down1"] + k + 1)
                S.activation(a_hi[:, k, :], x[:, k, :], ACT.Copy).then_inc(a_hi_done, 1)

            ab = UNIT0["ab"]
            for u in range(2):
                split_next(ab + u)
                act.wait_ge(gemm_done, gemm_at(ab + u))
                S.activation(gv[:, :, u * 256:(u + 1) * 256],
                             bank[:, 2 * u:2 * u + 2, :].rearrange("p b (t c) -> p (b t) c", t=2),
                             ACT.Gelu_apprx_tanh).then_inc(SIG["sgu_v"], 1)
            for u in (2, 3):
                split_next(ab + u)
                act.wait_ge(gemm_done, gemm_at(ab + u))
                S.activation(ug[:, 2 * (u - 2):2 * (u - 2) + 2, :], bank[:, 2 * (u % 2):2 * (u % 2) + 2, :],
                             ACT.Gelu_apprx_tanh).then_inc(SIG["sgu_u"], 1)
            act.wait_ge(SIG["sgu_stats"], 4)
            S.activation(rs4[:, :], mv4[:, :, 1], ACT.Sqrt, bias=eps5).then_inc(SIG["sgu_std"], 1)
            for u in (4, 5):
                split_next(ab + u)
                act.wait_ge(gemm_done, gemm_at(ab + u))
                S.activation(pool[0][:, 2 * (u - 4):2 * (u - 4) + 2, PAD:PAD + T],
                             bank[:, 2 * (u % 2):2 * (u % 2) + 2, :], ACT.Copy).then_inc(SIG["pool_in"], 1)
            act.wait_ge(mem_in, 16)
            S.activation(mem_hi[:, :, :], mem_raw[:, :, :], ACT.Copy).then_inc(SIG["mem_hi_done"], 1)
            for k in range(KD):
                act.wait_ge(*((SIG["ab_ya"], k + 1) if k < 4 else (SIG["ab_yb"], k - 3)))
                src = ug[:, k, :] if k < 4 else pool[1][:, k - 4, PAD:PAD + T]
                S.activation(a_hi[:, k, :], src, ACT.Copy).then_inc(a_hi_done, 1)
            for layer in range(2):
                if layer == 1:
                    ci = UNIT0["cin"]
                    cw = VCOL["c_conv_w_2"]
                    act.wait_ge(mem_in, 32)
                    S.activation(mem_hi[:, :, :], mem_raw[:, :, :], ACT.Copy).then_inc(SIG["mem_hi_done"], 1)
                    for u in range(12):
                        split_next(ci + u)
                        if u < 8:
                            b = 2 * (u % 2)
                            act.wait_ge(gemm_done, gemm_at(ci + u, 0))
                            if u >= 2:
                                act.wait_ge(SIG["c_product"], u - 2 + 1)
                            S.activation(cc[:, u % 2, :], bank[:, b, :], ACT.Copy).then_inc(SIG["c_gate"], 1)
                            act.wait_ge(SIG["c_product"], u + 1)
                            S.activation(yc[:, u, :], ch[:, u % 2, :], ACT.Copy,
                                         scale=vec[:, cw + 16 + u:cw + 17 + u]).then_inc(SIG["c_conv_start"], 1)
                    for k in range(KD):
                        act.wait_ge(SIG["c_y"], 4)
                        S.activation(a_hi[:, k, :], yc[:, k, :], ACT.Copy).then_inc(a_hi_done, 1)
                end = ("about", "cout")[layer]
                end_ln(end)
                ln_stats(end)
                kv = UNIT0[f"kv{layer}"]
                for k in range(KD):
                    ln_tile(end, k)
                    split_next(kv + k)
                    b = 2 * (k % 2)
                    act.wait_ge(gemm_done, gemm_at(kv + k))
                    dst = k_mem[:, 2 * k:2 * k + 2, :] if k < 4 else v_mem[:, :, (k - 4) * 256:(k - 3) * 256]
                    S.activation(dst, bank[:, b:b + 2, 0:MEM], ACT.Copy).then_inc(SIG["mem_kv"], 1)
                q0 = UNIT0[f"q{layer}"]
                for u in range(4):
                    split_next(q0 + u)
                    act.wait_ge(gemm_done, gemm_at(q0 + u))
                    S.activation(q_at[:, 2 * u:2 * u + 2, :], bank[:, 2 * (u % 2):2 * (u % 2) + 2, :],
                                 ACT.Copy).then_inc(SIG["attn_q"], 1)
                scale = 256.0 ** -0.5
                for h in range(HEADS + 1):
                    if h < HEADS:
                        act.wait_ge(SIG["attn_max"], 4 * layer + h + 1)
                        for t in range(NT):
                            S.activation(pe_at[:, h % 2, t, :],
                                         bank[:, 2 * (h % 2) + t // 2, (t % 2) * MEM:(t % 2) * MEM + MEM],
                                         ACT.Exp, scale=scale, bias=at_s[:, h % 2, 1, t:t + 1],
                                         accum_out=at_s[:, h % 2, 2, t:t + 1]).then_inc(SIG["attn_exp"], 1)
                    if h:
                        g = h - 1
                        act.wait_ge(SIG["probs_transposed"], 4 * layer + g + 1)
                        S.activation(p_t[:, g % 2, :, :], bank[:, 4:6, :], ACT.Copy).then_inc(SIG["probs_t"], 1)
                        act.wait_ge(SIG["attn_o32"], 4 * layer + g + 1)
                        for d in range(2):
                            S.activation(a_hi[:, 2 * g + d, :], o32[:, d, :], ACT.Copy).then_inc(a_hi_done, 1)
                end = f"wo{layer}"
                end_ln(end)
                ln_stats(end)
                for k in range(KD):
                    ln_tile(end, k)
                up(2 + layer)
                end = f"down{2 + layer}"
                end_ln(end)
                ln_stats(end)
                for k in range(KD):
                    ln_tile(end, k)

        @block.vector
        def _(dve):
            links = [0]

            def link(ins):
                links[0] += 1
                ins.then_inc(dve_link, 1)
                dve.wait_ge(dve_link, links[0])

            def split(unit, s, cols):
                dve.wait_ge(w_hi_done, unit + 1)
                V.tensor_tensor(w_lo[:, s, 0:cols], raw[:, s, 0:cols], w_hi[:, s, 0:cols],
                                ALU.subtract).then_inc(w_split, 1)

            def split_next(unit):
                if unit + 1 < N_UNITS:
                    split(unit + 1, (unit + 1) % 2, UNIT_COLS[unit + 1])

            def pairs(phase, post, per_pair=2):
                u0, n, cols = UNIT0[phase], UNITS[phase], UNIT_COLS[UNIT0[phase]]
                trips = n // per_pair
                if trips > 1:
                    with dve.Fori(0, trips - 1) as i:
                        for j in range(per_pair):
                            split(u0 + per_pair * i + (j + 1), (j + 1) % 2, cols)
                            post(i, j)
                for j in range(per_pair):
                    split_next(u0 + n - per_pair + j)
                    post(trips - 1, j)

            def up(f):
                conv = f >= 2
                u0, n0 = UNIT0[f"up{f}"], F0[f]
                vc = VCOL["ffn_conv_w_2"] + 3 * KF * (f - 2)

                def post(i, s):
                    n = 2 * i + s
                    if conv:
                        c0 = 2 * (n0 - F0[2]) + 4 * i + 2 * s
                        dve.wait_ge(conv0, (n0 - F0[2]) + n + 1)
                        for tap in (1, 2):
                            V.scalar_tensor_tensor(conv_out[:, s, tap:T], bank[:, 2 * s, 0:T - tap],
                                                   vec[:, bass.ds(vc + (2 - tap) * KF + n, 1)],
                                                   conv_out[:, s, tap:T], ALU.mult, ALU.add).then_inc(conv_done, 1)
                            if tap == 1:
                                dve.wait_ge(conv_done, c0 + 1)
                    dve.wait_ge(gate_done, n0 + n + 1)
                    dve.wait_ge(gemm_done, 2 * u0 + 4 * i + (2 * s + 6))
                    V.tensor_tensor(h32[:, s, :], act_out[:, s, :], bank[:, 2 * s + 1, :],
                                    ALU.mult).then_inc(banks_free, 1)
                    dve.wait_ge(h_hi_done, n0 + n + 1)
                    V.tensor_tensor(h_lo[:, bass.ds(n, 1), :], h32[:, s:s + 1, :], h_hi[:, bass.ds(n, 1), :],
                                    ALU.subtract).then_inc(h_done, 1)
                pairs(f"up{f}", post)

            def clear_acc(name, *read):
                dve.wait_ge(*read)
                V.memset(acc[:, :, :, :], 0.0).then_inc(acc_done, 1)
                dve.wait_ge(acc_done, ACC0[name] + 1)

            def end_rms(phase):
                u0, down = UNIT0[phase], phase[0] == "d"

                def post(i, j):
                    if down and j % 2 == 0:
                        return
                    n = 2 * i + (j // 2 if down else j)
                    dve.wait_ge(sq_done, SQ0[phase] + n + 1)
                    dve.wait_ge(banks_free, u0 + (4 * i + 2 * (j // 2) if down else 2 * i + j) + 2)
                    if down:
                        V.tensor_tensor(acc[:, 1, j // 2, :], acc[:, 1, j // 2, :], sq[:, 0, :],
                                        ALU.add).then_inc(banks_free, 2)
                    else:
                        V.tensor_tensor(acc[:, 1, :, :], acc[:, 1, :, :], sq[:, :, :],
                                        ALU.add).then_inc(banks_free, 1)
                pairs(phase, post, 4 if down else 2)

            def end_ln(phase):
                u0, down = UNIT0[phase], phase[0] == "d"

                def post(i, j):
                    if down and j % 2 == 0:
                        return
                    n = 2 * i + (j // 2 if down else j)
                    dve.wait_ge(gemm_done, 2 * u0 + (8 if down else 4) * i + (2 * j + 6))
                    if down:
                        xs, ys, par = x[:, bass.ds(n, 1), :], bank[:, 4 + j // 2:5 + j // 2, :], slice(j // 2, j // 2 + 1)
                    else:
                        xs, ys, par = x[:, bass.ds(2 * n, 2), :], bank[:, 2 * j:2 * j + 2, :], slice(0, 2)
                    V.scalar_tensor_tensor(xs, xs, ALPHA, ys, ALU.mult, ALU.add).then_inc(banks_free, 2 if down else 1)
                    dve.wait_ge(banks_free, u0 + (4 if down else 2) * i + (j + 3))
                    dve.wait_ge(acc_done, ACC0[phase] + 2 * n + 1)
                    V.tensor_tensor(acc[:, 0, par, :], acc[:, 0, par, :], xs, ALU.add).then_inc(acc_done, 1)
                    dve.wait_ge(sq_done, SQ0[phase] + n + 1)
                    V.tensor_tensor(acc[:, 1, par, :], acc[:, 1, par, :],
                                    sq[:, 0:1, :] if down else sq[:, :, :], ALU.add).then_inc(acc_done, 1)
                pairs(phase, post, 4 if down else 2)

            def inverse_root(name):
                dve.wait_ge(stat_a, SA0[name] + 1)
                V.reciprocal(rstd[:, :], rstd[:, :]).then_inc(stat_v, 1)
                dve.wait_ge(stat_v, SV0[name] + 1)

            def residual(name, y, gains):
                for k in range(KD):
                    link(V.tensor_tensor(nt[:, k % 2, :], y[:, k, :], rstd[:, :], ALU.mult))
                    V.scalar_tensor_tensor(x[:, k, :], nt[:, k % 2, :], gains[:, k:k + 1], x[:, k, :],
                                           ALU.mult, ALU.add).then_inc(x_dve, 1)

            def add_squares(name, *read):
                clear_acc(name, *read)
                for k in range(KD):
                    dve.wait_ge(sq_done, SQ0[name] + k + 1)
                    if k:
                        dve.wait_ge(acc_done, ACC0[name] + 1 + k)
                    V.tensor_tensor(acc[:, 1, k % 2, :], acc[:, 1, k % 2, :], sq[:, 0, :],
                                    ALU.add).then_inc(acc_done, 1)

            def normalise(gen, g0):
                def low(k):
                    dve.wait_ge(a_hi_done, gen_at(gen, k))
                    V.tensor_tensor(a_lo[:, k, :], nt[:, k % 2, :], a_hi[:, k, :], ALU.subtract).then_inc(a_done, 1)
                for k in range(KD):
                    if k >= 2:
                        low(k - 2)
                        dve.wait_ge(a_done, gen_at(gen, k - 2))
                    V.scalar_tensor_tensor(nt[:, k % 2, :], x[:, k, :], vec[:, g0 + k:g0 + k + 1], rstd[:, :],
                                           ALU.mult, ALU.mult).then_inc(norm_t, 1)
                    dve.wait_ge(norm_t, NORM0[gen] + k + 1)
                low(KD - 2)
                low(KD - 1)

            def ln_stats(name):
                dve.wait_ge(stat_a, SA0[name] + 2)
                V.tensor_tensor(rstd[:, :], bank[:, 7, :], rstd[:, :], ALU.subtract).then_inc(stat_v, 1)
                dve.wait_ge(stat_v, SV0[name] + 1)
                V.tensor_scalar(rstd[:, :], rstd[:, :], 0.0, None, ALU.max).then_inc(stat_v, 1)
                dve.wait_ge(stat_a, SA0[name] + 3)
                V.reciprocal(rstd[:, :], rstd[:, :]).then_inc(stat_v, 1)
                dve.wait_ge(stat_v, SV0[name] + 3)

            def ln_norm(name, k):
                n0 = NORM0[NEXT[name] or "out"]
                if k >= 2:
                    dve.wait_ge(x_act, XACT0[name] + k - 1)
                link(V.tensor_tensor(nt[:, k % 2, :], x[:, k, :], mean[:, :], ALU.subtract))
                V.tensor_tensor(nt[:, k % 2, :], nt[:, k % 2, :], rstd[:, :], ALU.mult).then_inc(norm_t, 1)

            def ln_low(name, k):
                if NEXT[name]:
                    dve.wait_ge(a_hi_done, gen_at(NEXT[name], k))
                    dve.wait_ge(x_act, XACT0[name] + k + 1)
                    V.tensor_tensor(a_lo[:, k, :], x[:, k, :], a_hi[:, k, :], ALU.subtract).then_inc(a_done, 1)

            def low_parts(gen, srcs):
                for k in range(KD):
                    dve.wait_ge(a_hi_done, gen_at(gen, k))
                    V.tensor_tensor(a_lo[:, k, :], srcs(k), a_hi[:, k, :], ALU.subtract).then_inc(a_done, 1)

            def mlstm_head(h):
                dve.wait_ge(SIG["mlstm_m_mm"], h + 1)
                for s in range(NT):
                    V.tensor_scalar(mp[:, s * T + s * P:(s + 1) * T], bank[:, 4, s * P:T],
                                    ct[:, s, h:h + 1], 0.0, ALU.add, ALU.min).then_inc(SIG["mlstm_arg"], 1)
                for s in range(NT):
                    dve.wait_ge(SIG["mlstm_scores_mm"], 4 * h + s + 1)
                    dve.wait_ge(SIG["mlstm_weight"], 4 * h + s + 1)
                    V.scalar_tensor_tensor(mp[:, s * T + s * P:(s + 1) * T], bank[:, 5 + s % 2, s * P:T], 64.0 ** -0.5,
                                           mp[:, s * T + s * P:(s + 1) * T], ALU.mult, ALU.mult).then_inc(SIG["mlstm_p"], 1)
                dve.wait_ge(SIG["mlstm_p"], 4 * h + NT)
                diag = mp[:, :].rearrange("p (s c) -> p s c", s=NT)[:, :, 0:P]
                V.tensor_tensor(diag, diag, tri[:, 0:1, :].broadcast_to([P, NT, P]), ALU.mult).then_inc(SIG["mlstm_masked"], 1)
                dve.wait_ge(SIG["mlstm_absden"], h + 1)
                dve.wait_ge(SIG["mlstm_em_mm"], h + 1)
                V.tensor_tensor(mtmp[:, 0, :], mtmp[:, 0, :], bank[:, 5, :], ALU.max).then_inc(SIG["mlstm_den"], 1)
                dve.wait_ge(SIG["mlstm_den"], h + 1)
                link(V.reciprocal(mtmp[:, 0, :], mtmp[:, 0, :]))
                V.tensor_tensor(mtmp[:, 0, :], mtmp[:, 0, :], bank[:, 7, :], ALU.mult).then_inc(SIG["mlstm_h"], 1)
                dve.wait_ge(SIG["mlstm_rms"], h + 1)
                link(V.reciprocal(mtmp[:, 2, :], mtmp[:, 2, :]))
                link(V.tensor_tensor(mtmp[:, 0, :], mtmp[:, 0, :], mtmp[:, 2, :], ALU.mult))
                c0 = VCOL["mlstm_norm"] + h
                V.scalar_tensor_tensor(mgate[:, h, :], mtmp[:, 0, :], vec[:, c0:c0 + 1], mgate[:, h, :],
                                       ALU.mult, ALU.mult).then_inc(SIG["mlstm_y"], 1)

            V.memset(mean_w[:, :], 1.0 / D)
            V.memset(eps6, 1e-6)
            V.memset(eps5, 1e-5)
            V.memset(one, 1.0).then_inc(consts_v, 1)
            dve.sem_inc(w_split, SLOTS)
            dve.sem_inc(gemm_done, 4)
            dve.sem_inc(banks_free, 2)
            dve.wait_ge(consts, 32)
            link(V.tensor_scalar(half_g[:, :], vec[:, VCOL["norm_post"]:VCOL["norm_post"] + 24], 0.5, None, ALU.mult))
            split(0, 0, FULL)
            add_squares("x0", consts_v, 1)
            inverse_root("x0")
            normalise("up0", VCOL["norm_pre"])
            up(0)
            clear_acc("down0", h_done, F0[0] + KF)
            end_rms("down0")
            inverse_root("down0")
            residual("down0", y_ff, half_g[:, 0:8])
            add_squares("pre_mixin", x_dve, XDVE0["down0"] + KD)
            inverse_root("pre_mixin")
            normalise("mixin", VCOL["norm_pre"] + 8)

            mi = UNIT0["mixin"]
            dve.wait_ge(mix_in, 80)
            V.tensor_tensor(lb[:, 0, :], lbt[:, 1, :], lbt[:, 0, :], ALU.subtract)
            V.tensor_tensor(lb[:, 1, :], lbt[:, 0, :], lbt[:, 1, :], ALU.subtract).then_inc(SIG["lb_diff"], 1)
            dve.wait_ge(SIG["gate_w_hi"], 1)
            V.tensor_tensor(wg_lo[:, :, :], wg_raw[:, :, :], wg_hi[:, :, :], ALU.subtract).then_inc(SIG["gate_w_lo"], 1)
            dve.wait_ge(SIG["lb_exp"], 2)
            link(V.tensor_scalar(lb[:, :, :], lb[:, :, :], 1.0, None, ALU.add))
            link(V.reciprocal(lb[:, :, :], lb[:, :, :]))
            cw = VCOL["conv_w"]
            for u in range(2):
                split_next(mi + u)
                for m in range(2):
                    t = 2 * u + m
                    dve.wait_ge(SIG["mconv_start"], t + 1)
                    for tap in (1, 2, 3):
                        ins = V.scalar_tensor_tensor(mqk[:, t, tap:T], bank[:, 2 * u + m, 0:T - tap],
                                                     vec[:, cw + 4 * (3 - tap) + t:cw + 4 * (3 - tap) + t + 1],
                                                     mqk[:, t, tap:T], ALU.mult, ALU.add)
                        if tap < 3:
                            link(ins)
                        else:
                            ins.then_inc(SIG["mconv_done"], 1)
                dve.wait_ge(SIG["mconv_done"], 2 * u + 1 + 1)
                dve.sem_inc(banks_free, 1)
            def value_unit(u):
                split_next(mi + u)
                dve.wait_ge(SIG["mlstm_v"], u - 1)
                dve.sem_inc(banks_free, 1)

            def scan(op):
                for n in range(9):
                    d = 1 << n
                    src, dst = rows[:, n % 2, :], rows[:, 1 - n % 2, :]
                    link(V.tensor_tensor(dst[:, 256:256 + T], src[:, 256:256 + T], src[:, 256 - d:256 - d + T], op))

            value_unit(2)
            V.memset(rows[:, :, 0:256], 0.0)
            dve.wait_ge(SIG["f_row_log"], 1)
            link(V.scalar_tensor_tensor(rows[:, 0, 256:256 + T], row_b[:, :], 0.0, row_t[:, :], ALU.min, ALU.subtract))
            scan(ALU.add)
            link(V.tensor_copy(row_b[:, :], rows[:, 1, 256:256 + T]))
            V.tensor_tensor(row_t[:, :], row_i[:, :], row_b[:, :], ALU.subtract).then_inc(SIG["c_row"], 1)
            value_unit(3)
            dve.wait_ge(SIG["c_row"], 1)
            link(V.tensor_scalar(rows[:, 0, 256:256 + T], row_t[:, :], 0.0, None, ALU.max))
            scan(ALU.max)
            V.tensor_scalar(row_nm[:, :], rows[:, 1, 256:256 + T], -1.0, None, ALU.mult).then_inc(SIG["neg_m_row"], 1)
            dve.wait_ge(SIG["neg_m_row"], 1)
            V.tensor_tensor(row_em[:, :], row_nm[:, :], row_b[:, :], ALU.subtract).then_inc(SIG["neg_bm_row"], 1)
            for u in (4, 5):
                split_next(mi + u)
                dve.wait_ge(SIG["mlstm_gate"], u - 4 + 1)
                dve.sem_inc(banks_free, 1)
            dve.wait_ge(SIG["c_columns_mm"], 1)
            V.tensor_copy(ct[:, :, :], bank[:, 5, 0:NT * HEADS].rearrange("p (s h) -> p s h", h=HEADS)
                          ).then_inc(SIG["c_columns"], 1)
            dve.wait_ge(SIG["c_columns"], 1)
            for h in range(HEADS):
                for j in range(2):
                    u = 6 + 2 * h + j
                    split_next(mi + u)
                    dve.wait_ge(SIG["hgrn_input"], 2 * h + j + 1)
                    dve.sem_inc(banks_free, 1)
                    if h == 0:
                        cols = slice(j * 256, (j + 1) * 256)
                        s4 = sigm[:, :, :, :].rearrange("p a t c -> p (a t) c")
                        link(V.tensor_tensor(s4, s4, lb[:, 1:2, cols].broadcast_to([P, NT, 256]), ALU.mult))
                        V.tensor_tensor(logf[:, :, cols], s4, lb[:, 0:1, cols].broadcast_to([P, NT, 256]),
                                        ALU.add).then_inc(SIG["forget_ready"], 1)
                mlstm_head(h)

            V.tensor_scalar(k_tm[:, :, :], logf[:, :, :], -1.0, 1.0, ALU.mult, ALU.add).then_inc(SIG["keys_tm"], 1)
            dve.wait_ge(SIG["rest_decay"], 1)
            dve.wait_ge(SIG["keys_tm"], 1)
            V.tensor_tensor(kdec[:, :, :], k_tm[:, :, :], lev[0][:, :, :], ALU.mult).then_inc(SIG["keys_decayed"], 1)
            dve.wait_ge(SIG["q_decay"], 1)
            link(V.tensor_tensor(q_dec[:, :, :], q_dec[:, :, :], q_fm[:, :, :], ALU.mult))
            link(V.memset(scores[:, :, :], 0.0))

            def blocks(t, hs):
                return t[:, :, :].rearrange("p h (n two c) -> p (h n) two c", two=2, c=hs)

            def level_dif(l):
                hs = LEVELS[l]
                g, d = blocks(Gc, hs), blocks(lev[l % 2], hs)
                n = HEADS * T // (2 * hs)
                mid = g[:, :, 0, hs - 1:hs].broadcast_to([P, n, hs])
                V.tensor_tensor(d[:, :, 1, :], g[:, :, 1, :], mid, ALU.subtract)
                V.tensor_tensor(d[:, :, 0, :], mid, g[:, :, 0, :], ALU.subtract).then_inc(SIG["level_diff"], 1)

            def level_mul(l):
                hs = LEVELS[l]
                d = blocks(lev[l % 2], hs)
                dve.wait_ge(SIG["level_exp"], l + 1)
                V.tensor_tensor(d[:, :, 1, :], d[:, :, 1, :], blocks(q_fm, hs)[:, :, 1, :], ALU.mult)
                V.tensor_tensor(d[:, :, 0, :], d[:, :, 0, :], blocks(k_fm, hs)[:, :, 0, :], ALU.mult).then_inc(SIG["level_ready"], 1)

            def take_scores(l):
                dve.wait_ge(SIG["level_scores_mm"], l + 1)
                if l:
                    dve.wait_ge(SIG["scores_taken"], l)
                V.copy_predicated(scores[:, :, :].rearrange("p h (n c) -> p (h n) c", c=P),
                                  masks[:, l:l + 1, :].broadcast_to([P, HEADS * NT, P]),
                                  bank[:, 4 * (l % 2):4 * (l % 2) + 4, :].rearrange("p h (n c) -> p (h n) c", c=P)
                                  ).then_inc(SIG["scores_taken"], 1)

            level_dif(0)
            dve.wait_ge(SIG["state_add_mm"], 1)
            link(V.tensor_copy(states[:, 0, :, :], bank[:, 4, :].rearrange("p (h v) -> p h v", h=HEADS)))
            dve.wait_ge(SIG["chunk_decay"], 1)
            for n in (1, 2):
                for h in range(HEADS):
                    ins = V.scalar_tensor_tensor(states[:, n, h, :], states[:, n - 1, h, :],
                                                 g_end[:, h * NT + n:h * NT + n + 1],
                                                 bank[:, 4 + n, h * P:(h + 1) * P], ALU.mult, ALU.add)
                    if h == HEADS - 1 and n == 1:
                        link(ins)
            ins.then_inc(SIG["states_ready"], 1)
            dve.wait_ge(mask_in, 16)
            level_mul(0)
            for l in range(1, len(LEVELS)):
                if l >= 2:
                    dve.wait_ge(SIG["level_scores_mm"], l)
                level_dif(l)
                take_scores(l - 1)
                level_mul(l)
            take_scores(len(LEVELS) - 1)
            take_scores(len(LEVELS))
            for h in range(HEADS):
                dve.wait_ge(SIG["hgrn_rms"], h + 1)
                link(V.reciprocal(lev[0][:, h, :], lev[0][:, h, :]))
                link(V.tensor_tensor(lev[0][:, h, :], lev[0][:, h, :], bank[:, h, :], ALU.mult))
                c0 = VCOL["hgrn_norm"] + h
                V.scalar_tensor_tensor(hgate[:, h, :], lev[0][:, h, :], vec[:, c0:c0 + 1], hgate[:, h, :],
                                       ALU.mult, ALU.mult).then_inc(SIG["hgrn_y"], 1)
            low_parts("mixout", lambda k: hgate[:, k, :] if k < HEADS else mgate[:, k - HEADS, :])
            clear_acc("mixout", a_done, gen_at("mixout"))
            end_rms("mixout")
            inverse_root("mixout")
            residual("mixout", y_mix, vec[:, VCOL["norm_post"] + 8:VCOL["norm_post"] + 16])
            add_squares("pre_up1", x_dve, XDVE0["mixout"] + KD)
            inverse_root("pre_up1")
            normalise("up1", VCOL["norm_pre"] + 16)
            up(1)
            clear_acc("down1", h_done, F0[1] + KF)
            end_rms("down1")
            inverse_root("down1")
            residual("down1", y_ff, half_g[:, 16:24])
            low_parts("ab", lambda k: x[:, k, :])

            ab = UNIT0["ab"]
            for u in range(2):
                split_next(ab + u)
                dve.wait_ge(SIG["sgu_v"], u + 1)
                dve.sem_inc(banks_free, 1)
            for t in range(NT):
                link(V.bn_stats(bn[:, t, :], gv[:, t, :]))
                V.bn_aggr(mv4[:, t, :], bn[:, t, :]).then_inc(SIG["sgu_stats"], 1)
            for u in (2, 3):
                split_next(ab + u)
                dve.wait_ge(SIG["sgu_u"], u - 2 + 1)
                dve.sem_inc(banks_free, 1)
            dve.wait_ge(SIG["sgu_std"], 1)
            link(V.reciprocal(rs4[:, :], rs4[:, :]))
            for t in range(NT):
                ins = V.tensor_scalar(gv[:, t, :], gv[:, t, :], mv4[:, t, 0:1], rs4[:, t:t + 1], ALU.subtract, ALU.mult)
            link(ins)
            dve.wait_ge(ab_in, 64)
            link(V.tensor_tensor(gv[:, :, :], gv[:, :, :], ab_rows[:, 0:1, :].broadcast_to([P, NT, T]), ALU.mult))
            V.memset(ws_t[64:128, :, 0:64], 0.0)
            V.tensor_tensor(gv[:, :, :], gv[:, :, :], ab_rows[:, 1:2, :].broadcast_to([P, NT, T]),
                            ALU.add).then_inc(SIG["sgu_v_ready"], 1)
            for n in range(3):
                V.memset(pool[n][:, :, 0:PAD], 0.0)
            for u in (4, 5):
                split_next(ab + u)
                dve.wait_ge(SIG["pool_in"], u - 4 + 1)
                dve.sem_inc(banks_free, 1)
            dve.wait_ge(SIG["spatial_mm"], 1)
            for g in range(4):
                b4 = bank[:, 4 + g, :].rearrange("p (n c) -> p n c", c=P)
                o4 = gv[:, g, :].rearrange("p (n c) -> p n c", c=P)
                link(V.tensor_tensor(o4, b4, ab_rows[:, 2:3, g * P:(g + 1) * P].broadcast_to([P, NT, P]), ALU.add))
                V.tensor_tensor(ug[:, g, :], ug[:, g, :], gv[:, g, :], ALU.mult).then_inc(SIG["ab_ya"], 1)
            for g in range(4):
                src = pool[0]
                for n in range(g + 1):
                    dst = pool[1 + n % 2]
                    link(V.tensor_tensor(dst[:, g, PAD:PAD + T], src[:, g, PAD:PAD + T],
                                         src[:, g, PAD - (1 << n):PAD - (1 << n) + T], ALU.add))
                    src = dst
                first, rest = slice(PAD, 2 * PAD), slice(2 * PAD, PAD + T)
                link(V.tensor_tensor(src[:, g, first], src[:, g, first], inv_cnt[:, g, :], ALU.mult))
                V.tensor_tensor(pool[2][:, g, first], src[:, g, first], pool[0][:, g, first], ALU.subtract)
                V.scalar_tensor_tensor(pool[2][:, g, rest], src[:, g, rest], 1.0 / (2 << g), pool[0][:, g, rest],
                                       ALU.mult, ALU.subtract).then_inc(SIG["pooled"], 1)
            for g in range(4):
                dve.wait_ge(SIG["pool_mm"], g + 1)
                c0 = VCOL["pool_scale_2"] + g
                V.tensor_scalar(pool[1][:, g, PAD:PAD + T], bank[:, g, :], vec[:, c0:c0 + 1], None,
                                ALU.mult).then_inc(SIG["ab_yb"], 1)
            dve.wait_ge(SIG["mem_hi_done"], 1)
            V.tensor_tensor(mem_lo[:, :, :], mem_raw[:, :, :], mem_hi[:, :, :], ALU.subtract).then_inc(SIG["mem_lo_done"], 1)
            low_parts("about", lambda k: ug[:, k, :] if k < 4 else pool[1][:, k - 4, PAD:PAD + T])
            for layer in range(2):
                if layer == 1:
                    ci, cw = UNIT0["cin"], VCOL["c_conv_w_2"]
                    dve.wait_ge(SIG["mem_hi_done"], 2)
                    V.tensor_tensor(mem_lo[:, :, :], mem_raw[:, :, :], mem_hi[:, :, :],
                                    ALU.subtract).then_inc(SIG["mem_lo_done"], 1)
                    for u in range(12):
                        split_next(ci + u)
                        b = 2 * (u % 2)
                        if u < 8:
                            dve.wait_ge(SIG["c_gate"], u + 1)
                            dve.wait_ge(gemm_done, gemm_at(ci + u))
                            V.tensor_tensor(ch[:, u % 2, :], cc[:, u % 2, :], bank[:, b + 1, :],
                                            ALU.mult).then_inc(SIG["c_product"], 1)
                            dve.wait_ge(SIG["c_product"], u + 1)
                            dve.sem_inc(banks_free, 1)
                            dve.wait_ge(SIG["c_conv_start"], u + 1)
                            for tap in (1, 2):
                                c0 = cw + 8 * (2 - tap) + u
                                link(V.scalar_tensor_tensor(yc[:, u, tap:T], ch[:, u % 2, 0:T - tap],
                                                            vec[:, c0:c0 + 1], yc[:, u, tap:T], ALU.mult, ALU.add))
                        else:
                            j = 2 * (u - 8)
                            dve.wait_ge(gemm_done, gemm_at(ci + u))
                            V.tensor_tensor(yc[:, j:j + 2, :], yc[:, j:j + 2, :], bank[:, b:b + 2, :],
                                            ALU.mult).then_inc(SIG["c_y"], 1)
                            dve.wait_ge(SIG["c_y"], u - 8 + 1)
                            dve.sem_inc(banks_free, 1)
                    low_parts("cout", lambda k: yc[:, k, :])
                end = ("about", "cout")[layer]
                clear_acc(end, a_done, gen_at(end))
                end_ln(end)
                ln_stats(end)
                kv = UNIT0[f"kv{layer}"]
                for k in range(KD):
                    ln_norm(end, k)
                    split_next(kv + k)
                    ln_low(end, k)
                    dve.wait_ge(SIG["mem_kv"], 8 * layer + k + 1)
                    dve.sem_inc(banks_free, 1)
                q0 = UNIT0[f"q{layer}"]
                for u in range(4):
                    split_next(q0 + u)
                    dve.wait_ge(SIG["attn_q"], 4 * layer + u + 1)
                    dve.sem_inc(banks_free, 1)
                for h in range(HEADS + 1):
                    if h < HEADS:
                        p, b = h % 2, 2 * (h % 2)
                        dve.wait_ge(SIG["attn_scores_mm"], 4 * layer + h + 1)
                        link(V.tensor_reduce(at_s[:, p, 0, :], bank[:, b:b + 2, :].rearrange("p b (t m) -> p (b t) m", t=2),
                                             AX.X, ALU.max))
                        V.tensor_scalar(at_s[:, p, 1, :], at_s[:, p, 0, :], -(256.0 ** -0.5), None,
                                        ALU.mult).then_inc(SIG["attn_max"], 1)
                    if h:
                        g = h - 1
                        dve.wait_ge(SIG["attn_out_mm"], 4 * layer + g + 1)
                        if g:
                            dve.wait_ge(a_done, gen_at(f"wo{layer}", 2 * g - 1))
                        V.tensor_copy(o32[:, :, :], bank[:, 6:8, :]).then_inc(SIG["attn_o32"], 1)
                        for d in range(2):
                            dve.wait_ge(a_hi_done, gen_at(f"wo{layer}", 2 * g + d))
                            V.tensor_tensor(a_lo[:, 2 * g + d, :], o32[:, d, :], a_hi[:, 2 * g + d, :],
                                            ALU.subtract).then_inc(a_done, 1)
                    if h < HEADS:
                        dve.wait_ge(SIG["attn_exp"], 16 * layer + 4 * h + 4)
                        link(V.reciprocal(at_s[:, p, 0, :], at_s[:, p, 2, :]))
                        V.tensor_tensor(pe_at[:, p, :, :], pe_at[:, p, :, :],
                                        at_s[:, p, 0, :].unsqueeze(2).broadcast_to([P, NT, MEM]),
                                        ALU.mult).then_inc(SIG["attn_probs"], 1)
                end = f"wo{layer}"
                for end in (f"wo{layer}", f"down{2 + layer}"):
                    if end[0] == "d":
                        up(2 + layer)
                    clear_acc(end, *((h_done, F0[2 + layer] + KF) if end[0] == "d" else (a_done, gen_at(end))))
                    end_ln(end)
                    ln_stats(end)
                    ln_norm(end, 0)
                    for k in range(KD):
                        if k + 1 < KD:
                            ln_norm(end, k + 1)
                        ln_low(end, k)


def kernel(**inputs):
    import numpy as np
    import concourse.bacc as bacc
    from concourse.bass_utils import run_bass_kernel_spmd

    def tiles(w, order):
        n = w.shape[1] // P
        w = w.reshape(KD, P, n, P).transpose(2, 1, 0, 3)[np.asarray(order)]
        return w.reshape(len(order) // 2, 2, P, KD * P).transpose(0, 2, 1, 3).reshape(-1, P, FULL)

    def columns(w, first, n):
        w = w[:, first:first + 256 * n]
        return w.reshape(KD, P, n, 256).transpose(2, 1, 0, 3).reshape(n, P, FULL)

    def down(w):
        return w.reshape(2, HALF_KF, P, KD, P).transpose(3, 0, 2, 1, 4).reshape(16, P, DOWN)

    def both(first, second):
        return [t for j in range(KF) for t in (first + j, second + j)]

    i = inputs
    mix, ab, cin = i["w_mix_in"][0], i["ab_w_in_2"][0], i["c_w_in_2"][0]
    full = [tiles(i["ffn1_w_in"][0], both(0, KF)),
            tiles(mix[:, :3584], [16, 17, 18, 19]), columns(mix, 2560, 2), tiles(mix[:, :3584], [24, 25, 26, 27]),
            columns(mix, 512, 2), columns(mix, 1024, 2),
            tiles(mix[:, :3584], [0, 1, 2, 3]), tiles(mix[:, :3584], [12, 13, 14, 15]),
            tiles(i["w_mix_out"][0], range(KD)),
            tiles(i["ffn2_w_in"][0], both(0, KF)),
            columns(ab, 512, 2), tiles(ab, [0, 1, 2, 3, 8, 9, 10, 11]), tiles(i["ab_w_out_2"][0], range(KD))]
    for layer in range(2):
        wkv = i["xa_wkv_2"][layer]
        if layer:
            full += [tiles(cin, [t for j in range(8) for t in (8 + j, 16 + j)] + list(range(8))),
                     tiles(i["c_w_out_2"][0], range(KD))]
        full += [tiles(wkv[:, :D], range(KD)), columns(wkv, D, 4), tiles(i["xa_wq_2"][layer], range(KD)),
                 tiles(i["xa_wo_2"][layer], range(KD)), tiles(i["ffn_w_up_2"][layer], both(KF, 0))]

    def vector(w):
        return np.asarray(w).reshape(-1, P).T

    steps = np.arange(P)
    s, t = steps[:, None], steps[None, :]
    masks = [s == t] + [(s // (2 * h) == t // (2 * h)) & (s // h % 2 == 0) & (t // h % 2 == 1) for h in LEVELS]
    counts = np.stack([1.0 / np.minimum(np.arange(16) + 1, 2 << g) for g in range(4)])

    def every(w):
        return np.broadcast_to(w, (P,) + w.shape)

    w_gates = np.zeros((D, P), np.float32)
    w_gates[:, 0:HEADS], w_gates[:, 32:32 + HEADS] = mix[:, 3584:3588], mix[:, 3588:3592]
    arrays = {
        "w_full": np.concatenate(full), "w_down": np.concatenate(
            [down(w) for w in (i["ffn1_w_out"][0], i["ffn2_w_out"][0], i["ffn_w_down_2"][0], i["ffn_w_down_2"][1])]),
        "vectors": np.concatenate([vector(i[n]) for n, _ in VECTORS], axis=1),
        "identity": np.eye(P, dtype=np.float32),
        "x": i["x"][0].T.reshape(KD, P, T).transpose(1, 0, 2),
        "w_gates": w_gates.reshape(KD, P, P).transpose(1, 0, 2),
        "gate_bias": i["mlstm_gate_bias"].reshape(2, HEADS).T,
        "sel": np.repeat(np.eye(HEADS, dtype=np.float32)[:, :, None], P, axis=2),
        "tri": np.stack([s <= t, s > t], axis=1).astype(np.float32),
        "masks": np.stack(masks, axis=1).astype(np.uint32),
        "lb_rows": every(i["hgrn_lb_logits"]),
        "ab_rows": every(np.stack([i["sgu_ln_g_2"][0], i["sgu_ln_b_2"][0], i["sgu_b_2"][0].reshape(-1)])),
        "ws_t": i["sgu_w_2"][0].transpose(2, 0, 1),
        "pool_w": i["pool_w_2"][0].transpose(1, 0, 2),
        "inv_cnt": every(counts.astype(np.float32)),
        "mem": i["mem_2"][0].T.reshape(KD, P, MEM).transpose(1, 0, 2),
    }
    arrays = {n: np.ascontiguousarray(v) for n, v in arrays.items()}
    nc = bacc.Bacc("TRN2", target_bir_lowering=False, num_devices=1)
    aps = {n: nc.dram_tensor(n, v.shape, mybir.dt.from_np(v.dtype), kind="ExternalInput").ap()
           for n, v in arrays.items()}
    aps["out"] = nc.dram_tensor("out", (P, KD, T), mybir.dt.float32, kind="ExternalOutput").ap()
    build(nc, aps)
    r = run_bass_kernel_spmd(nc, [arrays], core_ids=[0])
    y = r.results[0]["out"]
    return np.ascontiguousarray(y.transpose(1, 0, 2).reshape(D, T).T)[None]
```

```python
import concourse.bass as bass
from concourse import mybir
from contextlib import ExitStack

P = 128
T = 512
D = 1024
KD = D // P
FF = 2816
KF = FF // P
HALF_KF = KF // 2
MEM = 256
NT = T // P
HEADS = 4
CHUNK = 128
FULL = 16 * P
DOWN = HALF_KF * P
LEVELS = (64, 32, 16, 8, 4, 2, 1)
ALPHA = (2 * 2) ** 0.25
SLOTS = 2

PHASES = [("up0", KF, 16), ("down0", 16, HALF_KF), ("mixin", 14, 16), ("mixout", 4, 16),
          ("up1", KF, 16), ("down1", 16, HALF_KF),
          ("ab", 6, 16), ("about", 4, 16), ("kv0", 8, 16), ("q0", 4, 16), ("wo0", 4, 16),
          ("up2", KF, 16), ("down2", 16, HALF_KF),
          ("cin", 12, 16), ("cout", 4, 16), ("kv1", 8, 16), ("q1", 4, 16), ("wo1", 4, 16),
          ("up3", KF, 16), ("down3", 16, HALF_KF)]
UNIT0, UNITS, UNIT_COLS, SOURCE0 = {}, {}, [], {}
_full = _down = 0
for _name, _n, _tiles in PHASES:
    UNIT0[_name], UNITS[_name] = len(UNIT_COLS), _n
    UNIT_COLS += [_tiles * P] * _n
    SOURCE0[_name] = _full if _tiles == 16 else _down
    if _tiles == 16:
        _full += _n
    else:
        _down += _n
N_UNITS = len(UNIT_COLS)

VECTORS = [("norm_pre", 24), ("norm_post", 24), ("ln_mix_g_2", 16), ("ln_mix_b_2", 16), ("ln_xa_g_2", 16),
           ("ln_xa_b_2", 16), ("ln_ffn_g_2", 16), ("ln_ffn_b_2", 16), ("conv_w", 16), ("conv_b", 4),
           ("ffn_conv_w_2", 2 * 3 * KF), ("ffn_conv_b_2", 2 * KF), ("c_conv_w_2", 24), ("pool_scale_2", 4),
           ("hgrn_norm", 4), ("mlstm_norm", 4)]
VCOL, _c = {}, 0
for _name, _n in VECTORS:
    VCOL[_name] = _c
    _c += _n
N_VEC = _c

GEN = {n: i for i, n in enumerate(["up0", "mixin", "mixout", "up1", "ab", "about", "q0", "wo0", "up2",
                                   "cin", "cout", "q1", "wo1", "up3"])}
RMS_ENDS = ["down0", "mixout", "down1"]
LN_ENDS = ["about", "wo0", "down2", "cout", "wo1", "down3"]
GAINS = {"about": ("ln_mix", 0), "wo0": ("ln_xa", 0), "down2": ("ln_ffn", 0),
         "cout": ("ln_mix", 1), "wo1": ("ln_xa", 1), "down3": ("ln_ffn", 1)}
NEXT = {"about": "q0", "wo0": "up2", "down2": "cin", "cout": "q1", "wo1": "up3", "down3": None}


def build(nc, a):
    f32, f32r, u32 = mybir.dt.float32, mybir.dt.float32r, mybir.dt.uint32
    ACT, ALU, AX = mybir.ActivationFunctionType, mybir.AluOpType, mybir.AxisListType
    V, S, G = nc.vector, nc.scalar, nc.gpsimd

    ctx = ExitStack()
    with ctx:
        KB = 1024
        BASE = 16512
        slab = ctx.enter_context(nc.sbuf_tensor("slab", [P, 53200], f32))
        made = {}

        def at(name, shape, dt, off):
            made[name] = nc.alloc_sbuf_tensor_at(name, shape, dt, offset=BASE + int(off))
            return made[name]

        x = at("x", [P, KD, T], f32, 0)
        a_hi = at("a_hi", [P, KD, T], f32r, 16 * KB)
        a_lo = at("a_lo", [P, KD, T], f32r, 32 * KB)
        y_ff = at("y_ff", [P, KD, T], f32, 16 * KB)
        raw = at("raw", [P, SLOTS, FULL], f32, 48 * KB)
        w_hi = at("w_hi", [P, SLOTS, FULL], f32r, 64 * KB)
        w_lo = at("w_lo", [P, SLOTS, FULL], f32r, 80 * KB)
        C0 = 96 * KB
        ident = at("ident", [P, P], f32, C0)
        ones = at("ones", [P, P], f32, C0 + 512)
        vec = at("vec", [P, N_VEC], f32, C0 + 1024)
        small = at("small", [P, 16], f32, C0 + 1024 + N_VEC * 4)
        eps6, eps5, one = small[:, 0:1], small[:, 1:2], small[:, 2:3]
        stat = small[:, 4:16]
        half_g = at("half_g", [P, 24], f32, C0 + 1088 + N_VEC * 4)
        tri = at("tri", [P, 2, P], f32, C0 + 2688)
        A0 = C0 + 4 * KB - 256

        def arena(name, shape, dt, kb):
            return at(name, shape, dt, A0 + kb * KB)

        h_hi = arena("h_hi", [P, KF, T], f32r, 0)
        h_lo = arena("h_lo", [P, KF, T], f32r, 44)
        act_out = arena("act_out", [P, 2, T], f32, 88)
        h32 = arena("h32", [P, 2, T], f32, 92)
        conv_out = arena("conv_out", [P, 2, T], f32, 96)
        acc = arena("acc", [P, 2, 2, T], f32, 88)
        sq = arena("sq", [P, 2, T], f32, 96)
        diag = arena("diag", [P, 2, NT, P], f32, 100)
        nt = arena("nt", [P, 2, T], f32, 104)
        scale = arena("scale", [P, T], f32, 104)
        logf = arena("logf", [P, NT, T], f32, 0)
        kdec = arena("kdec", [P, NT, T], f32, 0)
        k_tm = arena("k_tm", [P, NT, T], f32, 8)
        v_tm = arena("v_tm", [P, NT, T], f32, 16)
        mv_tm = arena("mv_tm", [P, NT, T], f32, 24)
        scores = arena("scores", [P, HEADS, T], f32, 24)
        q_fm = arena("q_fm", [P, HEADS, T], f32, 32)
        hgate = arena("hgate", [P, HEADS, T], f32, 40)
        mgate = arena("mgate", [P, HEADS, T], f32, 48)
        mqk = arena("mqk", [P, HEADS, T], f32, 56)
        q_dec = arena("q_dec", [P, HEADS, T], f32, 64)
        Gc = arena("Gc", [P, HEADS, T], f32, 72)
        k_fm = arena("k_fm", [P, HEADS, T], f32, 80)
        lev = [arena("lev0", [P, HEADS, T], f32, 56), arena("lev1", [P, HEADS, T], f32, 88)]
        states = arena("states", [P, 3, HEADS, P], f32, 8)
        g_end = arena("g_end", [P, HEADS * NT], f32, 14)
        masks = arena("masks", [P, 8, P], u32, 96)
        gbias = arena("gbias", [P, 2], f32, 100)
        ct = arena("ct", [P, 2, NT, HEADS], f32, 100.25)
        mcol = arena("mcol", [P, 4, NT], f32, 100.5)
        hcol = arena("hcol", [P, NT, HEADS], f32, 101)
        mtmp = arena("mtmp", [P, 3, T], f32, 102)
        wg_raw = arena("wg_raw", [P, KD, P], f32, 64)
        wg_hi = arena("wg_hi", [P, KD, P], f32r, 68)
        wg_lo = arena("wg_lo", [P, KD, P], f32r, 72)
        rows = arena("rows", [HEADS, 2, 256 + T], f32, 76)
        row_i = arena("row_i", [HEADS, T], f32, 82)
        row_b = arena("row_b", [HEADS, T], f32, 84)
        row_t = arena("row_t", [HEADS, T], f32, 86)
        row_nm = arena("row_nm", [HEADS, T], f32, 88)
        row_em = arena("row_em", [HEADS, T], f32, 90)
        sel = arena("sel", [HEADS, HEADS, P], f32, 8)
        mp = arena("mp", [P, NT * (T + P)], f32, 64)
        lb = arena("lb", [P, 2, T], f32, 32)
        lbt = arena("lbt", [P, 2, T], f32, 36)
        sigm = arena("sigm", [P, 2, 2, MEM], f32, 94)
        y_mix = arena("y_mix", [P, KD, T], f32, 0)
        gv = arena("gv", [P, NT, T], f32, 0)
        ug = arena("ug", [P, 4, T], f32, 8)
        PAD = 16
        pool = [arena(f"pool{n}", [P, 4, PAD + T], f32, 16 + 8.5 * n) for n in range(3)]
        ab_rows = arena("ab_rows", [P, 3, T], f32, 42)
        ws_t = arena("ws_t", [P, 4, P], f32, 48)
        pool_w = arena("pool_w", [P, 4, P], f32, 50)
        inv_cnt = arena("inv_cnt", [P, 4, PAD], f32, 52)
        bn = arena("bn", [P, NT, 6], f32, 52.5)
        mv4 = arena("mv4", [P, NT, 2], f32, 53)
        rs4 = arena("rs4", [P, NT], f32, 53.5)
        cc = arena("cc", [P, 2, T], f32, 0)
        ch = arena("ch", [P, 2, T], f32, 4)
        yc = arena("yc", [P, KD, T], f32, 8)
        mem_raw = arena("mem_raw", [P, KD, MEM], f32, 56)
        mem_hi = arena("mem_hi", [P, KD, MEM], f32r, 64)
        mem_lo = arena("mem_lo", [P, KD, MEM], f32r, 72)
        k_mem = arena("k_mem", [P, KD, MEM], f32, 80)
        v_mem = arena("v_mem", [P, 2, D], f32, 0)
        q_at = arena("q_at", [P, KD, T], f32, 8)
        pe_at = arena("pe_at", [P, 2, NT, MEM], f32, 24)
        p_t = arena("p_t", [P, 2, 2, T], f32, 32)
        o32 = arena("o32", [P, 2, T], f32, 40)
        at_s = arena("at_s", [P, 2, 3, NT], f32, 44)

        bank = ctx.enter_context(nc.psum_tensor("bank", [P, 8, T], f32))

        def sem(name):
            return ctx.enter_context(nc.semaphore(name))

        w_loaded = [sem("w_loaded0"), sem("w_loaded1")]
        w_hi_done = sem("w_hi_done")
        w_split = sem("w_split")
        gemm_done = sem("gemm_done")
        banks_free = sem("banks_free")
        consts = sem("consts")
        consts_v = sem("consts_v")
        x_in = [sem(f"x_in{k}") for k in range(KD)]
        mix_in = [sem(f"mix_in{n}") for n in range(4)]
        mask_in = sem("mask_in")
        ab_in = [sem(f"ab_in{n}") for n in range(4)]
        mem_in = sem("mem_in")
        out_s = sem("out_s")
        a_hi_done = sem("a_hi_done")
        a_even = sem("a_even")
        a_odd = sem("a_odd")
        sq_read = sem("sq_read")
        scale_col = sem("scale_col")
        scale_bc = sem("scale_bc")
        x_pool = sem("x_pool")
        x_act = sem("x_act")
        x_dve = sem("x_dve")
        norm_t = sem("norm_t")
        gate_done = sem("gate_done")
        conv0 = sem("conv0")
        conv_done = sem("conv_done")
        h_hi_done = sem("h_hi_done")
        h_done = sem("h_done")
        y_copied = sem("y_copied")
        sq_done = sem("sq_done")
        acc_done = sem("acc_done")
        stats = sem("stats")
        stat_a = sem("stat_a")
        stat_v = sem("stat_v")
        dve_link = sem("dve_link")
        act_link = sem("act_link")
        SIG = {n: sem(n) for n in """gate_rows_mm c_columns_mm mlstm_m_mm mlstm_scores_mm mlstm_num_mm mlstm_den_mm cum_decay_mm
            keys_transposed rest_decay_mm state_add_mm level_scores_mm hgrn_out_mm attn_scores_mm probs_transposed
            attn_out_mm spatial_mm pool_mm mlstm_weight mlstm_square mlstm_rms gate_w_hi
            lb_sigmoid mconv_start mqk_ready i_row f_row_log mlstm_v exp_neg_m
            mlstm_gate hgrn_input logf_ready cum_decay keys_fm rest_decay q_decay
            chunk_decay level_exp hgrn_square hgrn_rms sgu_v sgu_u sgu_std
            pool_in mem_hi_done c_gate c_conv_start mem_kv attn_q attn_exp
            probs_t c_columns mlstm_arg mlstm_p mlstm_masked mlstm_y lb_diff
            gate_w_lo mconv_done c_row neg_m_row neg_bm_row forget_ready keys_tm
            keys_decayed level_diff level_ready scores_taken states_ready hgrn_y sgu_stats
            sgu_v_ready ab_ya pooled ab_yb mem_lo_done c_product c_y
            attn_max attn_o32 attn_probs rms_gate rms_up mlstm_scaled mlstm_turned mlstm_ms hgrn_scaled
            hgrn_turned hgrn_ms""".split()}

        def gemm_at(unit, tile=1):
            return 2 * unit + tile + 5

        def free_at(unit):
            return unit + 3

        def place(name, k):
            return (k + HEADS) % KD if name == "mixout" else k

        def gen_at(name, k=KD - 1):
            return KD * GEN[name] + place(name, k) + 1

        def low_at(name, k):
            return (a_odd if k % 2 else a_even), KD // 2 * GEN[name] + place(name, k) // 2 + 1

        SCORE_AT = {0: (5, 0), 1: (6, 0), 2: (7, 0), 3: (6, 3 * P)}
        SCALED = {"up0": "x0", "up1": "pre_up1"}
        PRE = ["x0", "pre_mixin", "pre_up1"]
        seq = ["x0", "down0", "pre_mixin", "mixout", "pre_up1", "down1"] + LN_ENDS
        SQ0, ACC0, SR0, ST0, SC0 = {}, {}, {}, {}, {}
        c = [0] * 4
        for n, name in enumerate(seq):
            SQ0[name], ACC0[name], SR0[name], SC0[name], ST0[name] = *c, n
            ln, pre = name in LN_ENDS, name in PRE
            steps = 8 if pre or name.startswith("down") else 4
            c = [c[0] + steps, c[1] + (0 if pre else 1 + 2 * (steps - 1) * ln), c[2] + 8 * pre, c[3] + (2 if ln else 1)]
        YC0 = {n: KD * i for i, n in enumerate(RMS_ENDS)}
        XPOOL0 = {n: KD // 2 * i for i, n in enumerate(RMS_ENDS)}
        NORM0, c = {}, 0
        for n in ["down0", "mixin", "mixout", "down1"] + [NEXT[e] or "out" for e in LN_ENDS]:
            NORM0[n] = c
            c += KD // 2 if n in RMS_ENDS else KD
        STAT_N = {n: i + 1 for i, n in enumerate(m for m in seq if m not in PRE)}
        XACT0 = {n: KD * i for i, n in enumerate(LN_ENDS)}
        XDVE0 = {n: KD // 2 * i for i, n in enumerate(RMS_ENDS)}

        def x_at(name, k):
            return (x_pool, XPOOL0[name] + k // 2 + 1) if k % 2 else (x_dve, XDVE0[name] + k // 2 + 1)

        def buf(k, n=4):
            return nt[:, k % 2, :] if k % n < 2 else sq[:, k % 2, :]
        F0 = {f: KF * f for f in range(4)}

        block = ctx.enter_context(nc.Block())

        @block.sync
        def _(sp):
            def stream(phase):
                u0, n, cols, s0 = UNIT0[phase], UNITS[phase], UNIT_COLS[UNIT0[phase]], SOURCE0[phase]
                src = a["w_full"] if cols == FULL else a["w_down"]
                with sp.Fori(0, n // 2) as i:
                    for s in range(SLOTS):
                        sp.wait_ge(w_split, u0 + 2 * i + (s + 1))
                        sp.dma_start(raw[:, s:s + 1, 0:cols],
                                     src[bass.ds(s0 + 2 * i + s, 1), :, :].rearrange("u p c -> p u c")
                                     ).then_inc(w_loaded[s], 16)

            sp.dma_start(vec[:, :], a["vectors"]).then_inc(consts, 16)
            sp.dma_start(ident[:, :], a["identity"]).then_inc(consts, 16)
            sp.dma_start(tri[:, :, :], a["tri"]).then_inc(consts, 16)
            for phase, _, _ in PHASES:
                stream(phase)
            for k in range(KD):
                sp.wait_ge(x_act, XACT0["down3"] + k + 1)
                sp.dma_start(a["out"][:, k, :], x[:, k, :]).then_inc(out_s, 16)
            sp.wait_ge(out_s, 16 * KD)

        @block.gpsimd
        def _(gp):
            def low_odd(gen, src, wait_x=None):
                for k in (5, 7, 1, 3) if gen == "mixout" else (1, 3, 5, 7):
                    gp.wait_ge(a_hi_done, gen_at(gen, k))
                    if wait_x:
                        gp.wait_ge(*wait_x(k))
                    G.tensor_tensor(a_lo[:, k, :], src(k), a_hi[:, k, :], ALU.subtract).then_inc(a_odd, 1)

            def residual_odd(name, y):
                for k in range(1, KD, 2):
                    gp.wait_ge(norm_t, NORM0[name] + k // 2 + 1)
                    G.tensor_tensor(x[:, k, :], x[:, k, :], y[:, k, :], ALU.add).then_inc(x_pool, 1)

            def x_tile(k):
                return x[:, k, :]

            residual_odd("down0", y_ff)
            low_odd("mixin", buf)
            low_odd("mixout", lambda k: hgate[:, k, :] if k < HEADS else mgate[:, k - HEADS, :])
            residual_odd("mixout", y_mix)
            residual_odd("down1", y_ff)
            low_odd("ab", x_tile)
            low_odd("about", lambda k: ug[:, k, :] if k < 4 else pool[1][:, k - 4, PAD:PAD + T])
            for layer in range(2):
                if layer:
                    low_odd("cout", lambda k: yc[:, k, :])
                for end in (("about", "cout")[layer], f"wo{layer}", f"down{2 + layer}"):
                    if NEXT[end]:
                        low_odd(NEXT[end], x_tile, lambda k: (x_act, XACT0[end] + k + 1))
                    if end[0] in "ac":
                        low_odd(f"wo{layer}", lambda k: o32[:, k % 2, :])

        @block.tensor
        def _(pe):
            mm = nc.tensor.matmul
            PARTS = ((w_hi, a_hi), (w_lo, a_hi), (w_hi, a_lo))

            def first_pair(u0, gen, norm=None):
                def step(kk, s):
                    k = place(gen, kk)
                    if kk == 0:
                        pe.wait_ge(w_split, u0 + s + 3)
                        pe.wait_ge(banks_free, u0 + s + 1)
                    for part, (w, act_in) in enumerate(PARTS):
                        if s == 0 and part == 0:
                            pe.wait_ge(a_hi_done, gen_at(gen, k))
                        if s == 0 and part == 2:
                            pe.wait_ge(*low_at(gen, k))
                        for m in range(2):
                            col = (m * KD + k) * P
                            last = mm(bank[:, 2 * s + m, :], w[:, s, col:col + P], act_in[:, k, :],
                                      start=(kk == 0 and part == 0), stop=(kk == KD - 1 and part == 2))
                            if kk == KD - 1 and part == 2:
                                last.then_inc(gemm_done, 1)
                    if norm and s == 0:
                        square_sum(norm, kk)
                    if norm and s == 1 and kk == KD - 3:
                        broadcast_scales(norm)
                for kk, s in ((0, 0), (1, 0), (0, 1), (1, 1), (2, 0), (2, 1), (3, 0),
                              (4, 0), (5, 0), (6, 0), (7, 0), (3, 1), (4, 1), (5, 1), (6, 1), (7, 1)):
                    step(kk, s)

            def feature_units(phase, wait_gen):
                u0, n = UNIT0[phase], UNITS[phase]
                first_pair(u0, wait_gen, SCALED.get(phase))
                if n > 2:
                    with pe.Fori(1, n // 2) as i:
                        for s in range(SLOTS):
                            pe.wait_ge(w_split, u0 + 2 * i + (s + 3))
                            pe.wait_ge(banks_free, u0 + 2 * i + (s + 1))
                            for m in range(2):
                                for k in range(KD):
                                    for j, (w, act_in) in enumerate(PARTS):
                                        col = (m * KD + k) * P
                                        last = mm(bank[:, 2 * s + m, :], w[:, s, col:col + P], act_in[:, k, :],
                                                  start=(k == 0 and j == 0), stop=(k == KD - 1 and j == 2))
                                last.then_inc(gemm_done, 1)

            def feature_slice(phase, first_unit, n):
                for u in range(first_unit, first_unit + n):
                    s, un = u % 2, UNIT0[phase] + u
                    pe.wait_ge(w_split, un + 3)
                    pe.wait_ge(banks_free, un + 1)
                    for m in range(2):
                        for k in range(KD):
                            for j, (w, act_in) in enumerate(PARTS):
                                col = (m * KD + k) * P
                                last = mm(bank[:, 2 * s + m, :], w[:, s, col:col + P], act_in[:, k, :],
                                          start=(k == 0 and j == 0), stop=(k == KD - 1 and j == 2))
                        last.then_inc(gemm_done, 1)

            def token_pair(u0, gen):
                for s in range(SLOTS):
                    pe.wait_ge(w_split, u0 + s + 3)
                    pe.wait_ge(banks_free, u0 + s + 1)

                def step(k, s, m, t):
                    tok = (2 * m + t) * P
                    for j, (w, act_in) in enumerate(PARTS):
                        last = mm(bank[:, 2 * s + m, t * 256:t * 256 + 256],
                                  act_in[:, k, tok:tok + P], w[:, s, k * 256:k * 256 + 256],
                                  start=(k == 0 and j == 0), stop=(k == KD - 1 and j == 2))
                    return last
                for k in range(KD):
                    pe.wait_ge(*low_at(gen, k))
                    for s in range(SLOTS):
                        for m in range(2):
                            step(k, s, m, 0)
                for s in range(SLOTS):
                    for m in range(2):
                        for k in range(KD):
                            last = step(k, s, m, 1)
                        last.then_inc(gemm_done, 1)

            def token_slice(phase, first_unit, n):
                for u in range(first_unit, first_unit + n):
                    s, un = u % 2, UNIT0[phase] + u
                    pe.wait_ge(w_split, un + 3)
                    pe.wait_ge(banks_free, un + 1)
                    for m in range(2):
                        for t in range(2):
                            tok = (2 * m + t) * P
                            for k in range(KD):
                                for j, (w, act_in) in enumerate(PARTS):
                                    last = mm(bank[:, 2 * s + m, t * 256:t * 256 + 256],
                                              act_in[:, k, tok:tok + P], w[:, s, k * 256:k * 256 + 256],
                                              start=(k == 0 and j == 0), stop=(k == KD - 1 and j == 2))
                        last.then_inc(gemm_done, 1)

            def down_units(phase, f):
                u0 = UNIT0[phase]
                pe.wait_ge(h_done, F0[f] + HALF_KF)
                with pe.Fori(0, KD // 2) as i:
                    for d in range(2):
                        for s in range(SLOTS):
                            pe.wait_ge(w_split, u0 + 4 * i + (2 * d + s + 3))
                            if s == 0:
                                pe.wait_ge(banks_free, u0 + 4 * i + 2 * d)
                            else:
                                pe.wait_ge(h_done, F0[f] + KF)
                            for k in range(HALF_KF):
                                for j, (w, h) in enumerate(((w_hi, h_hi), (w_hi, h_lo), (w_lo, h_hi))):
                                    last = mm(bank[:, 4 + d, :], w[:, s, k * P:(k + 1) * P],
                                              h[:, s * HALF_KF + k, :],
                                              start=(s == 0 and k == 0 and j == 0),
                                              stop=(s == 1 and k == HALF_KF - 1 and j == 2))
                            last.then_inc(gemm_done, 2)

            def norm_sums(name):
                ln, down = name in LN_ENDS, name[0] == "d"
                end = UNIT0[name] + UNITS[name] - 1
                steps = 8 if down else 4
                whiches = (0, 1) if ln else (1,)

                def column(which, n, src, start=False, stop=False):
                    c0 = which * NT + n
                    return mm(bank[:, 6, c0:c0 + 1], src[:, n * P:(n + 1) * P], ones[:, 0:1],
                              start=start, stop=stop, skip_group_check=True)
                if ln:
                    pe.wait_ge(acc_done, ACC0[name] + 1 + 2 * (steps - 1))
                else:
                    pe.wait_ge(banks_free, free_at(end - (2 if down else 1)))
                for which in whiches:
                    for par in range(2):
                        for n in range(NT):
                            column(which, n, acc[:, which, par, :], start=which == whiches[0] and par == 0 and n == 0)
                for which in whiches:
                    if which == 0:
                        pe.wait_ge(banks_free, free_at(end))
                    else:
                        pe.wait_ge(sq_done, SQ0[name] + steps)
                    srcs = [x[:, k, :] if which == 0 else sq[:, 0 if down else k % 2, :]
                            for k in range(7 if down else 6, 8)]
                    for src in srcs:
                        for n in range(NT):
                            last = column(which, n, src, stop=src is srcs[-1])
                last.then_inc(stats, 1)

            def square_sum(name, k):
                pe.wait_ge(sq_done, SQ0[name] + k + 1)
                for n in range(NT):
                    last = mm(bank[:, 7, NT + n:NT + n + 1], sq[:, k % 2, n * P:(n + 1) * P], ones[:, 0:1],
                              start=(k == 0 and n == 0), stop=(k == KD - 1), skip_group_check=True)
                last.then_inc(sq_read, 1)

            def broadcast_scales(name):
                for j in range(2 if name in LN_ENDS else 1):
                    pe.wait_ge(scale_col, SC0[name] + j + 1)
                    mm(bank[:, 7 if name in PRE or j else 6, :], ones[:, :], diag[:, j, :, :],
                       start=True, stop=True).then_inc(scale_bc, 1)

            def mlstm_rows():
                pe.wait_ge(SIG["gate_w_lo"], 1)
                for k in range(KD):
                    for j, (w, act_in) in enumerate(((wg_hi, a_hi), (wg_hi, a_lo), (wg_lo, a_hi))):
                        last = mm(bank[:, 4, :], w[:, k, :], act_in[:, k, :],
                                  start=(k == 0 and j == 0), stop=(k == KD - 1 and j == 2))
                last.then_inc(SIG["gate_rows_mm"], 1)

            def mlstm_columns():
                pe.wait_ge(SIG["c_row"], 1)
                for s in range(NT):
                    nc.tensor.transpose(bank[:, 5, 4 * s:4 * s + 4], row_t[:, s * P:(s + 1) * P],
                                        ident[0:HEADS, 0:HEADS])
                pe.wait_ge(SIG["exp_neg_m"], 1)
                for s in range(NT):
                    last = nc.tensor.transpose(bank[:, 5, 16 + 4 * s:20 + 4 * s], row_em[:, s * P:(s + 1) * P],
                                               ident[0:HEADS, 0:HEADS])
                last.then_inc(SIG["c_columns_mm"], 1)

            def mlstm_scores(h):
                r = 64 * (h % 2)
                q, k = mqk[r:r + 64, h // 2, :], mqk[r:r + 64, 2 + h // 2, :]
                if h == 0:
                    pe.wait_ge(SIG["neg_m_row"], 1)
                    pe.wait_ge(SIG["mqk_ready"], 4)
                    pe.wait_ge(SIG["c_columns"], 1)
                else:
                    pe.wait_ge(SIG["mlstm_scaled"], h)
                mm(bank[:, 4, :], sel[:, h, :], row_nm[:, :], start=True, stop=True).then_inc(SIG["mlstm_m_mm"], 1)
                for s in (0, 1, 3, 2):
                    if s == 2 and h:
                        pe.wait_ge(SIG["mlstm_y"], h)
                    b, c0 = SCORE_AT[s]
                    mm(bank[:, b, c0:c0 + T - s * P], k[:, s * P:(s + 1) * P], q[:, s * P:T],
                       start=True, stop=True).then_inc(SIG["mlstm_scores_mm"], 1)

            def mlstm_values(h):
                pe.wait_ge(SIG["mlstm_masked"], h + 1)
                if h == 0:
                    pe.wait_ge(SIG["mlstm_v"], 2)
                for n in range(NT):
                    for s in range(n + 1):
                        last = mm(bank[:, 5, n * P:(n + 1) * P], mp[:, s * T + n * P:s * T + (n + 1) * P],
                                  mv_tm[:, s, h * P:(h + 1) * P], start=(s == 0), stop=(s == n))
                last.then_inc(SIG["mlstm_num_mm"], 1)
                for n in range(NT):
                    for s in range(n + 1):
                        last = mm(bank[:, 6, n:n + 1], mp[:, s * T + n * P:s * T + (n + 1) * P], ones[:, 0:1],
                                  start=(s == 0), stop=(s == n))
                last.then_inc(SIG["mlstm_den_mm"], 1)

            def mlstm_turn(h):
                pe.wait_ge(SIG["mlstm_scaled"], h + 1)
                for n in range(NT):
                    last = nc.tensor.transpose(bank[:, 7, n * P:(n + 1) * P], mtmp[:, 0, n * P:(n + 1) * P], ident[:, :])
                last.then_inc(SIG["mlstm_turned"], 1)

            def hgrn_core():
                pe.wait_ge(SIG["logf_ready"], 1)
                pe.wait_ge(banks_free, free_at(UNIT0["mixin"] + 13))
                for h in range(HEADS):
                    for n in range(NT):
                        last = mm(bank[:, h, n * P:(n + 1) * P], logf[:, n, h * P:(h + 1) * P], tri[:, 0, :],
                                  start=True, stop=True)
                last.then_inc(SIG["cum_decay_mm"], 1)
                mlstm_turn(HEADS - 1)
                pe.wait_ge(SIG["keys_tm"], 1)
                pe.wait_ge(SIG["mlstm_y"], HEADS)
                for h in range(HEADS):
                    for n in range(NT):
                        last = nc.tensor.transpose(bank[:, 4 + h, n * P:(n + 1) * P],
                                                   k_tm[:, n, h * P:(h + 1) * P], ident[:, :])
                last.then_inc(SIG["keys_transposed"], 1)
                pe.wait_ge(SIG["cum_decay"], 1)
                for n in range(NT):
                    last = mm(bank[:, n, :], tri[:, 1, :], logf[:, n, :], start=True, stop=True)
                last.then_inc(SIG["rest_decay_mm"], 1)
                pe.wait_ge(SIG["keys_decayed"], 1)
                pe.wait_ge(SIG["keys_fm"], 1)
                for n in range(NT - 1):
                    for h in range(HEADS):
                        last = mm(bank[:, 4 + n, h * P:(h + 1) * P], kdec[:, n, h * P:(h + 1) * P],
                                  v_tm[:, n, h * P:(h + 1) * P], start=True, stop=True)
                last.then_inc(SIG["state_add_mm"], 1)
                pe.wait_ge(SIG["q_decay"], 1)
                for l in range(len(LEVELS) + 1):
                    if l:
                        pe.wait_ge(SIG["level_ready"], l)
                    if l >= 2:
                        pe.wait_ge(SIG["scores_taken"], l - 2 + 1)
                    if l == 1:
                        pe.wait_ge(SIG["states_ready"], 1)
                    for h in range(HEADS):
                        for n in range(NT):
                            c0 = n * P
                            lhs = k_fm if l == 0 else lev[(l - 1) % 2]
                            rhs = q_fm if l == 0 else lev[(l - 1) % 2]
                            last = mm(bank[:, 4 * (l % 2) + h, c0:c0 + P], lhs[:, h, c0:c0 + P],
                                      rhs[:, h, c0:c0 + P], start=True, stop=True)
                    last.then_inc(SIG["level_scores_mm"], 1)
                pe.wait_ge(SIG["scores_taken"], len(LEVELS) + 1)
                for n in range(NT):
                    for h in range(HEADS):
                        c0 = n * P
                        last = mm(bank[:, n, h * P:(h + 1) * P], scores[:, h, c0:c0 + P],
                                  v_tm[:, n, h * P:(h + 1) * P], start=True, stop=(n == 0))
                        if n:
                            last = mm(bank[:, n, h * P:(h + 1) * P], q_dec[:, h, c0:c0 + P],
                                      states[:, n - 1, h, :], start=False, stop=True)
                    last.then_inc(SIG["hgrn_out_mm"], 1)
                for n in range(NT):
                    pe.wait_ge(SIG["hgrn_scaled"], n + 1)
                    for h in range(HEADS):
                        last = nc.tensor.transpose(bank[:, 4 + h, n * P:(n + 1) * P],
                                                   lev[0][:, n, h * P:(h + 1) * P], ident[:, :])
                last.then_inc(SIG["hgrn_turned"], 1)

            def memory_unit(phase, u):
                s, un = u % 2, UNIT0[phase] + u
                layer = int(phase[-1])
                if u == 0:
                    pe.wait_ge(SIG["mem_lo_done"], layer + 1)
                pe.wait_ge(w_split, un + 3)
                pe.wait_ge(banks_free, un + 1)
                for m in range(2):
                    for k in range(KD):
                        for j, (w, src) in enumerate(((w_hi, mem_hi), (w_hi, mem_lo), (w_lo, mem_hi))):
                            if u < 4:
                                col = (m * KD + k) * P
                                ops = (w[:, s, col:col + P], src[:, k, :])
                            else:
                                ops = (src[:, k, m * P:(m + 1) * P], w[:, s, k * 256:k * 256 + 256])
                            last = mm(bank[:, 2 * s + m, 0:MEM], *ops,
                                      start=(k == 0 and j == 0), stop=(k == KD - 1 and j == 2))
                    last.then_inc(gemm_done, 1)

            def attention(layer):
                pe.wait_ge(banks_free, free_at(UNIT0[f"q{layer}"] + 3))
                for h in range(HEADS + 1):
                    if h < HEADS:
                        b = 2 * (h % 2)
                        if h >= 2:
                            pe.wait_ge(SIG["attn_probs"], 4 * layer + h - 2 + 1)
                        for t in range(NT):
                            for d in range(2):
                                last = mm(bank[:, b + t // 2, (t % 2) * MEM:(t % 2) * MEM + MEM],
                                          q_at[:, 2 * h + d, t * P:(t + 1) * P], k_mem[:, 2 * h + d, :],
                                          start=(d == 0), stop=(d == 1))
                        last.then_inc(SIG["attn_scores_mm"], 1)
                    if h:
                        g = h - 1
                        pe.wait_ge(SIG["attn_probs"], 4 * layer + g + 1)
                        if g:
                            pe.wait_ge(SIG["probs_t"], 4 * layer + g)
                        for m in range(2):
                            for t in range(NT):
                                last = nc.tensor.transpose(bank[:, 4 + m, t * P:(t + 1) * P],
                                                           pe_at[:, g % 2, t, m * P:(m + 1) * P], ident[:, :])
                        last.then_inc(SIG["probs_transposed"], 1)
                        pe.wait_ge(SIG["probs_t"], 4 * layer + g + 1)
                        if g:
                            pe.wait_ge(SIG["attn_o32"], 4 * layer + g)
                        for d in range(2):
                            for m in range(2):
                                last = mm(bank[:, 6 + d, :], v_mem[:, m, (2 * g + d) * P:(2 * g + d + 1) * P],
                                          p_t[:, g % 2, m, :], start=(m == 0), stop=(m == 1))
                        last.then_inc(SIG["attn_out_mm"], 1)

            def ab_core():
                pe.wait_ge(SIG["sgu_v_ready"], 1)
                for g in range(4):
                    for n in range(NT):
                        last = mm(bank[:, 4 + g, n * P:(n + 1) * P], gv[:, n, g * P:(g + 1) * P],
                                  ws_t[:, g, :], start=True, stop=True)
                last.then_inc(SIG["spatial_mm"], 1)
                pe.wait_ge(banks_free, free_at(UNIT0["ab"] + 5))
                for g in range(4):
                    pe.wait_ge(SIG["pooled"], g + 1)
                    mm(bank[:, g, :], pool_w[:, g, :], pool[2][:, g, PAD:PAD + T],
                       start=True, stop=True).then_inc(SIG["pool_mm"], 1)

            pe.wait_ge(consts_v, 1)
            pe.wait_ge(consts, 48)
            feature_units("up0", "up0")
            down_units("down0", 0)
            norm_sums("down0")
            broadcast_scales("down0")
            for k in range(KD):
                square_sum("pre_mixin", k)
            broadcast_scales("pre_mixin")
            first_pair(UNIT0["mixin"], "mixin")
            mlstm_rows()
            token_slice("mixin", 2, 2)
            feature_slice("mixin", 4, 2)
            mlstm_columns()
            for h in range(HEADS):
                unit = token_slice if h < 2 else feature_slice
                unit("mixin", 6 + 2 * h, 1)
                if h:
                    mlstm_turn(h - 1)
                mlstm_scores(h)
                unit("mixin", 7 + 2 * h, 1)
                mlstm_values(h)
            hgrn_core()
            feature_units("mixout", "mixout")
            norm_sums("mixout")
            broadcast_scales("mixout")
            feature_units("up1", "up1")
            down_units("down1", 1)
            norm_sums("down1")
            broadcast_scales("down1")
            token_pair(UNIT0["ab"], "ab")
            feature_slice("ab", 2, 4)
            ab_core()
            pe.wait_ge(SIG["ab_yb"], 4)
            feature_units("about", "about")
            for layer in range(2):
                memory_unit(f"kv{layer}", 0)
                norm_sums(("about", "cout")[layer])
                memory_unit(f"kv{layer}", 1)
                broadcast_scales(("about", "cout")[layer])
                for u in range(2, 8):
                    memory_unit(f"kv{layer}", u)
                feature_units(f"q{layer}", f"q{layer}")
                attention(layer)
                feature_units(f"wo{layer}", f"wo{layer}")
                norm_sums(f"wo{layer}")
                broadcast_scales(f"wo{layer}")
                feature_units(f"up{2 + layer}", f"up{2 + layer}")
                down_units(f"down{2 + layer}", 2 + layer)
                norm_sums(f"down{2 + layer}")
                broadcast_scales(f"down{2 + layer}")
                if layer == 0:
                    feature_units("cin", "cin")
                    feature_units("cout", "cout")

        @block.scalar
        def _(act):
            links = [0]

            def link(ins):
                links[0] += 1
                ins.then_inc(act_link, 1)
                act.wait_ge(act_link, links[0])

            def split(unit, s, cols):
                half = unit // 2 if isinstance(unit, int) else None
                act.wait_ge(w_loaded[s], 16 * (half + 1))
                act.wait_ge(gemm_done, 2 * unit + 2)
                S.activation(w_hi[:, s, 0:cols], raw[:, s, 0:cols], ACT.Copy).then_inc(w_hi_done, 1)

            def split_in(pair0, i, s, cols):
                act.wait_ge(w_loaded[s], 16 * (pair0 + i) + 16)
                act.wait_ge(gemm_done, 4 * (pair0 + i) + (2 * s + 2))
                S.activation(w_hi[:, s, 0:cols], raw[:, s, 0:cols], ACT.Copy).then_inc(w_hi_done, 1)

            split_early = set()

            def split_ahead(phase):
                split_next(UNIT0[phase])
                split_early.add(UNIT0[phase] + 1)

            def split_next(unit):
                if unit + 1 < N_UNITS and unit + 1 not in split_early:
                    split(unit + 1, (unit + 1) % 2, UNIT_COLS[unit + 1])

            def pairs(phase, post, per_pair=2):
                u0, n, cols = UNIT0[phase], UNITS[phase], UNIT_COLS[UNIT0[phase]]
                trips = n // per_pair
                split_next(u0)
                if trips > 1:
                    with act.Fori(0, trips - 1) as i:
                        for j in range(per_pair):
                            split_in((u0 + j + 2) // 2, i * (per_pair // 2), j % 2, cols)
                            post(i, j)
                for j in range(per_pair):
                    if j < per_pair - 1:
                        split_next(u0 + n - per_pair + j + 1)
                    post(trips - 1, j)

            def up(f):
                conv = f >= 2
                u0, n0 = UNIT0[f"up{f}"], F0[f]
                vc = VCOL["ffn_conv_w_2"] + 3 * KF * (f - 2)
                vb = VCOL["ffn_conv_b_2"] + KF * (f - 2)

                def post(i, s):
                    if conv:
                        act.wait_ge(gemm_done, 2 * u0 + 4 * i + (2 * s + 5))
                        n = 2 * i + s
                        S.activation(conv_out[:, s, :], bank[:, 2 * s, :], ACT.Identity,
                                     scale=vec[:, bass.ds(vc + 2 * KF + n, 1)],
                                     bias=vec[:, bass.ds(vb + n, 1)]).then_inc(conv0, 1)
                        act.wait_ge(conv_done, 2 * (n0 - F0[2]) + 4 * i + (2 * s + 2))
                        S.activation(act_out[:, s, :], conv_out[:, s, :],
                                     ACT.Gelu_apprx_tanh).then_inc(gate_done, 1)
                    else:
                        act.wait_ge(SIG["rms_gate"], n0 + 2 * i + (s + 1))
                        S.activation(act_out[:, s, :], conv_out[:, s, :], ACT.Silu).then_inc(gate_done, 1)
                    if conv:
                        act.wait_ge(banks_free, u0 + 2 * i + (s + 3))
                    else:
                        act.wait_ge(SIG["rms_up"], 2 * n0 + 4 * i + (2 * s + 2))
                    S.activation(h_hi[:, bass.ds(2 * i + s, 1), :], h32[:, s:s + 1, :],
                                 ACT.Copy).then_inc(h_hi_done, 1)
                pairs(f"up{f}", post)

            def end_rms(phase, y, gains):
                u0, down = UNIT0[phase], phase[0] == "d"

                def post(i, j):
                    if down and j % 2 == 0:
                        return
                    n = 2 * i + (j // 2 if down else j)
                    act.wait_ge(gemm_done, 2 * u0 + (8 if down else 4) * i + (2 * j + 6))
                    if down:
                        src, dst, sqd = bank[:, 4 + j // 2:5 + j // 2, :], y[:, bass.ds(n, 1), :], sq[:, 0:1, :]
                    else:
                        src, dst, sqd = bank[:, 2 * j:2 * j + 2, :], y[:, bass.ds(2 * n, 2), :], sq[:, :, :]
                    act.wait_ge(banks_free, u0 + (4 * i + 2 * (j // 2) if down else 2 * i + j) + 2)
                    S.activation(sqd, src, ACT.Square).then_inc(sq_done, 1)
                    for m in range(1 if down else 2):
                        S.activation(dst[:, m:m + 1, :], src[:, m:m + 1, :], ACT.Copy,
                                     scale=gains[:, bass.ds(n if down else 2 * n + m, 1)]).then_inc(y_copied, 1)
                pairs(phase, post, 4 if down else 2)

            def end_ln(phase):
                u0, down = UNIT0[phase], phase[0] == "d"

                def post(i, j):
                    if down and j % 2 == 0:
                        return
                    n = 2 * i + (j // 2 if down else j)
                    act.wait_ge(banks_free, u0 + (4 if down else 2) * i + (j + 3))
                    act.wait_ge(acc_done, ACC0[phase] + 2 * n + 1)
                    if down:
                        S.activation(sq[:, 0:1, :], x[:, bass.ds(n, 1), :], ACT.Square).then_inc(sq_done, 1)
                    else:
                        S.activation(sq[:, :, :], x[:, bass.ds(2 * n, 2), :], ACT.Square).then_inc(sq_done, 1)
                pairs(phase, post, 4 if down else 2)

            def root(name):
                if name in PRE:
                    act.wait_ge(sq_read, SR0[name] + KD)
                else:
                    act.wait_ge(stats, STAT_N[name])
                b = 7 if name in PRE else 6
                S.activation(stat[:, 8:12], bank[:, b, NT:2 * NT], ACT.Sqrt, scale=1.0 / D, bias=eps6
                             ).then_inc(stat_a, 1)

            def ln_root(name):
                act.wait_ge(stat_v, LN_ENDS.index(name) + 1)
                S.activation(stat[:, 8:12], stat[:, 8:12], ACT.Sqrt, bias=eps5).then_inc(stat_a, 1)

            def ln_tile(name, k):
                which, layer = GAINS[name]
                g0, b0 = VCOL[which + "_g_2"] + 8 * layer + k, VCOL[which + "_b_2"] + 8 * layer + k
                nxt = NEXT[name]
                act.wait_ge(norm_t, NORM0[nxt or "out"] + k + 1)
                if nxt:
                    S.activation(a_hi[:, k, :], buf(k), ACT.Identity, scale=vec[:, g0:g0 + 1],
                                 bias=vec[:, b0:b0 + 1]).then_inc(a_hi_done, 1)
                S.activation(x[:, k, :], buf(k), ACT.Identity, scale=vec[:, g0:g0 + 1],
                             bias=vec[:, b0:b0 + 1]).then_inc(x_act, 1)

            def squares_of_x(name, ready):
                for k in range(KD):
                    act.wait_ge(*ready(k))
                    if k >= 2:
                        act.wait_ge(sq_read, SR0[name] + k - 1)
                    S.activation(sq[:, k % 2, :], x[:, k, :], ACT.Square).then_inc(sq_done, 1)

            def scaled_input(gen, name, ready, g0):
                for k in range(KD):
                    if k == 2 and gen == "up0":
                        split_ahead(gen)
                    act.wait_ge(*ready(k))
                    S.activation(a_hi[:, k, :], x[:, k, :], ACT.Copy, scale=vec[:, g0 + k:g0 + k + 1]
                                 ).then_inc(a_hi_done, 1)
                    if k >= 2:
                        act.wait_ge(sq_read, SR0[name] + k - 1)
                    S.activation(sq[:, k % 2, :], x[:, k, :], ACT.Square).then_inc(sq_done, 1)

            def normalised(gen):
                for k in range(KD):
                    act.wait_ge(norm_t, NORM0[gen] + k + 1)
                    S.activation(a_hi[:, k, :], buf(k), ACT.Copy).then_inc(a_hi_done, 1)

            def mlstm_weights(h):
                for s in range(NT):
                    act.wait_ge(SIG["mlstm_arg"], 4 * h + s + 1)
                    S.activation(mp[:, s * T + s * P:(s + 1) * T], mp[:, s * T + s * P:(s + 1) * T],
                                 ACT.Exp).then_inc(SIG["mlstm_weight"], 1)

            def mlstm_squares(h):
                act.wait_ge(SIG["mlstm_num_mm"], h + 1)
                for n in range(NT):
                    S.activation(mtmp[:, 1, n * P:(n + 1) * P], bank[:, 5, n * P:(n + 1) * P], ACT.Square,
                                 accum_out=mcol[:, 0, n:n + 1]).then_inc(SIG["mlstm_square"], 1)

            def mlstm_root(h):
                act.wait_ge(SIG["mlstm_ms"], h + 1)
                S.activation(mcol[:, 1, :], mcol[:, 1, :], ACT.Sqrt, scale=1.0 / P,
                             bias=eps6).then_inc(SIG["mlstm_rms"], 1)

            act.wait_ge(consts_v, 1)
            for k in range(KD):
                act.dma_start(x[:, k, :], a["x"][:, k, :]).then_inc(x_in[k], 16)
            split(0, 0, FULL)
            scaled_input("up0", "x0", lambda k: (x_in[k], 16), VCOL["norm_pre"])
            root("x0")
            up(0)
            end_rms("down0", y_ff, half_g[:, 0:8])
            split_ahead("mixin")
            root("down0")
            for n, (dst, src) in enumerate([(wg_raw[:, :, :], a["w_gates"]), (lbt[:, :, :], a["lb_rows"]),
                                            (sel[:, :, :], a["sel"])]):
                act.dma_start(dst, src).then_inc(mix_in[n], 16)
            squares_of_x("pre_mixin", lambda k: x_at("down0", k))
            root("pre_mixin")
            normalised("mixin")

            act.wait_ge(*low_at("mixin", KD - 2))
            act.wait_ge(*low_at("mixin", KD - 1))
            act.dma_start(gbias[0:HEADS, :], a["gate_bias"]).then_inc(mix_in[3], 16)
            mi = UNIT0["mixin"]
            act.wait_ge(mix_in[0], 16)
            S.activation(wg_hi[:, :, :], wg_raw[:, :, :], ACT.Copy).then_inc(SIG["gate_w_hi"], 1)
            act.wait_ge(SIG["lb_diff"], 1)
            S.activation(lb[:, :, :], lb[:, :, :], ACT.Sigmoid).then_inc(SIG["lb_sigmoid"], 1)
            for u in range(2):
                split_next(mi + u)
                for m in range(2):
                    t = 2 * u + m
                    act.wait_ge(gemm_done, gemm_at(mi + u, m))
                    S.activation(mqk[:, t, :], bank[:, 2 * u + m, :], ACT.Identity,
                                 scale=vec[:, VCOL["conv_w"] + 12 + t:VCOL["conv_w"] + 13 + t],
                                 bias=vec[:, VCOL["conv_b"] + t:VCOL["conv_b"] + t + 1]).then_inc(SIG["mconv_start"], 1)
            for t in range(4):
                act.wait_ge(SIG["mconv_done"], t + 1)
                S.activation(mqk[:, t, :], mqk[:, t, :], ACT.Silu).then_inc(SIG["mqk_ready"], 1)
            act.wait_ge(mix_in[3], 16)
            act.wait_ge(SIG["gate_rows_mm"], 1)
            S.activation(row_i[:, :], bank[0:HEADS, 4, :], ACT.Identity, bias=gbias[0:HEADS, 0:1]).then_inc(SIG["i_row"], 1)
            link(S.activation(row_b[:, :], bank[32:32 + HEADS, 4, :], ACT.Identity, bias=gbias[0:HEADS, 1:2]))
            link(S.activation(row_t[:, :], row_b[:, :], ACT.Abs))
            link(S.activation(row_t[:, :], row_t[:, :], ACT.Exp, scale=-1.0))
            S.activation(row_t[:, :], row_t[:, :], ACT.Ln, bias=one[0:HEADS, :]).then_inc(SIG["f_row_log"], 1)
            for u in (2, 3):
                split_next(mi + u)
                act.wait_ge(gemm_done, gemm_at(mi + u))
                S.activation(mv_tm[:, :, (u - 2) * 256:(u - 1) * 256],
                             bank[:, 2 * (u % 2):2 * (u % 2) + 2, :].rearrange("p b (t c) -> p (b t) c", t=2),
                             ACT.Copy).then_inc(SIG["mlstm_v"], 1)
            act.wait_ge(SIG["neg_bm_row"], 1)
            S.activation(row_em[:, :], row_em[:, :], ACT.Exp).then_inc(SIG["exp_neg_m"], 1)
            for u in (4, 5):
                split_next(mi + u)
                act.wait_ge(gemm_done, gemm_at(mi + u))
                S.activation(mgate[:, 2 * (u - 4):2 * (u - 4) + 2, :], bank[:, 2 * (u % 2):2 * (u % 2) + 2, :],
                             ACT.Sigmoid).then_inc(SIG["mlstm_gate"], 1)
            for h in range(HEADS):
                for j in range(2):
                    u = 6 + 2 * h + j
                    b = 2 * (u % 2)
                    split_next(mi + u)
                    act.wait_ge(gemm_done, gemm_at(mi + u))
                    four = bank[:, b:b + 2, :].rearrange("p b (t c) -> p (b t) c", t=2)
                    if h == 0:
                        if j == 1:
                            act.wait_ge(SIG["forget_ready"], 1)
                        S.activation(sigm[:, :, :, :].rearrange("p a t c -> p (a t) c"), four,
                                     ACT.Sigmoid).then_inc(SIG["hgrn_input"], 1)
                    elif h == 1:
                        S.activation(v_tm[:, :, j * 256:(j + 1) * 256], four, ACT.Copy).then_inc(SIG["hgrn_input"], 1)
                    else:
                        dst = q_fm if h == 2 else hgate
                        S.activation(dst[:, 2 * j:2 * j + 2, :], bank[:, b:b + 2, :], ACT.Silu).then_inc(SIG["hgrn_input"], 1)
                    if j == 0:
                        mlstm_weights(h)
                    else:
                        mlstm_squares(h)
                        mlstm_root(h)
            act.dma_start(masks[:, :, :], a["masks"]).then_inc(mask_in, 16)
            act.wait_ge(SIG["keys_tm"], 1)
            S.activation(logf[:, :, :], logf[:, :, :], ACT.Ln).then_inc(SIG["logf_ready"], 1)
            act.wait_ge(SIG["cum_decay_mm"], 1)
            S.activation(Gc[:, :, :], bank[:, 0:4, :], ACT.Copy).then_inc(SIG["cum_decay"], 1)
            act.wait_ge(SIG["keys_transposed"], 1)
            S.activation(k_fm[:, :, :], bank[:, 4:8, :], ACT.Copy).then_inc(SIG["keys_fm"], 1)
            act.wait_ge(SIG["rest_decay_mm"], 1)
            S.activation(lev[0][:, :, :], bank[:, 0:4, :], ACT.Exp).then_inc(SIG["rest_decay"], 1)
            S.activation(q_dec[:, :, :], Gc[:, :, :], ACT.Exp).then_inc(SIG["q_decay"], 1)
            act.wait_ge(SIG["keys_decayed"], 1)
            S.activation(g_end[:, :], Gc[:, :, :].rearrange("p h (n c) -> p (h n) c", c=CHUNK)[:, :, CHUNK - 1],
                         ACT.Exp).then_inc(SIG["chunk_decay"], 1)
            split_ahead("mixout")
            act.wait_ge(SIG["mlstm_y"], HEADS)
            for k in range(HEADS, KD):
                S.activation(a_hi[:, k, :], mgate[:, k - HEADS, :], ACT.Copy).then_inc(a_hi_done, 1)
            for l in range(len(LEVELS)):
                act.wait_ge(SIG["level_diff"], l + 1)
                S.activation(lev[l % 2][:, :, :], lev[l % 2][:, :, :], ACT.Exp).then_inc(SIG["level_exp"], 1)
            for h in range(HEADS):
                act.wait_ge(SIG["hgrn_out_mm"], h + 1)
                S.activation(lev[1][:, h, :], bank[:, h, :], ACT.Square).then_inc(SIG["hgrn_square"], 1)
            act.wait_ge(SIG["hgrn_ms"], 1)
            S.activation(hcol[:, :, :], hcol[:, :, :], ACT.Sqrt, scale=1.0 / P, bias=eps6).then_inc(SIG["hgrn_rms"], 1)
            for k in range(HEADS):
                act.wait_ge(SIG["hgrn_y"], k + 1)
                S.activation(a_hi[:, k, :], hgate[:, k, :], ACT.Copy).then_inc(a_hi_done, 1)
            end_rms("mixout", y_mix, vec[:, VCOL["norm_post"] + 8:VCOL["norm_post"] + 16])
            split_ahead("up1")
            root("mixout")
            scaled_input("up1", "pre_up1", lambda k: x_at("mixout", k), VCOL["norm_pre"] + 16)
            root("pre_up1")
            up(1)
            end_rms("down1", y_ff, half_g[:, 16:24])
            split_ahead("ab")
            root("down1")
            for n, (dst, src) in enumerate([(ab_rows[:, :, :], a["ab_rows"]), (ws_t[:, :, :], a["ws_t"]),
                                            (pool_w[:, :, :], a["pool_w"]), (inv_cnt[:, :, :], a["inv_cnt"])]):
                act.dma_start(dst, src).then_inc(ab_in[n], 16)
            act.dma_start(mem_raw[:, :, :], a["mem"]).then_inc(mem_in, 16)
            for k in range(KD):
                act.wait_ge(*x_at("down1", k))
                S.activation(a_hi[:, k, :], x[:, k, :], ACT.Copy).then_inc(a_hi_done, 1)

            ab = UNIT0["ab"]
            for u in range(2):
                split_next(ab + u)
                act.wait_ge(gemm_done, gemm_at(ab + u))
                S.activation(gv[:, :, u * 256:(u + 1) * 256],
                             bank[:, 2 * u:2 * u + 2, :].rearrange("p b (t c) -> p (b t) c", t=2),
                             ACT.Gelu_apprx_tanh).then_inc(SIG["sgu_v"], 1)
            for u in (2, 3):
                split_next(ab + u)
                act.wait_ge(gemm_done, gemm_at(ab + u))
                S.activation(ug[:, 2 * (u - 2):2 * (u - 2) + 2, :], bank[:, 2 * (u % 2):2 * (u % 2) + 2, :],
                             ACT.Gelu_apprx_tanh).then_inc(SIG["sgu_u"], 1)
            act.wait_ge(SIG["sgu_stats"], 4)
            S.activation(rs4[:, :], mv4[:, :, 1], ACT.Sqrt, bias=eps5).then_inc(SIG["sgu_std"], 1)
            for u in (4, 5):
                split_next(ab + u)
                act.wait_ge(gemm_done, gemm_at(ab + u))
                S.activation(pool[0][:, 2 * (u - 4):2 * (u - 4) + 2, PAD:PAD + T],
                             bank[:, 2 * (u % 2):2 * (u % 2) + 2, :], ACT.Copy).then_inc(SIG["pool_in"], 1)
            split_ahead("about")
            act.wait_ge(mem_in, 16)
            S.activation(mem_hi[:, :, :], mem_raw[:, :, :], ACT.Copy).then_inc(SIG["mem_hi_done"], 1)
            for k in range(KD):
                act.wait_ge(*((SIG["ab_ya"], k + 1) if k < 4 else (SIG["ab_yb"], k - 3)))
                src = ug[:, k, :] if k < 4 else pool[1][:, k - 4, PAD:PAD + T]
                S.activation(a_hi[:, k, :], src, ACT.Copy).then_inc(a_hi_done, 1)
            for layer in range(2):
                if layer == 1:
                    ci = UNIT0["cin"]
                    cw = VCOL["c_conv_w_2"]
                    act.dma_start(mem_raw[:, :, :], a["mem"]).then_inc(mem_in, 16)
                    act.wait_ge(mem_in, 32)
                    S.activation(mem_hi[:, :, :], mem_raw[:, :, :], ACT.Copy).then_inc(SIG["mem_hi_done"], 1)
                    for u in range(12):
                        split_next(ci + u)
                        if u < 8:
                            b = 2 * (u % 2)
                            act.wait_ge(gemm_done, gemm_at(ci + u, 0))
                            if u >= 2:
                                act.wait_ge(SIG["c_product"], u - 2 + 1)
                            S.activation(cc[:, u % 2, :], bank[:, b, :], ACT.Copy).then_inc(SIG["c_gate"], 1)
                            act.wait_ge(SIG["c_product"], u + 1)
                            S.activation(yc[:, u, :], ch[:, u % 2, :], ACT.Copy,
                                         scale=vec[:, cw + 16 + u:cw + 17 + u]).then_inc(SIG["c_conv_start"], 1)
                    split_ahead("cout")
                    for k in range(KD):
                        act.wait_ge(SIG["c_y"], 4)
                        S.activation(a_hi[:, k, :], yc[:, k, :], ACT.Copy).then_inc(a_hi_done, 1)
                end = ("about", "cout")[layer]
                end_ln(end)
                kv = UNIT0[f"kv{layer}"]
                split_ahead(f"kv{layer}")
                ln_root(end)
                def mem_out(u):
                    act.wait_ge(gemm_done, gemm_at(kv + u))
                    dst = k_mem[:, 2 * u:2 * u + 2, :] if u < 4 else v_mem[:, :, (u - 4) * 256:(u - 3) * 256]
                    S.activation(dst, bank[:, 2 * (u % 2):2 * (u % 2) + 2, 0:MEM], ACT.Copy).then_inc(SIG["mem_kv"], 1)
                for k in range(KD):
                    if k:
                        split_next(kv + k)
                        mem_out(k - 1)
                    ln_tile(end, k)
                mem_out(KD - 1)
                q0 = UNIT0[f"q{layer}"]
                for u in range(4):
                    split_next(q0 + u)
                    act.wait_ge(gemm_done, gemm_at(q0 + u))
                    S.activation(q_at[:, 2 * u:2 * u + 2, :], bank[:, 2 * (u % 2):2 * (u % 2) + 2, :],
                                 ACT.Copy).then_inc(SIG["attn_q"], 1)
                split_ahead(f"wo{layer}")
                scale = 256.0 ** -0.5
                for h in range(HEADS + 1):
                    if h < HEADS:
                        act.wait_ge(SIG["attn_max"], 4 * layer + h + 1)
                        for t in range(NT):
                            S.activation(pe_at[:, h % 2, t, :],
                                         bank[:, 2 * (h % 2) + t // 2, (t % 2) * MEM:(t % 2) * MEM + MEM],
                                         ACT.Exp, scale=scale, bias=at_s[:, h % 2, 1, t:t + 1],
                                         accum_out=at_s[:, h % 2, 2, t:t + 1]).then_inc(SIG["attn_exp"], 1)
                    if h:
                        g = h - 1
                        act.wait_ge(SIG["probs_transposed"], 4 * layer + g + 1)
                        S.activation(p_t[:, g % 2, :, :], bank[:, 4:6, :], ACT.Copy).then_inc(SIG["probs_t"], 1)
                        act.wait_ge(SIG["attn_o32"], 4 * layer + g + 1)
                        for d in range(2):
                            S.activation(a_hi[:, 2 * g + d, :], o32[:, d, :], ACT.Copy).then_inc(a_hi_done, 1)
                end = f"wo{layer}"
                end_ln(end)
                if NEXT[end]:
                    split_ahead(NEXT[end])
                ln_root(end)
                for k in range(KD):
                    ln_tile(end, k)
                up(2 + layer)
                end = f"down{2 + layer}"
                end_ln(end)
                if NEXT[end]:
                    split_ahead(NEXT[end])
                ln_root(end)
                for k in range(KD):
                    ln_tile(end, k)

        @block.vector
        def _(dve):
            links = [0]

            def link(ins):
                links[0] += 1
                ins.then_inc(dve_link, 1)
                dve.wait_ge(dve_link, links[0])

            def split(unit, s, cols):
                dve.wait_ge(w_hi_done, unit + 1)
                V.tensor_tensor(w_lo[:, s, 0:cols], raw[:, s, 0:cols], w_hi[:, s, 0:cols],
                                ALU.subtract).then_inc(w_split, 1)

            split_early = set()

            def split_ahead(phase):
                split_next(UNIT0[phase])
                split_early.add(UNIT0[phase] + 1)

            def split_next(unit):
                if unit + 1 < N_UNITS and unit + 1 not in split_early:
                    split(unit + 1, (unit + 1) % 2, UNIT_COLS[unit + 1])

            def pairs(phase, post, per_pair=2):
                u0, n, cols = UNIT0[phase], UNITS[phase], UNIT_COLS[UNIT0[phase]]
                trips = n // per_pair
                split_next(u0)
                if trips > 1:
                    with dve.Fori(0, trips - 1) as i:
                        for j in range(per_pair):
                            split(u0 + per_pair * i + (j + 2), j % 2, cols)
                            post(i, j)
                for j in range(per_pair):
                    if j < per_pair - 1:
                        split_next(u0 + n - per_pair + j + 1)
                    post(trips - 1, j)

            def up(f):
                conv = f >= 2
                u0, n0 = UNIT0[f"up{f}"], F0[f]
                vc = VCOL["ffn_conv_w_2"] + 3 * KF * (f - 2)

                def post(i, s):
                    n = 2 * i + s
                    if conv:
                        c0 = 2 * (n0 - F0[2]) + 4 * i + 2 * s
                        dve.wait_ge(conv0, (n0 - F0[2]) + n + 1)
                        for tap in (1, 2):
                            V.scalar_tensor_tensor(conv_out[:, s, tap:T], bank[:, 2 * s, 0:T - tap],
                                                   vec[:, bass.ds(vc + (2 - tap) * KF + n, 1)],
                                                   conv_out[:, s, tap:T], ALU.mult, ALU.add).then_inc(conv_done, 1)
                            if tap == 1:
                                dve.wait_ge(conv_done, c0 + 1)
                    if conv:
                        dve.wait_ge(gate_done, n0 + n + 1)
                        dve.wait_ge(gemm_done, 2 * u0 + 4 * i + (2 * s + 6))
                        V.tensor_tensor(h32[:, s, :], act_out[:, s, :], bank[:, 2 * s + 1, :],
                                        ALU.mult).then_inc(banks_free, 1)
                    else:
                        dve.wait_ge(gemm_done, 2 * u0 + 4 * i + (2 * s + 5))
                        V.tensor_tensor(conv_out[:, s, :], bank[:, 2 * s, :], scale[:, :],
                                        ALU.mult).then_inc(SIG["rms_gate"], 1)
                        dve.wait_ge(gemm_done, 2 * u0 + 4 * i + (2 * s + 6))
                        V.tensor_tensor(h32[:, s, :], bank[:, 2 * s + 1, :], scale[:, :],
                                        ALU.mult).then_inc(SIG["rms_up"], 1)
                        dve.wait_ge(SIG["rms_gate"], n0 + n + 1)
                        dve.wait_ge(SIG["rms_up"], 2 * (n0 + n) + 1)
                        dve.sem_inc(banks_free, 1)
                        dve.wait_ge(gate_done, n0 + n + 1)
                        V.tensor_tensor(h32[:, s, :], act_out[:, s, :], h32[:, s, :],
                                        ALU.mult).then_inc(SIG["rms_up"], 1)
                    dve.wait_ge(h_hi_done, n0 + n + 1)
                    V.tensor_tensor(h_lo[:, bass.ds(n, 1), :], h32[:, s:s + 1, :], h_hi[:, bass.ds(n, 1), :],
                                    ALU.subtract).then_inc(h_done, 1)
                pairs(f"up{f}", post)

            def is_last(phase, i, j):
                per_pair = 4 if phase[0] == "d" else 2
                return isinstance(i, int) and per_pair * i + j == UNITS[phase] - 1

            def clear_acc(name, *read):
                dve.wait_ge(*read)
                V.memset(acc[:, :, :, :], 0.0).then_inc(acc_done, 1)
                dve.wait_ge(acc_done, ACC0[name] + 1)

            def end_rms(phase):
                u0, down = UNIT0[phase], phase[0] == "d"

                def post(i, j):
                    if down and j % 2 == 0:
                        return
                    n = 2 * i + (j // 2 if down else j)
                    dve.wait_ge(sq_done, SQ0[phase] + n + 1)
                    dve.wait_ge(y_copied, YC0[phase] + (n + 1 if down else 2 * n + 2))
                    if is_last(phase, i, j):
                        dve.sem_inc(banks_free, 2 if down else 1)
                        return
                    dve.wait_ge(banks_free, u0 + (4 * i + 2 * (j // 2) if down else 2 * i + j) + 2)
                    if down:
                        V.tensor_tensor(acc[:, 1, j // 2, :], acc[:, 1, j // 2, :], sq[:, 0, :],
                                        ALU.add).then_inc(banks_free, 2)
                    else:
                        V.tensor_tensor(acc[:, 1, :, :], acc[:, 1, :, :], sq[:, :, :],
                                        ALU.add).then_inc(banks_free, 1)
                pairs(phase, post, 4 if down else 2)

            def end_ln(phase):
                u0, down = UNIT0[phase], phase[0] == "d"

                def post(i, j):
                    if down and j % 2 == 0:
                        return
                    n = 2 * i + (j // 2 if down else j)
                    dve.wait_ge(gemm_done, 2 * u0 + (8 if down else 4) * i + (2 * j + 6))
                    if down:
                        xs, ys, par = x[:, bass.ds(n, 1), :], bank[:, 4 + j // 2:5 + j // 2, :], slice(j // 2, j // 2 + 1)
                    else:
                        xs, ys, par = x[:, bass.ds(2 * n, 2), :], bank[:, 2 * j:2 * j + 2, :], slice(0, 2)
                    V.scalar_tensor_tensor(xs, xs, ALPHA, ys, ALU.mult, ALU.add).then_inc(banks_free, 2 if down else 1)
                    if is_last(phase, i, j):
                        return
                    dve.wait_ge(banks_free, u0 + (4 if down else 2) * i + (j + 3))
                    dve.wait_ge(acc_done, ACC0[phase] + 2 * n + 1)
                    V.tensor_tensor(acc[:, 0, par, :], acc[:, 0, par, :], xs, ALU.add).then_inc(acc_done, 1)
                    dve.wait_ge(sq_done, SQ0[phase] + n + 1)
                    V.tensor_tensor(acc[:, 1, par, :], acc[:, 1, par, :],
                                    sq[:, 0:1, :] if down else sq[:, :, :], ALU.add).then_inc(acc_done, 1)
                pairs(phase, post, 4 if down else 2)

            def spread(column, j):
                V.tensor_tensor(diag[:, j, :, :], ident[:, :].unsqueeze(1).broadcast_to([P, NT, P]),
                                column.unsqueeze(2).broadcast_to([P, NT, P]), ALU.mult).then_inc(scale_col, 1)

            def inverse_root(name, ahead=None):
                dve.wait_ge(stat_a, ST0[name] + 1)
                link(V.reciprocal(stat[:, 8:12], stat[:, 8:12]))
                spread(stat[:, 8:12], 0)
                if ahead:
                    split_ahead(ahead)
                dve.wait_ge(scale_bc, SC0[name] + 1)

            def residual(name, y, then=lambda k: None):
                for k in range(KD):
                    ins = V.tensor_tensor(y[:, k, :], y[:, k, :], bank[:, 6, :], ALU.mult)
                    if k % 2:
                        ins.then_inc(norm_t, 1)
                    else:
                        link(ins)
                        V.tensor_tensor(x[:, k, :], x[:, k, :], y[:, k, :], ALU.add).then_inc(x_dve, 1)
                    if k >= 2:
                        then(k - 2)
                then(KD - 2)
                then(KD - 1)

            def scaled_low(gen, g0, k):
                dve.wait_ge(a_hi_done, gen_at(gen, k))
                V.scalar_tensor_tensor(a_lo[:, k, :], x[:, k, :], vec[:, g0 + k:g0 + k + 1], a_hi[:, k, :],
                                       ALU.mult, ALU.subtract).then_inc(a_odd if k % 2 else a_even, 1)

            def take_scale(name):
                inverse_root(name)
                link(V.tensor_copy(scale[:, :], bank[:, 7, :]))

            def normalise(gen, g0):
                def low(k):
                    dve.wait_ge(a_hi_done, gen_at(gen, k))
                    V.tensor_tensor(a_lo[:, k, :], buf(k), a_hi[:, k, :], ALU.subtract).then_inc(a_even, 1)
                for k in range(KD):
                    if k >= 4:
                        dve.wait_ge(*low_at(gen, k - 4))
                    V.scalar_tensor_tensor(buf(k), x[:, k, :], vec[:, g0 + k:g0 + k + 1], bank[:, 7, :],
                                           ALU.mult, ALU.mult).then_inc(norm_t, 1)
                    if k % 2 and k >= 1:
                        low(k - 1)

            def ln_columns(name):
                n = LN_ENDS.index(name)
                dve.wait_ge(stats, STAT_N[name])
                link(V.tensor_scalar(stat[:, 0:8], bank[:, 6, 0:2 * NT], 1.0 / D, None, ALU.mult))
                link(V.tensor_tensor(stat[:, 8:12], stat[:, 0:4], stat[:, 0:4], ALU.mult))
                link(V.tensor_tensor(stat[:, 8:12], stat[:, 4:8], stat[:, 8:12], ALU.subtract))
                V.tensor_scalar(stat[:, 8:12], stat[:, 8:12], 0.0, None, ALU.max).then_inc(stat_v, 1)
                dve.wait_ge(stat_a, ST0[name] + 1)
                link(V.reciprocal(stat[:, 8:12], stat[:, 8:12]))
                spread(stat[:, 8:12], 0)
                link(V.scalar_tensor_tensor(stat[:, 0:4], stat[:, 0:4], -1.0, stat[:, 8:12], ALU.mult, ALU.mult))
                spread(stat[:, 0:4], 1)
                if NEXT[name] and name[:5] not in ("about", "cout"):
                    split_ahead(NEXT[name])
                dve.wait_ge(scale_bc, SC0[name] + 2)

            def ln_norm(name, k):
                if k >= 4:
                    dve.wait_ge(x_act, XACT0[name] + k - 3)
                link(V.tensor_tensor(buf(k), x[:, k, :], bank[:, 6, :], ALU.mult))
                V.tensor_tensor(buf(k), buf(k), bank[:, 7, :], ALU.add).then_inc(norm_t, 1)

            def ln_low(name, k):
                if NEXT[name] and k % 2 == 0:
                    dve.wait_ge(a_hi_done, gen_at(NEXT[name], k))
                    dve.wait_ge(x_act, XACT0[name] + k + 1)
                    V.tensor_tensor(a_lo[:, k, :], x[:, k, :], a_hi[:, k, :], ALU.subtract).then_inc(a_even, 1)

            def low_parts(gen, srcs, ks=(0, 2, 4, 6)):
                for k in ks:
                    dve.wait_ge(a_hi_done, gen_at(gen, k))
                    V.tensor_tensor(a_lo[:, k, :], srcs(k), a_hi[:, k, :], ALU.subtract).then_inc(a_even, 1)

            def mlstm_args(h):
                dve.wait_ge(SIG["mlstm_m_mm"], h + 1)
                if h:
                    dve.wait_ge(SIG["mlstm_den_mm"], h)
                for s in range(NT):
                    V.tensor_scalar(mp[:, s * T + s * P:(s + 1) * T], bank[:, 4, s * P:T],
                                    ct[:, 0, s, h:h + 1], 0.0, ALU.add, ALU.min).then_inc(SIG["mlstm_arg"], 1)

            def mlstm_probs(h):
                for i, s in enumerate((0, 1, 3, 2)):
                    b, c0 = SCORE_AT[s]
                    dve.wait_ge(SIG["mlstm_scores_mm"], 4 * h + (1, 3, 3, 4)[i])
                    dve.wait_ge(SIG["mlstm_weight"], 4 * h + s + 1)
                    V.scalar_tensor_tensor(mp[:, s * T + s * P:(s + 1) * T], bank[:, b, c0:c0 + T - s * P], 64.0 ** -0.5,
                                           mp[:, s * T + s * P:(s + 1) * T], ALU.mult, ALU.mult
                                           ).then_inc(SIG["mlstm_p"], 1)
                dve.wait_ge(SIG["mlstm_p"], 4 * h + NT)
                diags = mp[:, :].rearrange("p (s c) -> p s c", s=NT)[:, :, 0:P]
                V.tensor_tensor(diags, diags, tri[:, 0:1, :].broadcast_to([P, NT, P]),
                                ALU.mult).then_inc(SIG["mlstm_masked"], 1)

            def mlstm_scale(h):
                den, scale = mcol[:, 2, :], mcol[:, 3, :]
                dve.wait_ge(SIG["mlstm_den_mm"], h + 1)
                link(V.tensor_scalar(den, bank[:, 6, 0:NT], -1.0, None, ALU.mult))
                link(V.tensor_tensor(den, den, bank[:, 6, 0:NT], ALU.max))
                link(V.tensor_tensor(den, den, ct[:, 1, :, h], ALU.max))
                link(V.reciprocal(den, den))
                link(V.tensor_tensor(mcol[:, 1, :], den, den, ALU.mult))
                dve.wait_ge(SIG["mlstm_square"], 4 * h + 4)
                V.tensor_tensor(mcol[:, 1, :], mcol[:, 1, :], mcol[:, 0, :], ALU.mult).then_inc(SIG["mlstm_ms"], 1)
                dve.wait_ge(SIG["mlstm_rms"], h + 1)
                link(V.reciprocal(scale, mcol[:, 1, :]))
                link(V.tensor_tensor(scale, scale, den, ALU.mult))
                if h:
                    dve.wait_ge(SIG["mlstm_turned"], h)
                V.tensor_tensor(mtmp[:, 0, :].rearrange("p (n v) -> p n v", n=NT),
                                bank[:, 5, :].rearrange("p (n v) -> p n v", n=NT),
                                scale.unsqueeze(2).broadcast_to([P, NT, P]), ALU.mult).then_inc(SIG["mlstm_scaled"], 1)

            def mlstm_gated(h):
                dve.wait_ge(SIG["mlstm_turned"], h + 1)
                c0 = VCOL["mlstm_norm"] + h
                V.scalar_tensor_tensor(mgate[:, h, :], bank[:, 7, :], vec[:, c0:c0 + 1], mgate[:, h, :],
                                       ALU.mult, ALU.mult).then_inc(SIG["mlstm_y"], 1)

            V.memset(ones[:, :], 1.0)
            V.memset(eps6, 1e-6)
            V.memset(eps5, 1e-5)
            V.memset(one, 1.0).then_inc(consts_v, 1)
            dve.sem_inc(w_split, SLOTS)
            dve.sem_inc(gemm_done, 4)
            dve.sem_inc(banks_free, 2)
            dve.wait_ge(consts, 48)
            link(V.tensor_scalar(half_g[:, :], vec[:, VCOL["norm_post"]:VCOL["norm_post"] + 24], 0.5, None, ALU.mult))
            split(0, 0, FULL)
            for k in range(KD):
                if k == 2:
                    split_ahead("up0")
                scaled_low("up0", VCOL["norm_pre"], k)
            take_scale("x0")
            up(0)
            clear_acc("down0", h_done, F0[0] + KF)
            end_rms("down0")
            inverse_root("down0", "mixin")
            residual("down0", y_ff)
            inverse_root("pre_mixin")
            normalise("mixin", VCOL["norm_pre"] + 8)

            mi = UNIT0["mixin"]
            dve.wait_ge(mix_in[0], 16)
            dve.wait_ge(mix_in[1], 16)
            dve.wait_ge(mix_in[2], 16)
            V.tensor_tensor(lb[:, 0, :], lbt[:, 0, :], lbt[:, 1, :], ALU.subtract)
            V.tensor_tensor(lb[:, 1, :], lbt[:, 1, :], lbt[:, 0, :], ALU.subtract).then_inc(SIG["lb_diff"], 1)
            dve.wait_ge(SIG["gate_w_hi"], 1)
            V.tensor_tensor(wg_lo[:, :, :], wg_raw[:, :, :], wg_hi[:, :, :], ALU.subtract).then_inc(SIG["gate_w_lo"], 1)
            dve.wait_ge(SIG["lb_sigmoid"], 1)
            cw = VCOL["conv_w"]
            for u in range(2):
                split_next(mi + u)
                for m in range(2):
                    t = 2 * u + m
                    dve.wait_ge(SIG["mconv_start"], t + 1)
                    for tap in (1, 2, 3):
                        ins = V.scalar_tensor_tensor(mqk[:, t, tap:T], bank[:, 2 * u + m, 0:T - tap],
                                                     vec[:, cw + 4 * (3 - tap) + t:cw + 4 * (3 - tap) + t + 1],
                                                     mqk[:, t, tap:T], ALU.mult, ALU.add)
                        if tap < 3:
                            link(ins)
                        else:
                            ins.then_inc(SIG["mconv_done"], 1)
                dve.wait_ge(SIG["mconv_done"], 2 * u + 1 + 1)
                dve.sem_inc(banks_free, 1)
            def value_unit(u):
                split_next(mi + u)
                dve.wait_ge(SIG["mlstm_v"], u - 1)
                dve.sem_inc(banks_free, 1)

            def scan(op):
                for n in range(9):
                    d = 1 << n
                    src, dst = rows[:, n % 2, :], rows[:, 1 - n % 2, :]
                    link(V.tensor_tensor(dst[:, 256:256 + T], src[:, 256:256 + T], src[:, 256 - d:256 - d + T], op))

            value_unit(2)
            V.memset(rows[:, :, 0:256], 0.0)
            dve.wait_ge(SIG["f_row_log"], 1)
            link(V.scalar_tensor_tensor(rows[:, 0, 256:256 + T], row_b[:, :], 0.0, row_t[:, :], ALU.min, ALU.subtract))
            scan(ALU.add)
            link(V.tensor_copy(row_b[:, :], rows[:, 1, 256:256 + T]))
            V.tensor_tensor(row_t[:, :], row_i[:, :], row_b[:, :], ALU.subtract).then_inc(SIG["c_row"], 1)
            value_unit(3)
            dve.wait_ge(SIG["c_row"], 1)
            link(V.tensor_scalar(rows[:, 0, 256:256 + T], row_t[:, :], 0.0, None, ALU.max))
            scan(ALU.max)
            V.tensor_scalar(row_nm[:, :], rows[:, 1, 256:256 + T], -1.0, None, ALU.mult).then_inc(SIG["neg_m_row"], 1)
            dve.wait_ge(SIG["neg_m_row"], 1)
            V.tensor_tensor(row_em[:, :], row_nm[:, :], row_b[:, :], ALU.subtract).then_inc(SIG["neg_bm_row"], 1)
            for u in (4, 5):
                split_next(mi + u)
                dve.wait_ge(SIG["mlstm_gate"], u - 4 + 1)
                dve.sem_inc(banks_free, 1)
            dve.wait_ge(SIG["c_columns_mm"], 1)
            V.tensor_copy(ct[:, :, :, :], bank[:, 5, 0:2 * NT * HEADS].rearrange("p (w s h) -> p w s h", w=2, h=HEADS)
                          ).then_inc(SIG["c_columns"], 1)
            dve.wait_ge(SIG["c_columns"], 1)
            for h in range(HEADS):
                for j in range(2):
                    u = 6 + 2 * h + j
                    split_next(mi + u)
                    dve.wait_ge(SIG["hgrn_input"], 2 * h + j + 1)
                    dve.sem_inc(banks_free, 1)
                    if h == 0:
                        cols = slice(j * 256, (j + 1) * 256)
                        s4 = sigm[:, :, :, :].rearrange("p a t c -> p (a t) c")
                        link(V.tensor_tensor(s4, s4, lb[:, 1:2, cols].broadcast_to([P, NT, 256]), ALU.mult))
                        V.tensor_tensor(logf[:, :, cols], s4, lb[:, 0:1, cols].broadcast_to([P, NT, 256]),
                                        ALU.add).then_inc(SIG["forget_ready"], 1)
                    if j == 0:
                        mlstm_args(h)
                        if h:
                            mlstm_gated(h - 1)
                        mlstm_probs(h)
                    else:
                        mlstm_scale(h)

            V.tensor_scalar(k_tm[:, :, :], logf[:, :, :], -1.0, 1.0, ALU.mult, ALU.add).then_inc(SIG["keys_tm"], 1)
            mlstm_gated(HEADS - 1)
            dve.wait_ge(SIG["rest_decay"], 1)
            dve.wait_ge(SIG["keys_tm"], 1)
            V.tensor_tensor(kdec[:, :, :], k_tm[:, :, :], lev[0][:, :, :], ALU.mult).then_inc(SIG["keys_decayed"], 1)
            dve.wait_ge(SIG["q_decay"], 1)
            link(V.tensor_tensor(q_dec[:, :, :], q_dec[:, :, :], q_fm[:, :, :], ALU.mult))
            split_ahead("mixout")
            link(V.memset(scores[:, :, :], 0.0))

            def blocks(t, hs):
                return t[:, :, :].rearrange("p h (n two c) -> p (h n) two c", two=2, c=hs)

            def level_dif(l):
                hs = LEVELS[l]
                g, d = blocks(Gc, hs), blocks(lev[l % 2], hs)
                n = HEADS * T // (2 * hs)
                mid = g[:, :, 0, hs - 1:hs].broadcast_to([P, n, hs])
                V.tensor_tensor(d[:, :, 1, :], g[:, :, 1, :], mid, ALU.subtract)
                V.tensor_tensor(d[:, :, 0, :], mid, g[:, :, 0, :], ALU.subtract).then_inc(SIG["level_diff"], 1)

            def level_mul(l):
                hs = LEVELS[l]
                d = blocks(lev[l % 2], hs)
                dve.wait_ge(SIG["level_exp"], l + 1)
                V.tensor_tensor(d[:, :, 1, :], d[:, :, 1, :], blocks(q_fm, hs)[:, :, 1, :], ALU.mult)
                V.tensor_tensor(d[:, :, 0, :], d[:, :, 0, :], blocks(k_fm, hs)[:, :, 0, :], ALU.mult).then_inc(SIG["level_ready"], 1)

            def take_scores(l):
                dve.wait_ge(SIG["level_scores_mm"], l + 1)
                if l:
                    dve.wait_ge(SIG["scores_taken"], l)
                V.copy_predicated(scores[:, :, :].rearrange("p h (n c) -> p (h n) c", c=P),
                                  masks[:, l:l + 1, :].broadcast_to([P, HEADS * NT, P]),
                                  bank[:, 4 * (l % 2):4 * (l % 2) + 4, :].rearrange("p h (n c) -> p (h n) c", c=P)
                                  ).then_inc(SIG["scores_taken"], 1)

            level_dif(0)
            low_parts("mixout", lambda k: mgate[:, k - HEADS, :], (4, 6))
            dve.wait_ge(SIG["state_add_mm"], 1)
            link(V.tensor_copy(states[:, 0, :, :], bank[:, 4, :].rearrange("p (h v) -> p h v", h=HEADS)))
            dve.wait_ge(SIG["chunk_decay"], 1)
            for n in (1, 2):
                for h in range(HEADS):
                    ins = V.scalar_tensor_tensor(states[:, n, h, :], states[:, n - 1, h, :],
                                                 g_end[:, h * NT + n:h * NT + n + 1],
                                                 bank[:, 4 + n, h * P:(h + 1) * P], ALU.mult, ALU.add)
                    if h == HEADS - 1 and n == 1:
                        link(ins)
            ins.then_inc(SIG["states_ready"], 1)
            dve.wait_ge(mask_in, 16)
            level_mul(0)
            for l in range(1, len(LEVELS)):
                if l >= 2:
                    dve.wait_ge(SIG["level_scores_mm"], l)
                level_dif(l)
                take_scores(l - 1)
                level_mul(l)
            take_scores(len(LEVELS) - 1)
            take_scores(len(LEVELS))
            for n in range(NT):
                dve.wait_ge(SIG["hgrn_square"], n + 1)
                ins = V.tensor_reduce(hcol[:, n, :], lev[1][:, n, :].rearrange("p (h v) -> p h v", h=HEADS), AX.X, ALU.add)
            ins.then_inc(SIG["hgrn_ms"], 1)
            dve.wait_ge(SIG["hgrn_rms"], 1)
            link(V.reciprocal(hcol[:, :, :], hcol[:, :, :]))
            for n in range(NT):
                V.tensor_tensor(lev[0][:, n, :].rearrange("p (h v) -> p h v", h=HEADS),
                                bank[:, n, :].rearrange("p (h v) -> p h v", h=HEADS),
                                hcol[:, n, :].unsqueeze(2).broadcast_to([P, HEADS, P]),
                                ALU.mult).then_inc(SIG["hgrn_scaled"], 1)
            dve.wait_ge(SIG["hgrn_turned"], 1)
            for h in range(HEADS):
                c0 = VCOL["hgrn_norm"] + h
                V.scalar_tensor_tensor(hgate[:, h, :], bank[:, 4 + h, :], vec[:, c0:c0 + 1], hgate[:, h, :],
                                       ALU.mult, ALU.mult).then_inc(SIG["hgrn_y"], 1)
            low_parts("mixout", lambda k: hgate[:, k, :], (0, 2))
            clear_acc("mixout", *low_at("mixout", 2))
            end_rms("mixout")
            inverse_root("mixout", "up1")
            residual("mixout", y_mix, lambda k: scaled_low("up1", VCOL["norm_pre"] + 16, k))
            take_scale("pre_up1")
            up(1)
            clear_acc("down1", h_done, F0[1] + KF)
            end_rms("down1")
            inverse_root("down1", "ab")
            residual("down1", y_ff)
            low_parts("ab", lambda k: x[:, k, :])

            ab = UNIT0["ab"]
            for u in range(2):
                split_next(ab + u)
                dve.wait_ge(SIG["sgu_v"], u + 1)
                dve.sem_inc(banks_free, 1)
            for t in range(NT):
                link(V.bn_stats(bn[:, t, :], gv[:, t, :]))
                V.bn_aggr(mv4[:, t, :], bn[:, t, :]).then_inc(SIG["sgu_stats"], 1)
            for u in (2, 3):
                split_next(ab + u)
                dve.wait_ge(SIG["sgu_u"], u - 2 + 1)
                dve.sem_inc(banks_free, 1)
            dve.wait_ge(SIG["sgu_std"], 1)
            link(V.reciprocal(rs4[:, :], rs4[:, :]))
            for t in range(NT):
                ins = V.tensor_scalar(gv[:, t, :], gv[:, t, :], mv4[:, t, 0:1], rs4[:, t:t + 1], ALU.subtract, ALU.mult)
            link(ins)
            for n in range(4):
                dve.wait_ge(ab_in[n], 16)
            link(V.tensor_tensor(gv[:, :, :], gv[:, :, :], ab_rows[:, 0:1, :].broadcast_to([P, NT, T]), ALU.mult))
            V.memset(ws_t[64:128, :, 0:64], 0.0)
            V.tensor_tensor(gv[:, :, :], gv[:, :, :], ab_rows[:, 1:2, :].broadcast_to([P, NT, T]),
                            ALU.add).then_inc(SIG["sgu_v_ready"], 1)
            for n in range(3):
                V.memset(pool[n][:, :, 0:PAD], 0.0)
            for u in (4, 5):
                split_next(ab + u)
                dve.wait_ge(SIG["pool_in"], u - 4 + 1)
                dve.sem_inc(banks_free, 1)
            split_ahead("about")
            dve.wait_ge(SIG["spatial_mm"], 1)
            for g in range(4):
                b4 = bank[:, 4 + g, :].rearrange("p (n c) -> p n c", c=P)
                o4 = gv[:, g, :].rearrange("p (n c) -> p n c", c=P)
                link(V.tensor_tensor(o4, b4, ab_rows[:, 2:3, g * P:(g + 1) * P].broadcast_to([P, NT, P]), ALU.add))
                V.tensor_tensor(ug[:, g, :], ug[:, g, :], gv[:, g, :], ALU.mult).then_inc(SIG["ab_ya"], 1)
            for g in range(4):
                src = pool[0]
                for n in range(g + 1):
                    dst = pool[1 + n % 2]
                    link(V.tensor_tensor(dst[:, g, PAD:PAD + T], src[:, g, PAD:PAD + T],
                                         src[:, g, PAD - (1 << n):PAD - (1 << n) + T], ALU.add))
                    src = dst
                first, rest = slice(PAD, 2 * PAD), slice(2 * PAD, PAD + T)
                link(V.tensor_tensor(src[:, g, first], src[:, g, first], inv_cnt[:, g, :], ALU.mult))
                V.tensor_tensor(pool[2][:, g, first], src[:, g, first], pool[0][:, g, first], ALU.subtract)
                V.scalar_tensor_tensor(pool[2][:, g, rest], src[:, g, rest], 1.0 / (2 << g), pool[0][:, g, rest],
                                       ALU.mult, ALU.subtract).then_inc(SIG["pooled"], 1)
            for g in range(4):
                dve.wait_ge(SIG["pool_mm"], g + 1)
                c0 = VCOL["pool_scale_2"] + g
                V.tensor_scalar(pool[1][:, g, PAD:PAD + T], bank[:, g, :], vec[:, c0:c0 + 1], None,
                                ALU.mult).then_inc(SIG["ab_yb"], 1)
            dve.wait_ge(SIG["mem_hi_done"], 1)
            V.tensor_tensor(mem_lo[:, :, :], mem_raw[:, :, :], mem_hi[:, :, :], ALU.subtract).then_inc(SIG["mem_lo_done"], 1)
            low_parts("about", lambda k: ug[:, k, :] if k < 4 else pool[1][:, k - 4, PAD:PAD + T])
            for layer in range(2):
                if layer == 1:
                    ci, cw = UNIT0["cin"], VCOL["c_conv_w_2"]
                    dve.wait_ge(SIG["mem_hi_done"], 2)
                    V.tensor_tensor(mem_lo[:, :, :], mem_raw[:, :, :], mem_hi[:, :, :],
                                    ALU.subtract).then_inc(SIG["mem_lo_done"], 1)
                    for u in range(12):
                        split_next(ci + u)
                        b = 2 * (u % 2)
                        if u < 8:
                            dve.wait_ge(SIG["c_gate"], u + 1)
                            dve.wait_ge(gemm_done, gemm_at(ci + u))
                            V.tensor_tensor(ch[:, u % 2, :], cc[:, u % 2, :], bank[:, b + 1, :],
                                            ALU.mult).then_inc(SIG["c_product"], 1)
                            dve.wait_ge(SIG["c_product"], u + 1)
                            dve.sem_inc(banks_free, 1)
                            dve.wait_ge(SIG["c_conv_start"], u + 1)
                            for tap in (1, 2):
                                c0 = cw + 8 * (2 - tap) + u
                                link(V.scalar_tensor_tensor(yc[:, u, tap:T], ch[:, u % 2, 0:T - tap],
                                                            vec[:, c0:c0 + 1], yc[:, u, tap:T], ALU.mult, ALU.add))
                        else:
                            j = 2 * (u - 8)
                            dve.wait_ge(gemm_done, gemm_at(ci + u))
                            V.tensor_tensor(yc[:, j:j + 2, :], yc[:, j:j + 2, :], bank[:, b:b + 2, :],
                                            ALU.mult).then_inc(SIG["c_y"], 1)
                            dve.wait_ge(SIG["c_y"], u - 8 + 1)
                            dve.sem_inc(banks_free, 1)
                    low_parts("cout", lambda k: yc[:, k, :], (0,))
                    split_ahead("cout")
                    low_parts("cout", lambda k: yc[:, k, :], (2, 4, 6))
                end = ("about", "cout")[layer]
                clear_acc(end, *low_at(end, 6))
                end_ln(end)
                kv = UNIT0[f"kv{layer}"]
                split_ahead(f"kv{layer}")
                ln_columns(end)
                ln_norm(end, 0)
                for k in range(KD):
                    if k:
                        split_next(kv + k)
                        dve.wait_ge(SIG["mem_kv"], 8 * layer + k)
                        dve.sem_inc(banks_free, 1)
                    if k + 1 < KD:
                        ln_norm(end, k + 1)
                    ln_low(end, k)
                dve.wait_ge(SIG["mem_kv"], 8 * layer + KD)
                dve.sem_inc(banks_free, 1)
                q0 = UNIT0[f"q{layer}"]
                for u in range(4):
                    split_next(q0 + u)
                    dve.wait_ge(SIG["attn_q"], 4 * layer + u + 1)
                    dve.sem_inc(banks_free, 1)
                split_ahead(f"wo{layer}")
                for h in range(HEADS + 1):
                    if h < HEADS:
                        p, b = h % 2, 2 * (h % 2)
                        dve.wait_ge(SIG["attn_scores_mm"], 4 * layer + h + 1)
                        link(V.tensor_reduce(at_s[:, p, 0, :], bank[:, b:b + 2, :].rearrange("p b (t m) -> p (b t) m", t=2),
                                             AX.X, ALU.max))
                        V.tensor_scalar(at_s[:, p, 1, :], at_s[:, p, 0, :], -(256.0 ** -0.5), None,
                                        ALU.mult).then_inc(SIG["attn_max"], 1)
                    if h:
                        g = h - 1
                        dve.wait_ge(SIG["attn_out_mm"], 4 * layer + g + 1)
                        if g:
                            dve.wait_ge(*low_at(f"wo{layer}", 2 * g - 2))
                            dve.wait_ge(*low_at(f"wo{layer}", 2 * g - 1))
                        V.tensor_copy(o32[:, :, :], bank[:, 6:8, :]).then_inc(SIG["attn_o32"], 1)
                        dve.wait_ge(a_hi_done, gen_at(f"wo{layer}", 2 * g))
                        V.tensor_tensor(a_lo[:, 2 * g, :], o32[:, 0, :], a_hi[:, 2 * g, :],
                                        ALU.subtract).then_inc(a_even, 1)
                    if h < HEADS:
                        dve.wait_ge(SIG["attn_exp"], 16 * layer + 4 * h + 4)
                        link(V.reciprocal(at_s[:, p, 0, :], at_s[:, p, 2, :]))
                        V.tensor_tensor(pe_at[:, p, :, :], pe_at[:, p, :, :],
                                        at_s[:, p, 0, :].unsqueeze(2).broadcast_to([P, NT, MEM]),
                                        ALU.mult).then_inc(SIG["attn_probs"], 1)
                end = f"wo{layer}"
                for end in (f"wo{layer}", f"down{2 + layer}"):
                    if end[0] == "d":
                        up(2 + layer)
                    clear_acc(end, *((h_done, F0[2 + layer] + KF) if end[0] == "d" else low_at(end, 6)))
                    end_ln(end)
                    ln_columns(end)
                    ln_norm(end, 0)
                    for k in range(KD):
                        if k + 1 < KD:
                            ln_norm(end, k + 1)
                        ln_low(end, k)


def kernel(**inputs):
    import numpy as np
    import concourse.bacc as bacc
    from concourse.bass_utils import run_bass_kernel_spmd

    def tiles(w, order):
        n = w.shape[1] // P
        w = w.reshape(KD, P, n, P).transpose(2, 1, 0, 3)[np.asarray(order)]
        return w.reshape(len(order) // 2, 2, P, KD * P).transpose(0, 2, 1, 3).reshape(-1, P, FULL)

    def columns(w, first, n):
        w = w[:, first:first + 256 * n]
        return w.reshape(KD, P, n, 256).transpose(2, 1, 0, 3).reshape(n, P, FULL)

    def down(w):
        return w.reshape(2, HALF_KF, P, KD, P).transpose(3, 0, 2, 1, 4).reshape(16, P, DOWN)

    def both(first, second):
        return [t for j in range(KF) for t in (first + j, second + j)]

    i = inputs
    mix, ab, cin = i["w_mix_in"][0], i["ab_w_in_2"][0], i["c_w_in_2"][0]
    full = [tiles(i["ffn1_w_in"][0], both(0, KF)),
            tiles(mix[:, :3584], [16, 17, 18, 19]), columns(mix, 2560, 2), tiles(mix[:, :3584], [24, 25, 26, 27]),
            columns(mix, 512, 2), columns(mix, 1024, 2),
            tiles(mix[:, :3584], [0, 1, 2, 3]), tiles(mix[:, :3584], [12, 13, 14, 15]),
            tiles(i["w_mix_out"][0], range(KD)),
            tiles(i["ffn2_w_in"][0], both(0, KF)),
            columns(ab, 512, 2), tiles(ab, [0, 1, 2, 3, 8, 9, 10, 11]), tiles(i["ab_w_out_2"][0], range(KD))]
    for layer in range(2):
        wkv = i["xa_wkv_2"][layer]
        if layer:
            full += [tiles(cin, [t for j in range(8) for t in (8 + j, 16 + j)] + list(range(8))),
                     tiles(i["c_w_out_2"][0], range(KD))]
        full += [tiles(wkv[:, :D], range(KD)), columns(wkv, D, 4), tiles(i["xa_wq_2"][layer], range(KD)),
                 tiles(i["xa_wo_2"][layer], range(KD)), tiles(i["ffn_w_up_2"][layer], both(KF, 0))]

    def vector(w):
        return np.asarray(w).reshape(-1, P).T

    steps = np.arange(P)
    s, t = steps[:, None], steps[None, :]
    masks = [s == t] + [(s // (2 * h) == t // (2 * h)) & (s // h % 2 == 0) & (t // h % 2 == 1) for h in LEVELS]
    counts = np.stack([1.0 / np.minimum(np.arange(16) + 1, 2 << g) for g in range(4)])

    def every(w):
        return np.broadcast_to(w, (P,) + w.shape)

    w_gates = np.zeros((D, P), np.float32)
    w_gates[:, 0:HEADS], w_gates[:, 32:32 + HEADS] = mix[:, 3584:3588], mix[:, 3588:3592]
    arrays = {
        "w_full": np.concatenate(full), "w_down": np.concatenate(
            [down(w) for w in (i["ffn1_w_out"][0], i["ffn2_w_out"][0], i["ffn_w_down_2"][0], i["ffn_w_down_2"][1])]),
        "vectors": np.concatenate([vector(i[n]) for n, _ in VECTORS], axis=1),
        "identity": np.eye(P, dtype=np.float32),
        "x": i["x"][0].T.reshape(KD, P, T).transpose(1, 0, 2),
        "w_gates": w_gates.reshape(KD, P, P).transpose(1, 0, 2),
        "gate_bias": i["mlstm_gate_bias"].reshape(2, HEADS).T,
        "sel": np.repeat(np.eye(HEADS, dtype=np.float32)[:, :, None], P, axis=2),
        "tri": np.stack([s <= t, s > t], axis=1).astype(np.float32),
        "masks": np.stack(masks, axis=1).astype(np.uint32),
        "lb_rows": every(i["hgrn_lb_logits"]),
        "ab_rows": every(np.stack([i["sgu_ln_g_2"][0], i["sgu_ln_b_2"][0], i["sgu_b_2"][0].reshape(-1)])),
        "ws_t": i["sgu_w_2"][0].transpose(2, 0, 1),
        "pool_w": i["pool_w_2"][0].transpose(1, 0, 2),
        "inv_cnt": every(counts.astype(np.float32)),
        "mem": i["mem_2"][0].T.reshape(KD, P, MEM).transpose(1, 0, 2),
    }
    arrays = {n: np.ascontiguousarray(v) for n, v in arrays.items()}
    nc = bacc.Bacc("TRN2", target_bir_lowering=False, num_devices=1)
    aps = {n: nc.dram_tensor(n, v.shape, mybir.dt.from_np(v.dtype), kind="ExternalInput").ap()
           for n, v in arrays.items()}
    aps["out"] = nc.dram_tensor("out", (P, KD, T), mybir.dt.float32, kind="ExternalOutput").ap()
    build(nc, aps)
    r = run_bass_kernel_spmd(nc, [arrays], core_ids=[0])
    y = r.results[0]["out"]
    return np.ascontiguousarray(y.transpose(1, 0, 2).reshape(D, T).T)[None]
```

```python
import concourse.bass as bass
from concourse import mybir
from contextlib import ExitStack

P = 128
T = 512
D = 1024
KD = D // P
FF = 2816
KF = FF // P
HALF_KF = KF // 2
MEM = 256
NT = T // P
HEADS = 4
CHUNK = 128
FULL = 16 * P
DOWN = HALF_KF * P
LEVELS = (64, 32, 16, 8, 4, 2, 1)
ALPHA = (2 * 2) ** 0.25
SLOTS = 2

PHASES = [("up0", KF, 16), ("down0", 16, HALF_KF), ("mixin", 14, 16), ("mixout", 4, 16),
          ("up1", KF, 16), ("down1", 16, HALF_KF),
          ("ab", 6, 16), ("about", 4, 16), ("kv0", 8, 16), ("q0", 4, 16), ("wo0", 4, 16),
          ("up2", KF, 16), ("down2", 16, HALF_KF),
          ("cin", 12, 16), ("cout", 4, 16), ("kv1", 8, 16), ("q1", 4, 16), ("wo1", 4, 16),
          ("up3", KF, 16), ("down3", 16, HALF_KF)]
UNIT0, UNITS, UNIT_COLS, SOURCE0 = {}, {}, [], {}
_full = _down = 0
for _name, _n, _tiles in PHASES:
    UNIT0[_name], UNITS[_name] = len(UNIT_COLS), _n
    UNIT_COLS += [_tiles * P] * _n
    SOURCE0[_name] = _full if _tiles == 16 else _down
    if _tiles == 16:
        _full += _n
    else:
        _down += _n
N_UNITS = len(UNIT_COLS)

VECTORS = [("norm_pre", 24), ("norm_post", 24), ("ln_mix_g_2", 16), ("ln_mix_b_2", 16), ("ln_xa_g_2", 16),
           ("ln_xa_b_2", 16), ("ln_ffn_g_2", 16), ("ln_ffn_b_2", 16), ("conv_w", 16), ("conv_b", 4),
           ("ffn_conv_w_2", 2 * 3 * KF), ("ffn_conv_b_2", 2 * KF), ("c_conv_w_2", 24), ("pool_scale_2", 4),
           ("hgrn_norm", 4), ("mlstm_norm", 4)]
VCOL, _c = {}, 0
for _name, _n in VECTORS:
    VCOL[_name] = _c
    _c += _n
N_VEC = _c

GEN = {n: i for i, n in enumerate(["up0", "mixin", "mixout", "up1", "ab", "about", "q0", "wo0", "up2",
                                   "cin", "cout", "q1", "wo1", "up3"])}
RMS_ENDS = ["down0", "mixout", "down1"]
LN_ENDS = ["about", "wo0", "down2", "cout", "wo1", "down3"]
GAINS = {"about": ("ln_mix", 0), "wo0": ("ln_xa", 0), "down2": ("ln_ffn", 0),
         "cout": ("ln_mix", 1), "wo1": ("ln_xa", 1), "down3": ("ln_ffn", 1)}
NEXT = {"about": "q0", "wo0": "up2", "down2": "cin", "cout": "q1", "wo1": "up3", "down3": None}


def build(nc, a):
    f32, f32r, u32 = mybir.dt.float32, mybir.dt.float32r, mybir.dt.uint32
    ACT, ALU, AX = mybir.ActivationFunctionType, mybir.AluOpType, mybir.AxisListType
    V, S, G = nc.vector, nc.scalar, nc.gpsimd

    ctx = ExitStack()
    with ctx:
        KB = 1024
        BASE = 16512
        slab = ctx.enter_context(nc.sbuf_tensor("slab", [P, 53200], f32))
        made = {}

        def at(name, shape, dt, off):
            made[name] = nc.alloc_sbuf_tensor_at(name, shape, dt, offset=BASE + int(off))
            return made[name]

        x = at("x", [P, KD, T], f32, 0)
        a_hi = at("a_hi", [P, KD, T], f32r, 16 * KB)
        a_lo = at("a_lo", [P, KD, T], f32r, 32 * KB)
        y_ff = at("y_ff", [P, KD, T], f32, 16 * KB)
        raw = at("raw", [P, SLOTS, FULL], f32, 48 * KB)
        w_hi = at("w_hi", [P, SLOTS, FULL], f32r, 64 * KB)
        w_lo = at("w_lo", [P, SLOTS, FULL], f32r, 80 * KB)
        C0 = 96 * KB
        ident = at("ident", [P, P], f32, C0)
        ones = at("ones", [P, P], f32, C0 + 512)
        vec = at("vec", [P, N_VEC], f32, C0 + 1024)
        small = at("small", [P, 16], f32, C0 + 1024 + N_VEC * 4)
        eps6, eps5, one, primed = (small[:, n:n + 1] for n in range(4))
        stat = small[:, 4:16]
        half_g = at("half_g", [P, 24], f32, C0 + 1088 + N_VEC * 4)
        tri = at("tri", [P, 2, P], f32, C0 + 2688)
        A0 = C0 + 4 * KB - 256

        def arena(name, shape, dt, kb):
            return at(name, shape, dt, A0 + kb * KB)

        h_hi = arena("h_hi", [P, KF, T], f32r, 0)
        h_lo = arena("h_lo", [P, KF, T], f32r, 44)
        act_out = arena("act_out", [P, 2, T], f32, 88)
        h32 = arena("h32", [P, 2, T], f32, 92)
        conv_out = arena("conv_out", [P, 2, T], f32, 96)
        acc = arena("acc", [P, 2, 2, T], f32, 88)
        sq = arena("sq", [P, 2, T], f32, 96)
        diag = arena("diag", [P, 2, NT, P], f32, 100)
        nt = arena("nt", [P, 2, T], f32, 104)
        scale = arena("scale", [P, T], f32, 104)
        logf = arena("logf", [P, NT, T], f32, 0)
        kdec = arena("kdec", [P, NT, T], f32, 0)
        k_tm = arena("k_tm", [P, NT, T], f32, 8)
        v_tm = arena("v_tm", [P, NT, T], f32, 16)
        mv_tm = arena("mv_tm", [P, NT, T], f32, 24)
        scores = arena("scores", [P, HEADS, T], f32, 24)
        q_fm = arena("q_fm", [P, HEADS, T], f32, 32)
        hgate = arena("hgate", [P, HEADS, T], f32, 40)
        mgate = arena("mgate", [P, HEADS, T], f32, 48)
        mqk = arena("mqk", [P, HEADS, T], f32, 56)
        q_dec = arena("q_dec", [P, HEADS, T], f32, 64)
        Gc = arena("Gc", [P, HEADS, T], f32, 72)
        k_fm = arena("k_fm", [P, HEADS, T], f32, 80)
        lev = [arena(f"lev{n}", [P, HEADS, T], f32, kb) for n, kb in enumerate((56, 88, 0))]
        states = arena("states", [P, 3, HEADS, P], f32, 8)
        g_end = arena("g_end", [P, HEADS * NT], f32, 14)
        masks = arena("masks", [P, 8, P], u32, 96)
        gbias = arena("gbias", [P, 2], f32, 100)
        ct = arena("ct", [P, 2, NT, HEADS], f32, 100.25)
        mcol = arena("mcol", [P, 4, NT], f32, 100.5)
        hcol = arena("hcol", [P, NT, HEADS], f32, 101)
        mtmp = arena("mtmp", [P, 2, T], f32, 102)
        wg_raw = arena("wg_raw", [P, KD, P], f32, 64)
        wg_hi = arena("wg_hi", [P, KD, P], f32r, 68)
        wg_lo = arena("wg_lo", [P, KD, P], f32r, 72)
        rows = arena("rows", [HEADS, 2, 256 + T], f32, 76)
        row_i = arena("row_i", [HEADS, T], f32, 82)
        row_b = arena("row_b", [HEADS, T], f32, 84)
        row_t = arena("row_t", [HEADS, T], f32, 86)
        row_nm = arena("row_nm", [HEADS, T], f32, 88)
        row_em = arena("row_em", [HEADS, T], f32, 90)
        sel = arena("sel", [HEADS, HEADS, P], f32, 106)
        mp = arena("mp", [P, NT * (T + P)], f32, 64)
        lb = arena("lb", [P, 2, T], f32, 32)
        lbt = arena("lbt", [P, 2, T], f32, 36)
        sigm = arena("sigm", [P, 2, 2, MEM], f32, 94)
        y_mix = arena("y_mix", [P, KD, T], f32, 0)
        gv = arena("gv", [P, NT, T], f32, 0)
        ug = arena("ug", [P, 4, T], f32, 8)
        PAD = 16
        pool = [arena(f"pool{n}", [P, 4, PAD + T], f32, 16 + 8.5 * n) for n in range(3)]
        ab_rows = arena("ab_rows", [P, 3, T], f32, 42)
        ws_t = arena("ws_t", [P, 4, P], f32, 48)
        pool_w = arena("pool_w", [P, 4, P], f32, 50)
        inv_cnt = arena("inv_cnt", [P, 4, PAD], f32, 52)
        bn = arena("bn", [P, NT, 6], f32, 52.5)
        mv4 = arena("mv4", [P, NT, 2], f32, 53)
        rs4 = arena("rs4", [P, NT], f32, 53.5)
        cc = arena("cc", [P, 2, T], f32, 0)
        ch = arena("ch", [P, 2, T], f32, 4)
        yc = arena("yc", [P, KD, T], f32, 8)
        mem_raw = arena("mem_raw", [P, KD, MEM], f32, 56)
        mem_hi = arena("mem_hi", [P, KD, MEM], f32r, 64)
        mem_lo = arena("mem_lo", [P, KD, MEM], f32r, 72)
        k_mem = arena("k_mem", [P, KD, MEM], f32, 80)
        v_mem = arena("v_mem", [P, 2, D], f32, 0)
        q_at = arena("q_at", [P, KD, T], f32, 8)
        pe_at = arena("pe_at", [P, 2, NT, MEM], f32, 24)
        p_t = arena("p_t", [P, 2, 2, T], f32, 32)
        o32 = arena("o32", [P, 2, T], f32, 40)
        at_s = arena("at_s", [P, 2, 3, NT], f32, 44)

        bank = ctx.enter_context(nc.psum_tensor("bank", [P, 8, T], f32))

        def sem(name):
            return ctx.enter_context(nc.semaphore(name))

        w_loaded = [sem("w_loaded0"), sem("w_loaded1")]
        w_hi_done = sem("w_hi_done")
        w_split = sem("w_split")
        gemm_done = sem("gemm_done")
        banks_free = sem("banks_free")
        consts = sem("consts")
        consts_v = sem("consts_v")
        x_in = [sem(f"x_in{k}") for k in range(KD)]
        mix_in = [sem(f"mix_in{n}") for n in range(4)]
        mask_in = sem("mask_in")
        ab_in = [sem(f"ab_in{n}") for n in range(4)]
        mem_in = sem("mem_in")
        out_s = sem("out_s")
        a_hi_done = sem("a_hi_done")
        a_even = sem("a_even")
        a_odd = sem("a_odd")
        sq_read = sem("sq_read")
        scale_col = sem("scale_col")
        scale_bc = sem("scale_bc")
        x_pool = sem("x_pool")
        x_act = sem("x_act")
        x_dve = sem("x_dve")
        norm_t = sem("norm_t")
        gate_done = sem("gate_done")
        conv0 = sem("conv0")
        conv_done = sem("conv_done")
        h_hi_done = sem("h_hi_done")
        h_done = sem("h_done")
        y_copied = sem("y_copied")
        sq_done = sem("sq_done")
        acc_done = sem("acc_done")
        stats = sem("stats")
        stat_a = sem("stat_a")
        stat_v = sem("stat_v")
        dve_link = sem("dve_link")
        act_link = sem("act_link")
        SIG = {n: sem(n) for n in """gate_rows_mm c_columns_mm mlstm_m_mm mlstm_scores_mm mlstm_num_mm mlstm_den_mm cum_decay_mm
            keys_transposed rest_decay_mm state_add_mm level_scores_mm hgrn_out_mm attn_scores_mm probs_transposed
            attn_out_mm spatial_mm pool_mm mlstm_weight mlstm_square mlstm_rms gate_w_hi
            lb_sigmoid mconv_start mqk_ready f_row_log mlstm_v exp_neg_m
            mlstm_gate hgrn_input logf_ready cum_decay keys_fm rest_decay q_decay
            chunk_decay level_exp hgrn_square hgrn_rms sgu_v sgu_u sgu_std
            pool_in mem_hi_done c_gate c_conv_start mem_kv attn_q attn_exp
            probs_t c_columns mlstm_arg mlstm_p mlstm_masked mlstm_y lb_diff
            gate_w_lo mconv_done c_row neg_m_row neg_bm_row forget_ready keys_tm
            keys_decayed level_diff level_ready scores_taken states_ready hgrn_y sgu_stats
            sgu_v_ready ab_ya pooled ab_yb mem_lo_done c_product c_y
            attn_max attn_o32 attn_probs rms_gate rms_up mlstm_scaled mlstm_turned mlstm_ms hgrn_scaled
            hgrn_turned hgrn_ms""".split()}

        def gemm_at(unit, tile=1):
            return 2 * unit + tile + 5

        def free_at(unit):
            return unit + 3

        def place(name, k):
            return (k + HEADS) % KD if name in ("mixout", "about") else k

        def gen_at(name, k=KD - 1):
            return KD * GEN[name] + place(name, k) + 1

        def low_at(name, k):
            return (a_odd if k % 2 else a_even), KD // 2 * GEN[name] + place(name, k) // 2 + 1

        SCORE_AT = {0: (5, 0), 1: (6, 0), 2: (7, 0), 3: (6, 3 * P)}
        SCALED = {"up0": "x0", "up1": "pre_up1"}
        PRE = ["x0", "pre_mixin", "pre_up1"]
        seq = ["x0", "down0", "pre_mixin", "mixout", "pre_up1", "down1"] + LN_ENDS
        SQ0, ACC0, SR0, ST0, SC0 = {}, {}, {}, {}, {}
        c = [0] * 4
        for n, name in enumerate(seq):
            SQ0[name], ACC0[name], SR0[name], SC0[name], ST0[name] = *c, n
            ln, pre = name in LN_ENDS, name in PRE
            steps = 8 if pre or name.startswith("down") else 4
            sums = 0 if pre else 1 + 2 * (steps - 1) * ln + (steps == 4)
            c = [c[0] + steps, c[1] + sums, c[2] + KD * pre, c[3] + (2 if ln else 1)]
        YC0 = {n: KD * i for i, n in enumerate(RMS_ENDS)}
        XPOOL0 = {n: KD // 2 * i for i, n in enumerate(RMS_ENDS)}
        NORM0, c = {}, 0
        for n in ["down0", "mixin", "mixout", "down1"] + [NEXT[e] or "out" for e in LN_ENDS]:
            NORM0[n] = c
            c += KD // 2 if n in RMS_ENDS else KD
        STAT_N = {n: i + 1 for i, n in enumerate(m for m in seq if m not in PRE)}
        XACT0 = {n: KD * i for i, n in enumerate(LN_ENDS)}
        XDVE0 = {n: KD // 2 * i for i, n in enumerate(RMS_ENDS)}

        def x_at(name, k):
            return (x_pool, XPOOL0[name] + k // 2 + 1) if k % 2 else (x_dve, XDVE0[name] + k // 2 + 1)

        def buf(k):
            return nt[:, k % 2, :] if k % 4 < 2 else sq[:, k % 2, :]

        def square_buf(k):
            return sq[:, k % 2, :] if k % 4 < 2 else acc[:, 1, k % 2, :]
        F0 = {f: KF * f for f in range(4)}

        def blocks(t, hs):
            return t[:, :, :].rearrange("p h (n two c) -> p (h n) two c", two=2, c=hs)

        block = ctx.enter_context(nc.Block())

        @block.sync
        def _(sp):
            def stream(phase):
                u0, n, cols, s0 = UNIT0[phase], UNITS[phase], UNIT_COLS[UNIT0[phase]], SOURCE0[phase]
                src = a["w_full"] if cols == FULL else a["w_down"]
                with sp.Fori(0, n // 2) as i:
                    for s in range(SLOTS):
                        sp.wait_ge(w_split, u0 + 2 * i + (s + 1))
                        sp.dma_start(raw[:, s:s + 1, 0:cols],
                                     src[bass.ds(s0 + 2 * i + s, 1), :, :].rearrange("u p c -> p u c")
                                     ).then_inc(w_loaded[s], 16)

            sp.dma_start(vec[:, :], a["vectors"]).then_inc(consts, 16)
            sp.dma_start(ident[:, :], a["identity"]).then_inc(consts, 16)
            sp.dma_start(tri[:, :, :], a["tri"]).then_inc(consts, 16)
            for phase, _, _ in PHASES:
                stream(phase)
            for k in range(KD):
                sp.wait_ge(x_act, XACT0["down3"] + k + 1)
                sp.dma_start(a["out"][:, k, :], x[:, k, :]).then_inc(out_s, 16)
            sp.wait_ge(out_s, 16 * KD)

        @block.gpsimd
        def _(gp):
            def low_odd(gen, src, wait_x=None):
                for k in (5, 7, 1, 3) if gen in ("mixout", "about") else (1, 3, 5, 7):
                    gp.wait_ge(a_hi_done, gen_at(gen, k))
                    if wait_x:
                        gp.wait_ge(*wait_x(k))
                    G.tensor_tensor(a_lo[:, k, :], src(k), a_hi[:, k, :], ALU.subtract).then_inc(a_odd, 1)

            def residual_odd(name, y, gen=None):
                for k in range(1, KD, 2):
                    gp.wait_ge(norm_t, NORM0[name] + k // 2 + 1)
                    G.tensor_tensor(x[:, k, :], x[:, k, :], y[:, k, :], ALU.add).then_inc(x_pool, 1)
                    if gen:
                        gp.wait_ge(a_hi_done, gen_at(gen, k))
                        G.tensor_tensor(a_lo[:, k, :], x[:, k, :], a_hi[:, k, :], ALU.subtract).then_inc(a_odd, 1)

            def x_tile(k):
                return x[:, k, :]

            residual_odd("down0", y_ff)
            low_odd("mixin", buf)
            for l, hs in enumerate(LEVELS):
                if l == 0:
                    gp.wait_ge(SIG["cum_decay"], 1)
                    gp.wait_ge(SIG["keys_decayed"], 1)
                elif l == 2:
                    gp.wait_ge(SIG["state_add_mm"], 1)
                elif l > 2:
                    gp.wait_ge(SIG["level_scores_mm"], l - 1)
                g, d = blocks(Gc, hs), blocks(lev[l % 3], hs)
                mid = g[:, :, 0, hs - 1:hs].broadcast_to([P, HEADS * T // (2 * hs), hs])
                G.tensor_tensor(d[:, :, 1, :], g[:, :, 1, :], mid, ALU.subtract)
                G.tensor_tensor(d[:, :, 0, :], mid, g[:, :, 0, :], ALU.subtract).then_inc(SIG["level_diff"], 1)
            low_odd("mixout", lambda k: hgate[:, k, :] if k < HEADS else mgate[:, k - HEADS, :])
            residual_odd("mixout", y_mix)
            residual_odd("down1", y_ff, "ab")
            low_odd("about", lambda k: ug[:, k, :] if k < 4 else pool[1][:, k - 4, PAD:PAD + T])
            for layer in range(2):
                if layer:
                    low_odd("cout", lambda k: yc[:, k, :])
                for end in (("about", "cout")[layer], f"wo{layer}", f"down{2 + layer}"):
                    if NEXT[end]:
                        low_odd(NEXT[end], x_tile, lambda k: (x_act, XACT0[end] + k + 1))
                    if end[0] in "ac":
                        low_odd(f"wo{layer}", lambda k: o32[:, k % 2, :])

        @block.tensor
        def _(pe):
            mm = nc.tensor.matmul
            PARTS = ((w_hi, a_hi), (w_lo, a_hi), (w_hi, a_lo))

            def first_pair(u0, gen, norm=None):
                def step(kk, s):
                    k = place(gen, kk)
                    if kk == 0:
                        pe.wait_ge(w_split, u0 + s + 3)
                        pe.wait_ge(banks_free, u0 + s + 1)
                    for part, (w, act_in) in enumerate(PARTS):
                        if s == 0 and part == 0:
                            pe.wait_ge(a_hi_done, gen_at(gen, k))
                        if s == 0 and part == 2:
                            pe.wait_ge(*low_at(gen, k))
                        for m in range(2):
                            col = (m * KD + k) * P
                            last = mm(bank[:, 2 * s + m, :], w[:, s, col:col + P], act_in[:, k, :],
                                      start=(kk == 0 and part == 0), stop=(kk == KD - 1 and part == 2))
                            if kk == KD - 1 and part == 2:
                                last.then_inc(gemm_done, 1)
                    if norm and s == 0:
                        square_sum(norm, kk)
                    if norm and s == 1 and kk == KD - 3:
                        broadcast_scales(norm)
                for kk, s in ((0, 0), (1, 0), (0, 1), (1, 1), (2, 0), (2, 1), (3, 0),
                              (4, 0), (5, 0), (6, 0), (7, 0), (3, 1), (4, 1), (5, 1), (6, 1), (7, 1)):
                    step(kk, s)

            def feature_units(phase, wait_gen):
                u0, n = UNIT0[phase], UNITS[phase]
                first_pair(u0, wait_gen, SCALED.get(phase))
                if n > 2:
                    with pe.Fori(1, n // 2) as i:
                        for s in range(SLOTS):
                            pe.wait_ge(w_split, u0 + 2 * i + (s + 3))
                            pe.wait_ge(banks_free, u0 + 2 * i + (s + 1))
                            for m in range(2):
                                for k in range(KD):
                                    for j, (w, act_in) in enumerate(PARTS):
                                        col = (m * KD + k) * P
                                        last = mm(bank[:, 2 * s + m, :], w[:, s, col:col + P], act_in[:, k, :],
                                                  start=(k == 0 and j == 0), stop=(k == KD - 1 and j == 2))
                                last.then_inc(gemm_done, 1)

            def feature_slice(phase, first_unit, n):
                for u in range(first_unit, first_unit + n):
                    s, un = u % 2, UNIT0[phase] + u
                    pe.wait_ge(w_split, un + 3)
                    pe.wait_ge(banks_free, un + 1)
                    for m in range(2):
                        for k in range(KD):
                            for j, (w, act_in) in enumerate(PARTS):
                                col = (m * KD + k) * P
                                last = mm(bank[:, 2 * s + m, :], w[:, s, col:col + P], act_in[:, k, :],
                                          start=(k == 0 and j == 0), stop=(k == KD - 1 and j == 2))
                        last.then_inc(gemm_done, 1)

            def token_pair(u0, gen):
                def step(k, s, m, t):
                    tok = (2 * m + t) * P
                    for j, (w, act_in) in enumerate(PARTS):
                        last = mm(bank[:, 2 * s + m, t * 256:t * 256 + 256],
                                  act_in[:, k, tok:tok + P], w[:, s, k * 256:k * 256 + 256],
                                  start=(k == 0 and j == 0), stop=(k == KD - 1 and j == 2))
                    return last
                for k, s in [(0, 0), (1, 0), (0, 1), (1, 1)] + [(k, s) for k in range(2, KD) for s in range(SLOTS)]:
                    if k == 0:
                        pe.wait_ge(w_split, u0 + s + 3)
                        pe.wait_ge(banks_free, u0 + s + 1)
                    if s == 0:
                        pe.wait_ge(a_hi_done, gen_at(gen, k))
                        pe.wait_ge(*low_at(gen, k))
                    for m in range(2):
                        step(k, s, m, 0)
                for s in range(SLOTS):
                    for m in range(2):
                        for k in range(KD):
                            last = step(k, s, m, 1)
                        last.then_inc(gemm_done, 1)

            def token_slice(phase, first_unit, n):
                for u in range(first_unit, first_unit + n):
                    s, un = u % 2, UNIT0[phase] + u
                    pe.wait_ge(w_split, un + 3)
                    pe.wait_ge(banks_free, un + 1)
                    for m in range(2):
                        for t in range(2):
                            tok = (2 * m + t) * P
                            for k in range(KD):
                                for j, (w, act_in) in enumerate(PARTS):
                                    last = mm(bank[:, 2 * s + m, t * 256:t * 256 + 256],
                                              act_in[:, k, tok:tok + P], w[:, s, k * 256:k * 256 + 256],
                                              start=(k == 0 and j == 0), stop=(k == KD - 1 and j == 2))
                        last.then_inc(gemm_done, 1)

            def down_units(phase, f):
                u0 = UNIT0[phase]
                pe.wait_ge(h_done, F0[f] + HALF_KF)
                with pe.Fori(0, KD // 2) as i:
                    for d in range(2):
                        for s in range(SLOTS):
                            pe.wait_ge(w_split, u0 + 4 * i + (2 * d + s + 3))
                            if s == 0:
                                pe.wait_ge(banks_free, u0 + 4 * i + 2 * d)
                            else:
                                pe.wait_ge(h_done, F0[f] + KF)
                            for k in range(HALF_KF):
                                for j, (w, h) in enumerate(((w_hi, h_hi), (w_hi, h_lo), (w_lo, h_hi))):
                                    last = mm(bank[:, 4 + d, :], w[:, s, k * P:(k + 1) * P],
                                              h[:, s * HALF_KF + k, :],
                                              start=(s == 0 and k == 0 and j == 0),
                                              stop=(s == 1 and k == HALF_KF - 1 and j == 2))
                            last.then_inc(gemm_done, 2)

            def keep_warm(name, n):
                for _ in range(n):
                    mm(bank[:, 0 if name[0] == "d" else 4, 0:P], ident[:, :], ones[:, :], start=True, stop=True)

            def norm_sums(name):
                ln, down = name in LN_ENDS, name[0] == "d"
                end = UNIT0[name] + UNITS[name] - 1
                steps = 8 if down else 4
                whiches = (0, 1) if ln else (1,)

                def column(which, n, src, start=False, stop=False):
                    c0 = which * NT + n
                    return mm(bank[:, 6, c0:c0 + 1], src[:, n * P:(n + 1) * P], ones[:, 0:1],
                              start=start, stop=stop, skip_group_check=True)
                if ln or not down:
                    pe.wait_ge(acc_done, ACC0[name] + 1 + 2 * (steps - 1) * ln + (not down))
                else:
                    pe.wait_ge(banks_free, free_at(end - 2))
                for which in whiches:
                    for n in range(NT):
                        column(which, n, acc[:, which, 0, :], start=which == whiches[0] and n == 0)
                for which in whiches:
                    if which == 0:
                        pe.wait_ge(banks_free, free_at(end))
                    else:
                        pe.wait_ge(sq_done, SQ0[name] + steps)
                    srcs = [x[:, k, :] if which == 0 else sq[:, 0 if down else k % 2, :]
                            for k in range(7 if down else 6, 8)]
                    for src in srcs:
                        for n in range(NT):
                            last = column(which, n, src, stop=src is srcs[-1])
                last.then_inc(stats, 1)
                keep_warm(name, 6)

            def square_sum(name, k):
                pe.wait_ge(sq_done, SQ0[name] + k + 1)
                for n in range(NT):
                    last = mm(bank[:, 7, NT + n:NT + n + 1], square_buf(k)[:, n * P:(n + 1) * P], ones[:, 0:1],
                              start=(k == 0 and n == 0), stop=(k == KD - 1), skip_group_check=True)
                last.then_inc(sq_read, 1)

            def broadcast_scales(name):
                for j in range(2 if name in LN_ENDS else 1):
                    pe.wait_ge(scale_col, SC0[name] + j + 1)
                    mm(bank[:, 7 if name in PRE or j else 6, :], ones[:, :], diag[:, j, :, :],
                       start=True, stop=True).then_inc(scale_bc, 1)
                if name not in PRE:
                    keep_warm(name, 6)

            def mlstm_rows():
                pe.wait_ge(SIG["gate_w_lo"], 1)
                for k in range(KD):
                    for j, (w, act_in) in enumerate(((wg_hi, a_hi), (wg_hi, a_lo), (wg_lo, a_hi))):
                        last = mm(bank[:, 4, :], w[:, k, :], act_in[:, k, :],
                                  start=(k == 0 and j == 0), stop=(k == KD - 1 and j == 2))
                last.then_inc(SIG["gate_rows_mm"], 1)

            def mlstm_columns():
                pe.wait_ge(SIG["c_row"], 1)
                for s in range(NT):
                    nc.tensor.transpose(bank[:, 5, 4 * s:4 * s + 4], row_t[:, s * P:(s + 1) * P],
                                        ident[0:HEADS, 0:HEADS])
                pe.wait_ge(SIG["exp_neg_m"], 1)
                for s in range(NT):
                    last = nc.tensor.transpose(bank[:, 5, 16 + 4 * s:20 + 4 * s], row_em[:, s * P:(s + 1) * P],
                                               ident[0:HEADS, 0:HEADS])
                last.then_inc(SIG["c_columns_mm"], 1)

            def mlstm_scores(h):
                r = 64 * (h % 2)
                q, k = mqk[r:r + 64, h // 2, :], mqk[r:r + 64, 2 + h // 2, :]
                if h == 0:
                    pe.wait_ge(mix_in[2], 16)
                    pe.wait_ge(SIG["neg_m_row"], 1)
                    pe.wait_ge(SIG["mqk_ready"], 4)
                    pe.wait_ge(SIG["c_columns"], 1)
                else:
                    pe.wait_ge(SIG["mlstm_scaled"], h)
                mm(bank[:, 4, :], sel[:, h, :], row_nm[:, :], start=True, stop=True).then_inc(SIG["mlstm_m_mm"], 1)
                for s in (0, 1, 3, 2):
                    if s == 2 and h:
                        pe.wait_ge(SIG["mlstm_y"], h)
                    b, c0 = SCORE_AT[s]
                    mm(bank[:, b, c0:c0 + T - s * P], k[:, s * P:(s + 1) * P], q[:, s * P:T],
                       start=True, stop=True).then_inc(SIG["mlstm_scores_mm"], 1)

            def mlstm_values(h):
                pe.wait_ge(SIG["mlstm_masked"], h + 1)
                if h == 0:
                    pe.wait_ge(SIG["mlstm_v"], 2)
                for n in range(NT):
                    for s in range(n + 1):
                        last = mm(bank[:, 5, n * P:(n + 1) * P], mp[:, s * T + n * P:s * T + (n + 1) * P],
                                  mv_tm[:, s, h * P:(h + 1) * P], start=(s == 0), stop=(s == n))
                last.then_inc(SIG["mlstm_num_mm"], 1)
                for n in range(NT):
                    for s in range(n + 1):
                        last = mm(bank[:, 6, n:n + 1], mp[:, s * T + n * P:s * T + (n + 1) * P], ones[:, 0:1],
                                  start=(s == 0), stop=(s == n))
                last.then_inc(SIG["mlstm_den_mm"], 1)

            def mlstm_turn(h):
                pe.wait_ge(SIG["mlstm_scaled"], h + 1)
                for n in range(NT):
                    last = nc.tensor.transpose(bank[:, 7, n * P:(n + 1) * P], mtmp[:, 0, n * P:(n + 1) * P], ident[:, :])
                last.then_inc(SIG["mlstm_turned"], 1)

            def cum_decays():
                pe.wait_ge(SIG["logf_ready"], 1)
                pe.wait_ge(banks_free, free_at(UNIT0["mixin"] + 11))
                for h in range(HEADS):
                    for n in range(NT):
                        last = mm(bank[:, h, n * P:(n + 1) * P], logf[:, n, h * P:(h + 1) * P], tri[:, 0, :],
                                  start=True, stop=True)
                last.then_inc(SIG["cum_decay_mm"], 1)

            def rest_decays():
                pe.wait_ge(SIG["cum_decay"], 1)
                for n in range(NT):
                    last = mm(bank[:, n, :], tri[:, 1, :], logf[:, n, :], start=True, stop=True)
                last.then_inc(SIG["rest_decay_mm"], 1)

            def level_scores(l):
                if l == 0:
                    pe.wait_ge(SIG["rest_decay"], 1)
                else:
                    pe.wait_ge(SIG["level_ready"], l)
                    if l == 1:
                        pe.wait_ge(SIG["states_ready"], 1)
                    else:
                        pe.wait_ge(SIG["scores_taken"], l)
                for h in range(HEADS):
                    for n in range(NT):
                        c0 = n * P
                        lhs = k_fm if l == 0 else lev[(l - 1) % 3]
                        rhs = q_fm if l == 0 else lev[(l - 1) % 3]
                        last = mm(bank[:, 4 * (l > 0) + h, c0:c0 + P], lhs[:, h, c0:c0 + P],
                                  rhs[:, h, c0:c0 + P], start=True, stop=True)
                last.then_inc(SIG["level_scores_mm"], 1)

            def hgrn_core():
                pe.wait_ge(SIG["keys_tm"], 1)
                pe.wait_ge(SIG["mlstm_y"], HEADS)
                for h in range(HEADS):
                    for n in range(NT):
                        last = nc.tensor.transpose(bank[:, 4 + h, n * P:(n + 1) * P],
                                                   k_tm[:, n, h * P:(h + 1) * P], ident[:, :])
                last.then_inc(SIG["keys_transposed"], 1)
                pe.wait_ge(SIG["keys_decayed"], 1)
                pe.wait_ge(SIG["keys_fm"], 1)
                for n in range(NT - 1):
                    for h in range(HEADS):
                        last = mm(bank[:, 4 + n, h * P:(h + 1) * P], kdec[:, n, h * P:(h + 1) * P],
                                  v_tm[:, n, h * P:(h + 1) * P], start=True, stop=True)
                last.then_inc(SIG["state_add_mm"], 1)
                level_scores(0)
                steps = [(u, m, k) for u in (12, 13) for m in range(2) for k in range(KD)]
                shares = (0, 6, 11, 16, 20, 24, 28, 32)
                for l in range(1, len(LEVELS) + 1):
                    level_scores(l)
                    for u, m, k in steps[shares[l - 1]:shares[l]]:
                        s, un = u % 2, UNIT0["mixin"] + u
                        if m == 0 and k == 0:
                            pe.wait_ge(w_split, un + 3)
                            pe.wait_ge(banks_free, un + 1)
                            pe.wait_ge(SIG["scores_taken"], 1)
                        for j, (w, act_in) in enumerate(PARTS):
                            col = (m * KD + k) * P
                            last = mm(bank[:, 2 * s + m, :], w[:, s, col:col + P], act_in[:, k, :],
                                      start=(k == 0 and j == 0), stop=(k == KD - 1 and j == 2))
                        if k == KD - 1:
                            last.then_inc(gemm_done, 1)
                pe.wait_ge(SIG["scores_taken"], len(LEVELS) + 1)
                for n in range(NT):
                    if n % 2 == 0:
                        pe.wait_ge(banks_free, free_at(UNIT0["mixin"] + 12 + n // 2))
                    for h in range(HEADS):
                        c0 = n * P
                        last = mm(bank[:, n, h * P:(h + 1) * P], scores[:, h, c0:c0 + P],
                                  v_tm[:, n, h * P:(h + 1) * P], start=True, stop=(n == 0))
                        if n:
                            last = mm(bank[:, n, h * P:(h + 1) * P], q_dec[:, h, c0:c0 + P],
                                      states[:, n - 1, h, :], start=False, stop=True)
                    last.then_inc(SIG["hgrn_out_mm"], 1)
                for n in range(NT):
                    pe.wait_ge(SIG["hgrn_scaled"], n + 1)
                    for h in range(HEADS):
                        last = nc.tensor.transpose(bank[:, 4 + h, n * P:(n + 1) * P],
                                                   lev[0][:, n, h * P:(h + 1) * P], ident[:, :])
                last.then_inc(SIG["hgrn_turned"], 1)

            def memory_unit(phase, u):
                s, un = u % 2, UNIT0[phase] + u
                layer = int(phase[-1])
                if u == 0:
                    pe.wait_ge(SIG["mem_lo_done"], layer + 1)
                pe.wait_ge(w_split, un + 3)
                pe.wait_ge(banks_free, un + 1)
                for m in range(2):
                    for k in range(KD):
                        for j, (w, src) in enumerate(((w_hi, mem_hi), (w_hi, mem_lo), (w_lo, mem_hi))):
                            if u < 4:
                                col = (m * KD + k) * P
                                ops = (w[:, s, col:col + P], src[:, k, :])
                            else:
                                ops = (src[:, k, m * P:(m + 1) * P], w[:, s, k * 256:k * 256 + 256])
                            last = mm(bank[:, 2 * s + m, 0:MEM], *ops,
                                      start=(k == 0 and j == 0), stop=(k == KD - 1 and j == 2))
                    last.then_inc(gemm_done, 1)

            def attention(layer):
                pe.wait_ge(banks_free, free_at(UNIT0[f"q{layer}"] + 3))

                def scores(h):
                    b = 2 * (h % 2)
                    if h >= 2:
                        pe.wait_ge(SIG["attn_probs"], 4 * layer + h - 2 + 1)
                    for t in range(NT):
                        for d in range(2):
                            last = mm(bank[:, b + t // 2, (t % 2) * MEM:(t % 2) * MEM + MEM],
                                      q_at[:, 2 * h + d, t * P:(t + 1) * P], k_mem[:, 2 * h + d, :],
                                      start=(d == 0), stop=(d == 1))
                    last.then_inc(SIG["attn_scores_mm"], 1)
                scores(0)
                scores(1)
                for g in range(HEADS):
                    pe.wait_ge(SIG["attn_probs"], 4 * layer + g + 1)
                    if g:
                        pe.wait_ge(SIG["probs_t"], 4 * layer + g)
                    for m in range(2):
                        for t in range(NT):
                            last = nc.tensor.transpose(bank[:, 4 + m, t * P:(t + 1) * P],
                                                       pe_at[:, g % 2, t, m * P:(m + 1) * P], ident[:, :])
                    last.then_inc(SIG["probs_transposed"], 1)
                    if g + 2 < HEADS:
                        scores(g + 2)
                    pe.wait_ge(SIG["probs_t"], 4 * layer + g + 1)
                    if g:
                        pe.wait_ge(SIG["attn_o32"], 4 * layer + g)
                    for d in range(2):
                        for m in range(2):
                            last = mm(bank[:, 6 + d, :], v_mem[:, m, (2 * g + d) * P:(2 * g + d + 1) * P],
                                      p_t[:, g % 2, m, :], start=(m == 0), stop=(m == 1))
                    last.then_inc(SIG["attn_out_mm"], 1)

            def ab_pool():
                for g in range(4):
                    pe.wait_ge(SIG["pooled"], g + 1)
                    mm(bank[:, 4 + g, :], pool_w[:, g, :], pool[2][:, g, PAD:PAD + T],
                       start=True, stop=True).then_inc(SIG["pool_mm"], 1)

            def ab_spatial():
                pe.wait_ge(SIG["sgu_v_ready"], 1)
                pe.wait_ge(SIG["ab_yb"], 4)
                for g in range(4):
                    for n in range(NT):
                        last = mm(bank[:, 4 + g, n * P:(n + 1) * P], gv[:, n, g * P:(g + 1) * P],
                                  ws_t[:, g, :], start=True, stop=True)
                    last.then_inc(SIG["spatial_mm"], 1)

            pe.wait_ge(consts_v, 1)
            pe.wait_ge(consts, 48)
            keep_warm("down0", 20)
            feature_units("up0", "up0")
            down_units("down0", 0)
            norm_sums("down0")
            broadcast_scales("down0")
            for k in range(KD):
                keep_warm("down0", 1)
                square_sum("pre_mixin", k)
            broadcast_scales("pre_mixin")
            first_pair(UNIT0["mixin"], "mixin")
            mlstm_rows()
            token_slice("mixin", 2, 2)
            feature_slice("mixin", 4, 2)
            mlstm_columns()
            for h in range(HEADS):
                unit = token_slice if h < 2 else feature_slice
                if h < 3:
                    unit("mixin", 6 + 2 * h, 1)
                if h:
                    mlstm_turn(h - 1)
                mlstm_scores(h)
                if h < 3:
                    unit("mixin", 7 + 2 * h, 1)
                else:
                    cum_decays()
                mlstm_values(h)
            rest_decays()
            mlstm_turn(HEADS - 1)
            hgrn_core()
            feature_units("mixout", "mixout")
            norm_sums("mixout")
            broadcast_scales("mixout")
            feature_units("up1", "up1")
            down_units("down1", 1)
            norm_sums("down1")
            broadcast_scales("down1")
            token_pair(UNIT0["ab"], "ab")
            feature_slice("ab", 2, 3)
            ab_pool()
            feature_slice("ab", 5, 1)
            ab_spatial()
            feature_units("about", "about")
            for layer in range(2):
                memory_unit(f"kv{layer}", 0)
                norm_sums(("about", "cout")[layer])
                memory_unit(f"kv{layer}", 1)
                broadcast_scales(("about", "cout")[layer])
                for u in range(2, 8):
                    memory_unit(f"kv{layer}", u)
                feature_units(f"q{layer}", f"q{layer}")
                attention(layer)
                feature_units(f"wo{layer}", f"wo{layer}")
                norm_sums(f"wo{layer}")
                broadcast_scales(f"wo{layer}")
                feature_units(f"up{2 + layer}", f"up{2 + layer}")
                down_units(f"down{2 + layer}", 2 + layer)
                norm_sums(f"down{2 + layer}")
                broadcast_scales(f"down{2 + layer}")
                if layer == 0:
                    feature_units("cin", "cin")
                    feature_units("cout", "cout")

        @block.scalar
        def _(act):
            links = [0]

            def link(ins):
                links[0] += 1
                ins.then_inc(act_link, 1)
                act.wait_ge(act_link, links[0])

            def split(unit, s, cols):
                half = unit // 2 if isinstance(unit, int) else None
                act.wait_ge(w_loaded[s], 16 * (half + 1))
                act.wait_ge(gemm_done, 2 * unit + 2)
                S.activation(w_hi[:, s, 0:cols], raw[:, s, 0:cols], ACT.Copy).then_inc(w_hi_done, 1)

            def split_in(pair0, i, s, cols):
                act.wait_ge(w_loaded[s], 16 * (pair0 + i) + 16)
                act.wait_ge(gemm_done, 4 * (pair0 + i) + (2 * s + 2))
                S.activation(w_hi[:, s, 0:cols], raw[:, s, 0:cols], ACT.Copy).then_inc(w_hi_done, 1)

            split_early = set()

            def split_ahead(phase):
                split_next(UNIT0[phase])
                split_early.add(UNIT0[phase] + 1)

            def split_next(unit):
                if unit + 1 < N_UNITS and unit + 1 not in split_early:
                    split(unit + 1, (unit + 1) % 2, UNIT_COLS[unit + 1])

            def pairs(phase, post, per_pair=2):
                u0, n, cols = UNIT0[phase], UNITS[phase], UNIT_COLS[UNIT0[phase]]
                trips = n // per_pair
                split_next(u0)
                if trips > 1:
                    with act.Fori(0, trips - 1) as i:
                        for j in range(per_pair):
                            split_in((u0 + j + 2) // 2, i * (per_pair // 2), j % 2, cols)
                            post(i, j)
                for j in range(per_pair):
                    if j < per_pair - 1:
                        split_next(u0 + n - per_pair + j + 1)
                    post(trips - 1, j)

            def up(f):
                conv = f >= 2
                u0, n0 = UNIT0[f"up{f}"], F0[f]
                vc = VCOL["ffn_conv_w_2"] + 3 * KF * (f - 2)
                vb = VCOL["ffn_conv_b_2"] + KF * (f - 2)

                def post(i, s):
                    if conv:
                        act.wait_ge(gemm_done, 2 * u0 + 4 * i + (2 * s + 5))
                        n = 2 * i + s
                        S.activation(conv_out[:, s, :], bank[:, 2 * s, :], ACT.Identity,
                                     scale=vec[:, bass.ds(vc + 2 * KF + n, 1)],
                                     bias=vec[:, bass.ds(vb + n, 1)]).then_inc(conv0, 1)
                        act.wait_ge(conv_done, 2 * (n0 - F0[2]) + 4 * i + (2 * s + 2))
                        S.activation(act_out[:, s, :], conv_out[:, s, :],
                                     ACT.Gelu_apprx_tanh).then_inc(gate_done, 1)
                    else:
                        act.wait_ge(SIG["rms_gate"], n0 + 2 * i + (s + 1))
                        S.activation(act_out[:, s, :], conv_out[:, s, :], ACT.Silu).then_inc(gate_done, 1)
                    if conv:
                        act.wait_ge(banks_free, u0 + 2 * i + (s + 3))
                    else:
                        act.wait_ge(SIG["rms_up"], 2 * n0 + 4 * i + (2 * s + 2))
                    S.activation(h_hi[:, bass.ds(2 * i + s, 1), :], h32[:, s:s + 1, :],
                                 ACT.Copy).then_inc(h_hi_done, 1)
                pairs(f"up{f}", post)

            def end_rms(phase, y, gains):
                u0, down = UNIT0[phase], phase[0] == "d"

                def post(i, j):
                    if down and j % 2 == 0:
                        return
                    n = 2 * i + (j // 2 if down else j)
                    act.wait_ge(gemm_done, 2 * u0 + (8 if down else 4) * i + (2 * j + 6))
                    if down:
                        src, dst, sqd = bank[:, 4 + j // 2:5 + j // 2, :], y[:, bass.ds(n, 1), :], sq[:, 0:1, :]
                    else:
                        src, dst, sqd = bank[:, 2 * j:2 * j + 2, :], y[:, bass.ds(2 * n, 2), :], sq[:, :, :]
                    act.wait_ge(banks_free, u0 + (4 * i + 2 * (j // 2) if down else 2 * i + j) + 2)
                    S.activation(sqd, src, ACT.Square).then_inc(sq_done, 1)
                    for m in range(1 if down else 2):
                        S.activation(dst[:, m:m + 1, :], src[:, m:m + 1, :], ACT.Copy,
                                     scale=gains[:, bass.ds(n if down else 2 * n + m, 1)]).then_inc(y_copied, 1)
                pairs(phase, post, 4 if down else 2)

            def end_ln(phase):
                u0, down = UNIT0[phase], phase[0] == "d"

                def post(i, j):
                    if down and j % 2 == 0:
                        return
                    n = 2 * i + (j // 2 if down else j)
                    act.wait_ge(banks_free, u0 + (4 if down else 2) * i + (j + 3))
                    act.wait_ge(acc_done, ACC0[phase] + 2 * n + 1)
                    if down:
                        S.activation(sq[:, 0:1, :], x[:, bass.ds(n, 1), :], ACT.Square).then_inc(sq_done, 1)
                    else:
                        S.activation(sq[:, :, :], x[:, bass.ds(2 * n, 2), :], ACT.Square).then_inc(sq_done, 1)
                pairs(phase, post, 4 if down else 2)

            def root(name):
                if name in PRE:
                    act.wait_ge(sq_read, SR0[name] + KD)
                else:
                    act.wait_ge(stats, STAT_N[name])
                b = 7 if name in PRE else 6
                S.activation(stat[:, 8:12], bank[:, b, NT:2 * NT], ACT.Sqrt, scale=1.0 / D, bias=eps6
                             ).then_inc(stat_a, 1)

            def ln_root(name):
                act.wait_ge(stat_v, LN_ENDS.index(name) + 1)
                S.activation(stat[:, 8:12], stat[:, 8:12], ACT.Sqrt, bias=eps5).then_inc(stat_a, 1)

            def ln_tile(name, k):
                which, layer = GAINS[name]
                g0, b0 = VCOL[which + "_g_2"] + 8 * layer + k, VCOL[which + "_b_2"] + 8 * layer + k
                nxt = NEXT[name]
                act.wait_ge(norm_t, NORM0[nxt or "out"] + k + 1)
                if nxt:
                    S.activation(a_hi[:, k, :], buf(k), ACT.Identity, scale=vec[:, g0:g0 + 1],
                                 bias=vec[:, b0:b0 + 1]).then_inc(a_hi_done, 1)
                S.activation(x[:, k, :], buf(k), ACT.Identity, scale=vec[:, g0:g0 + 1],
                             bias=vec[:, b0:b0 + 1]).then_inc(x_act, 1)

            def squares_of_x(name, ready):
                for k in range(KD):
                    act.wait_ge(*ready(k))
                    if k >= 4:
                        act.wait_ge(sq_read, SR0[name] + k - 3)
                    S.activation(square_buf(k), x[:, k, :], ACT.Square).then_inc(sq_done, 1)

            def scaled_input(gen, name, ready, g0):
                for k in range(KD):
                    if k == 2 and gen == "up0":
                        split_ahead(gen)
                    act.wait_ge(*ready(k))
                    S.activation(a_hi[:, k, :], x[:, k, :], ACT.Copy, scale=vec[:, g0 + k:g0 + k + 1]
                                 ).then_inc(a_hi_done, 1)
                    if k >= 4:
                        act.wait_ge(sq_read, SR0[name] + k - 3)
                    S.activation(square_buf(k), x[:, k, :], ACT.Square).then_inc(sq_done, 1)

            def normalised(gen):
                for k in range(KD):
                    act.wait_ge(norm_t, NORM0[gen] + k + 1)
                    S.activation(a_hi[:, k, :], buf(k), ACT.Copy).then_inc(a_hi_done, 1)

            def mlstm_weights(h):
                for s in range(NT):
                    act.wait_ge(SIG["mlstm_arg"], 4 * h + s + 1)
                    S.activation(mp[:, s * T + s * P:(s + 1) * T], mp[:, s * T + s * P:(s + 1) * T],
                                 ACT.Exp).then_inc(SIG["mlstm_weight"], 1)

            def mlstm_squares(h):
                act.wait_ge(SIG["mlstm_num_mm"], h + 1)
                for n in range(NT):
                    S.activation(mtmp[:, 1, n * P:(n + 1) * P], bank[:, 5, n * P:(n + 1) * P], ACT.Square,
                                 accum_out=mcol[:, 0, n:n + 1]).then_inc(SIG["mlstm_square"], 1)

            def mlstm_root(h):
                act.wait_ge(SIG["mlstm_ms"], h + 1)
                S.activation(mcol[:, 1, :], mcol[:, 1, :], ACT.Sqrt, scale=1.0 / P,
                             bias=eps6).then_inc(SIG["mlstm_rms"], 1)

            act.wait_ge(consts_v, 1)
            for k in range(KD):
                act.dma_start(x[:, k, :], a["x"][:, k, :]).then_inc(x_in[k], 16)
            split(0, 0, FULL)
            scaled_input("up0", "x0", lambda k: (x_in[k], 16), VCOL["norm_pre"])
            root("x0")
            up(0)
            end_rms("down0", y_ff, half_g[:, 0:8])
            root("down0")
            split_ahead("mixin")
            for n, (dst, src) in enumerate([(wg_raw[:, :, :], a["w_gates"]), (lbt[:, :, :], a["lb_rows"])]):
                act.dma_start(dst, src).then_inc(mix_in[n], 16)
            squares_of_x("pre_mixin", lambda k: x_at("down0", k))
            root("pre_mixin")
            normalised("mixin")

            act.wait_ge(*low_at("mixin", KD - 2))
            act.wait_ge(*low_at("mixin", KD - 1))
            act.dma_start(gbias[0:HEADS, :], a["gate_bias"]).then_inc(mix_in[3], 16)
            act.dma_start(sel[:, :, :], a["sel"]).then_inc(mix_in[2], 16)
            mi = UNIT0["mixin"]
            act.wait_ge(mix_in[0], 16)
            S.activation(wg_hi[:, :, :], wg_raw[:, :, :], ACT.Copy).then_inc(SIG["gate_w_hi"], 1)
            act.wait_ge(SIG["lb_diff"], 1)
            S.activation(lb[:, :, :], lb[:, :, :], ACT.Sigmoid).then_inc(SIG["lb_sigmoid"], 1)
            for u in range(2):
                split_next(mi + u)
                for m in range(2):
                    t = 2 * u + m
                    act.wait_ge(gemm_done, gemm_at(mi + u, m))
                    S.activation(mqk[:, t, :], bank[:, 2 * u + m, :], ACT.Identity,
                                 scale=vec[:, VCOL["conv_w"] + 12 + t:VCOL["conv_w"] + 13 + t],
                                 bias=vec[:, VCOL["conv_b"] + t:VCOL["conv_b"] + t + 1]).then_inc(SIG["mconv_start"], 1)
            for t in range(4):
                act.wait_ge(SIG["mconv_done"], t + 1)
                S.activation(mqk[:, t, :], mqk[:, t, :], ACT.Silu).then_inc(SIG["mqk_ready"], 1)
            act.wait_ge(mix_in[3], 16)
            act.wait_ge(SIG["gate_rows_mm"], 1)
            link(S.activation(row_i[:, :], bank[0:HEADS, 4, :], ACT.Identity, bias=gbias[0:HEADS, 0:1]))
            link(S.activation(row_b[:, :], bank[32:32 + HEADS, 4, :], ACT.Identity, bias=gbias[0:HEADS, 1:2]))
            link(S.activation(row_t[:, :], row_b[:, :], ACT.Abs))
            link(S.activation(row_t[:, :], row_t[:, :], ACT.Exp, scale=-1.0))
            S.activation(row_t[:, :], row_t[:, :], ACT.Ln, bias=one[0:HEADS, :]).then_inc(SIG["f_row_log"], 1)
            for u in (2, 3):
                split_next(mi + u)
                act.wait_ge(gemm_done, gemm_at(mi + u))
                S.activation(mv_tm[:, :, (u - 2) * 256:(u - 1) * 256],
                             bank[:, 2 * (u % 2):2 * (u % 2) + 2, :].rearrange("p b (t c) -> p (b t) c", t=2),
                             ACT.Copy).then_inc(SIG["mlstm_v"], 1)
            act.wait_ge(SIG["neg_bm_row"], 1)
            S.activation(row_em[:, :], row_em[:, :], ACT.Exp).then_inc(SIG["exp_neg_m"], 1)
            for u in (4, 5):
                split_next(mi + u)
                act.wait_ge(gemm_done, gemm_at(mi + u))
                S.activation(mgate[:, 2 * (u - 4):2 * (u - 4) + 2, :], bank[:, 2 * (u % 2):2 * (u % 2) + 2, :],
                             ACT.Sigmoid).then_inc(SIG["mlstm_gate"], 1)
            for h in range(3):
                for j in range(2):
                    u = 6 + 2 * h + j
                    b = 2 * (u % 2)
                    split_next(mi + u)
                    act.wait_ge(gemm_done, gemm_at(mi + u))
                    four = bank[:, b:b + 2, :].rearrange("p b (t c) -> p (b t) c", t=2)
                    if h == 0:
                        if j == 1:
                            act.wait_ge(SIG["forget_ready"], 1)
                        S.activation(sigm[:, :, :, :].rearrange("p a t c -> p (a t) c"), four,
                                     ACT.Sigmoid).then_inc(SIG["hgrn_input"], 1)
                    elif h == 1:
                        S.activation(v_tm[:, :, j * 256:(j + 1) * 256], four, ACT.Copy).then_inc(SIG["hgrn_input"], 1)
                    else:
                        S.activation(q_fm[:, 2 * j:2 * j + 2, :], bank[:, b:b + 2, :], ACT.Silu).then_inc(SIG["hgrn_input"], 1)
                    if j == 0:
                        mlstm_weights(h)
                    else:
                        mlstm_squares(h)
                        mlstm_root(h)
                if h == 0:
                    act.wait_ge(SIG["keys_tm"], 1)
                    S.activation(logf[:, :, :], logf[:, :, :], ACT.Ln).then_inc(SIG["logf_ready"], 1)
            mlstm_weights(3)
            act.dma_start(masks[:, :, :], a["masks"]).then_inc(mask_in, 16)
            split_next(mi + 12)
            act.wait_ge(SIG["cum_decay_mm"], 1)
            act.wait_ge(SIG["mlstm_den_mm"], HEADS)
            S.activation(Gc[:, :, :], bank[:, 0:4, :], ACT.Copy).then_inc(SIG["cum_decay"], 1)
            mlstm_squares(3)
            mlstm_root(3)
            act.wait_ge(SIG["rest_decay_mm"], 1)
            S.activation(lev[0][:, :, :], bank[:, 0:4, :], ACT.Exp).then_inc(SIG["rest_decay"], 1)
            S.activation(q_dec[:, :, :], Gc[:, :, :], ACT.Exp).then_inc(SIG["q_decay"], 1)
            act.wait_ge(SIG["keys_transposed"], 1)
            S.activation(k_fm[:, :, :], bank[:, 4:8, :], ACT.Copy).then_inc(SIG["keys_fm"], 1)
            act.wait_ge(SIG["keys_decayed"], 1)
            S.activation(g_end[:, :], Gc[:, :, :].rearrange("p h (n c) -> p (h n) c", c=CHUNK)[:, :, CHUNK - 1],
                         ACT.Exp).then_inc(SIG["chunk_decay"], 1)
            for l in range(len(LEVELS)):
                act.wait_ge(SIG["level_diff"], l + 1)
                S.activation(lev[l % 3][:, :, :], lev[l % 3][:, :, :], ACT.Exp).then_inc(SIG["level_exp"], 1)
                if l in (4, 6):
                    j = (l - 4) // 2
                    act.wait_ge(gemm_done, gemm_at(mi + 12 + j))
                    S.activation(hgate[:, 2 * j:2 * j + 2, :], bank[:, 2 * j:2 * j + 2, :],
                                 ACT.Silu).then_inc(SIG["hgrn_input"], 1)
                    split_next(mi + 13 + j)
            split_early.add(UNIT0["mixout"] + 1)
            for h in range(HEADS):
                if h == HEADS - 1:
                    S.activation(primed, one, ACT.Sqrt)
                act.wait_ge(SIG["hgrn_out_mm"], h + 1)
                S.activation(lev[1][:, h, :], bank[:, h, :], ACT.Square).then_inc(SIG["hgrn_square"], 1)
            act.wait_ge(SIG["hgrn_ms"], 1)
            S.activation(hcol[:, :, :], hcol[:, :, :], ACT.Sqrt, scale=1.0 / P, bias=eps6).then_inc(SIG["hgrn_rms"], 1)
            for k in range(HEADS, KD):
                S.activation(a_hi[:, k, :], mgate[:, k - HEADS, :], ACT.Copy).then_inc(a_hi_done, 1)
            for k in range(HEADS):
                act.wait_ge(SIG["hgrn_y"], k + 1)
                S.activation(a_hi[:, k, :], hgate[:, k, :], ACT.Copy).then_inc(a_hi_done, 1)
            end_rms("mixout", y_mix, vec[:, VCOL["norm_post"] + 8:VCOL["norm_post"] + 16])
            root("mixout")
            split_ahead("up1")
            scaled_input("up1", "pre_up1", lambda k: x_at("mixout", k), VCOL["norm_pre"] + 16)
            root("pre_up1")
            up(1)
            end_rms("down1", y_ff, half_g[:, 16:24])
            root("down1")
            split_ahead("ab")
            for n, (dst, src) in enumerate([(ab_rows[:, :, :], a["ab_rows"]), (ws_t[:, :, :], a["ws_t"]),
                                            (pool_w[:, :, :], a["pool_w"]), (inv_cnt[:, :, :], a["inv_cnt"])]):
                act.dma_start(dst, src).then_inc(ab_in[n], 16)
            act.dma_start(mem_raw[:, :, :], a["mem"]).then_inc(mem_in, 16)
            for k in range(KD):
                act.wait_ge(*x_at("down1", k))
                S.activation(a_hi[:, k, :], x[:, k, :], ACT.Copy).then_inc(a_hi_done, 1)

            ab = UNIT0["ab"]
            for u in range(2):
                split_next(ab + u)
                act.wait_ge(gemm_done, gemm_at(ab + u))
                S.activation(gv[:, :, u * 256:(u + 1) * 256],
                             bank[:, 2 * u:2 * u + 2, :].rearrange("p b (t c) -> p (b t) c", t=2),
                             ACT.Gelu_apprx_tanh).then_inc(SIG["sgu_v"], 1)
            for u in (2, 3):
                split_next(ab + u)
                act.wait_ge(gemm_done, gemm_at(ab + u))
                S.activation(pool[0][:, 2 * (u - 2):2 * (u - 2) + 2, PAD:PAD + T],
                             bank[:, 2 * (u % 2):2 * (u % 2) + 2, :], ACT.Copy).then_inc(SIG["pool_in"], 1)
                if u == 2:
                    act.wait_ge(SIG["sgu_stats"], 4)
                    S.activation(rs4[:, :], mv4[:, :, 1], ACT.Sqrt, bias=eps5).then_inc(SIG["sgu_std"], 1)
            act.wait_ge(mem_in, 16)
            S.activation(mem_hi[:, :, :], mem_raw[:, :, :], ACT.Copy).then_inc(SIG["mem_hi_done"], 1)
            for u in (4, 5):
                split_next(ab + u)
                act.wait_ge(gemm_done, gemm_at(ab + u))
                S.activation(ug[:, 2 * (u - 4):2 * (u - 4) + 2, :], bank[:, 2 * (u % 2):2 * (u % 2) + 2, :],
                             ACT.Gelu_apprx_tanh).then_inc(SIG["sgu_u"], 1)
            for k in (4, 5, 6, 7, 0, 1, 2, 3):
                if k == 6:
                    split_ahead("about")
                act.wait_ge(*((SIG["ab_ya"], k + 1) if k < 4 else (SIG["ab_yb"], k - 3)))
                src = ug[:, k, :] if k < 4 else pool[1][:, k - 4, PAD:PAD + T]
                S.activation(a_hi[:, k, :], src, ACT.Copy).then_inc(a_hi_done, 1)
            for layer in range(2):
                if layer == 1:
                    ci = UNIT0["cin"]
                    cw = VCOL["c_conv_w_2"]
                    act.dma_start(mem_raw[:, :, :], a["mem"]).then_inc(mem_in, 16)
                    act.wait_ge(mem_in, 32)
                    S.activation(mem_hi[:, :, :], mem_raw[:, :, :], ACT.Copy).then_inc(SIG["mem_hi_done"], 1)
                    for u in range(12):
                        split_next(ci + u)
                        if 1 <= u <= 8:
                            act.wait_ge(SIG["c_product"], u)
                            S.activation(yc[:, u - 1, :], ch[:, (u - 1) % 2, :], ACT.Copy,
                                         scale=vec[:, cw + 15 + u:cw + 16 + u]).then_inc(SIG["c_conv_start"], 1)
                        if u < 8:
                            b = 2 * (u % 2)
                            act.wait_ge(gemm_done, gemm_at(ci + u, 0))
                            if u >= 2:
                                act.wait_ge(SIG["c_product"], u - 2 + 1)
                            S.activation(cc[:, u % 2, :], bank[:, b, :], ACT.Copy).then_inc(SIG["c_gate"], 1)
                    split_ahead("cout")
                    for k in range(KD):
                        act.wait_ge(SIG["c_y"], 4)
                        S.activation(a_hi[:, k, :], yc[:, k, :], ACT.Copy).then_inc(a_hi_done, 1)
                end = ("about", "cout")[layer]
                end_ln(end)
                kv = UNIT0[f"kv{layer}"]
                split_ahead(f"kv{layer}")

                def mem_out(u):
                    act.wait_ge(gemm_done, gemm_at(kv + u))
                    dst = k_mem[:, 2 * u:2 * u + 2, :] if u < 4 else v_mem[:, :, (u - 4) * 256:(u - 3) * 256]
                    S.activation(dst, bank[:, 2 * (u % 2):2 * (u % 2) + 2, 0:MEM], ACT.Copy).then_inc(SIG["mem_kv"], 1)
                mem_out(0)
                split_next(kv + 1)
                ln_root(end)
                ln_tile(end, 0)
                for k in range(1, KD):
                    mem_out(k)
                    if k < KD - 1:
                        split_next(kv + k + 1)
                    else:
                        split_ahead(f"q{layer}")
                    ln_tile(end, k)
                q0 = UNIT0[f"q{layer}"]
                for u in range(4):
                    split_next(q0 + u)
                    act.wait_ge(gemm_done, gemm_at(q0 + u))
                    S.activation(q_at[:, 2 * u:2 * u + 2, :], bank[:, 2 * (u % 2):2 * (u % 2) + 2, :],
                                 ACT.Copy).then_inc(SIG["attn_q"], 1)
                split_ahead(f"wo{layer}")
                scale = 256.0 ** -0.5

                def exps(h):
                    act.wait_ge(SIG["attn_max"], 4 * layer + h + 1)
                    if h >= 2:
                        act.wait_ge(SIG["probs_transposed"], 4 * layer + h - 1)
                    for t in range(NT):
                        S.activation(pe_at[:, h % 2, t, :],
                                     bank[:, 2 * (h % 2) + t // 2, (t % 2) * MEM:(t % 2) * MEM + MEM],
                                     ACT.Exp, scale=scale, bias=at_s[:, h % 2, 1, t:t + 1],
                                     accum_out=at_s[:, h % 2, 2, t:t + 1]).then_inc(SIG["attn_exp"], 1)

                def transposed(g):
                    act.wait_ge(SIG["probs_transposed"], 4 * layer + g + 1)
                    S.activation(p_t[:, g % 2, :, :], bank[:, 4:6, :], ACT.Copy).then_inc(SIG["probs_t"], 1)
                exps(0)
                exps(1)
                transposed(0)
                for g in range(HEADS):
                    if g + 2 < HEADS:
                        exps(g + 2)
                    if g + 1 < HEADS:
                        transposed(g + 1)
                    act.wait_ge(SIG["attn_o32"], 4 * layer + g + 1)
                    for d in range(2):
                        S.activation(a_hi[:, 2 * g + d, :], o32[:, d, :], ACT.Copy).then_inc(a_hi_done, 1)
                end = f"wo{layer}"
                end_ln(end)
                if NEXT[end]:
                    split_ahead(NEXT[end])
                ln_root(end)
                for k in range(KD):
                    ln_tile(end, k)
                up(2 + layer)
                end = f"down{2 + layer}"
                end_ln(end)
                if NEXT[end]:
                    split_ahead(NEXT[end])
                ln_root(end)
                for k in range(KD):
                    ln_tile(end, k)

        @block.vector
        def _(dve):
            links = [0]

            def link(ins):
                links[0] += 1
                ins.then_inc(dve_link, 1)
                dve.wait_ge(dve_link, links[0])

            def split(unit, s, cols):
                dve.wait_ge(w_hi_done, unit + 1)
                V.tensor_tensor(w_lo[:, s, 0:cols], raw[:, s, 0:cols], w_hi[:, s, 0:cols],
                                ALU.subtract).then_inc(w_split, 1)

            split_early = set()

            def split_ahead(phase):
                split_next(UNIT0[phase])
                split_early.add(UNIT0[phase] + 1)

            def split_next(unit):
                if unit + 1 < N_UNITS and unit + 1 not in split_early:
                    split(unit + 1, (unit + 1) % 2, UNIT_COLS[unit + 1])

            def pairs(phase, post, per_pair=2):
                u0, n, cols = UNIT0[phase], UNITS[phase], UNIT_COLS[UNIT0[phase]]
                trips = n // per_pair
                split_next(u0)
                if trips > 1:
                    with dve.Fori(0, trips - 1) as i:
                        for j in range(per_pair):
                            split(u0 + per_pair * i + (j + 2), j % 2, cols)
                            post(i, j)
                for j in range(per_pair):
                    if j < per_pair - 1:
                        split_next(u0 + n - per_pair + j + 1)
                    post(trips - 1, j)

            def up(f):
                conv = f >= 2
                u0, n0 = UNIT0[f"up{f}"], F0[f]
                vc = VCOL["ffn_conv_w_2"] + 3 * KF * (f - 2)

                def post(i, s):
                    n = 2 * i + s
                    if conv:
                        c0 = 2 * (n0 - F0[2]) + 4 * i + 2 * s
                        dve.wait_ge(conv0, (n0 - F0[2]) + n + 1)
                        for tap in (1, 2):
                            V.scalar_tensor_tensor(conv_out[:, s, tap:T], bank[:, 2 * s, 0:T - tap],
                                                   vec[:, bass.ds(vc + (2 - tap) * KF + n, 1)],
                                                   conv_out[:, s, tap:T], ALU.mult, ALU.add).then_inc(conv_done, 1)
                            if tap == 1:
                                dve.wait_ge(conv_done, c0 + 1)
                    if conv:
                        dve.wait_ge(gate_done, n0 + n + 1)
                        dve.wait_ge(gemm_done, 2 * u0 + 4 * i + (2 * s + 6))
                        V.tensor_tensor(h32[:, s, :], act_out[:, s, :], bank[:, 2 * s + 1, :],
                                        ALU.mult).then_inc(banks_free, 1)
                    else:
                        dve.wait_ge(gemm_done, 2 * u0 + 4 * i + (2 * s + 5))
                        V.tensor_tensor(conv_out[:, s, :], bank[:, 2 * s, :], scale[:, :],
                                        ALU.mult).then_inc(SIG["rms_gate"], 1)
                        dve.wait_ge(gemm_done, 2 * u0 + 4 * i + (2 * s + 6))
                        V.tensor_tensor(h32[:, s, :], bank[:, 2 * s + 1, :], scale[:, :],
                                        ALU.mult).then_inc(SIG["rms_up"], 1)
                        dve.wait_ge(SIG["rms_gate"], n0 + n + 1)
                        dve.wait_ge(SIG["rms_up"], 2 * (n0 + n) + 1)
                        dve.sem_inc(banks_free, 1)
                        dve.wait_ge(gate_done, n0 + n + 1)
                        V.tensor_tensor(h32[:, s, :], act_out[:, s, :], h32[:, s, :],
                                        ALU.mult).then_inc(SIG["rms_up"], 1)
                    dve.wait_ge(h_hi_done, n0 + n + 1)
                    V.tensor_tensor(h_lo[:, bass.ds(n, 1), :], h32[:, s:s + 1, :], h_hi[:, bass.ds(n, 1), :],
                                    ALU.subtract).then_inc(h_done, 1)
                pairs(f"up{f}", post)

            def is_last(phase, i, j):
                per_pair = 4 if phase[0] == "d" else 2
                return isinstance(i, int) and per_pair * i + j == UNITS[phase] - 1

            def clear_acc(name, *read):
                dve.wait_ge(*read)
                V.memset(acc[:, :, :, :], 0.0).then_inc(acc_done, 1)
                dve.wait_ge(acc_done, ACC0[name] + 1)

            def fold_acc(which):
                V.tensor_tensor(acc[:, which, 0, :], acc[:, which, 0, :], acc[:, which, 1, :],
                                ALU.add).then_inc(acc_done, 1)

            def end_rms(phase):
                u0, down = UNIT0[phase], phase[0] == "d"

                def post(i, j):
                    if down and j % 2 == 0:
                        return
                    n = 2 * i + (j // 2 if down else j)
                    dve.wait_ge(sq_done, SQ0[phase] + n + 1)
                    dve.wait_ge(y_copied, YC0[phase] + (n + 1 if down else 2 * n + 2))
                    if is_last(phase, i, j):
                        dve.sem_inc(banks_free, 2 if down else 1)
                        return
                    dve.wait_ge(banks_free, u0 + (4 * i + 2 * (j // 2) if down else 2 * i + j) + 2)
                    if down:
                        V.tensor_tensor(acc[:, 1, 0, :], acc[:, 1, 0, :], sq[:, 0, :],
                                        ALU.add).then_inc(banks_free, 2)
                    else:
                        V.tensor_tensor(acc[:, 1, :, :], acc[:, 1, :, :], sq[:, :, :],
                                        ALU.add).then_inc(banks_free, 1)
                        if is_last(phase, i, j + 1):
                            dve.wait_ge(banks_free, free_at(u0 + UNITS[phase] - 2))
                            fold_acc(slice(1, 2))
                pairs(phase, post, 4 if down else 2)

            def end_ln(phase):
                u0, down = UNIT0[phase], phase[0] == "d"

                def post(i, j):
                    if down and j % 2 == 0:
                        return
                    n = 2 * i + (j // 2 if down else j)
                    dve.wait_ge(gemm_done, 2 * u0 + (8 if down else 4) * i + (2 * j + 6))
                    if down:
                        xs, ys, par = x[:, bass.ds(n, 1), :], bank[:, 4 + j // 2:5 + j // 2, :], slice(0, 1)
                    else:
                        xs, ys, par = x[:, bass.ds(2 * n, 2), :], bank[:, 2 * j:2 * j + 2, :], slice(0, 2)
                    V.scalar_tensor_tensor(xs, xs, ALPHA, ys, ALU.mult, ALU.add).then_inc(banks_free, 2 if down else 1)
                    if is_last(phase, i, j):
                        return
                    dve.wait_ge(banks_free, u0 + (4 if down else 2) * i + (j + 3))
                    dve.wait_ge(acc_done, ACC0[phase] + 2 * n + 1)
                    V.tensor_tensor(acc[:, 0, par, :], acc[:, 0, par, :], xs, ALU.add).then_inc(acc_done, 1)
                    dve.wait_ge(sq_done, SQ0[phase] + n + 1)
                    V.tensor_tensor(acc[:, 1, par, :], acc[:, 1, par, :],
                                    sq[:, 0:1, :] if down else sq[:, :, :], ALU.add).then_inc(acc_done, 1)
                    if not down and is_last(phase, i, j + 1):
                        dve.wait_ge(acc_done, ACC0[phase] + 2 * n + 3)
                        fold_acc(slice(0, 2))
                pairs(phase, post, 4 if down else 2)

            def spread(column, j):
                V.tensor_tensor(diag[:, j, :, :], ident[:, :].unsqueeze(1).broadcast_to([P, NT, P]),
                                column.unsqueeze(2).broadcast_to([P, NT, P]), ALU.mult).then_inc(scale_col, 1)

            def inverse_root(name):
                dve.wait_ge(stat_a, ST0[name] + 1)
                link(V.reciprocal(stat[:, 8:12], stat[:, 8:12]))
                spread(stat[:, 8:12], 0)
                dve.wait_ge(scale_bc, SC0[name] + 1)

            def residual(name, y, then=lambda k: None, ahead=None):
                for k in range(KD):
                    if k == 3 and ahead:
                        split_ahead(ahead)
                    ins = V.tensor_tensor(y[:, k, :], y[:, k, :], bank[:, 6, :], ALU.mult)
                    if k % 2:
                        ins.then_inc(norm_t, 1)
                    else:
                        link(ins)
                        V.tensor_tensor(x[:, k, :], x[:, k, :], y[:, k, :], ALU.add).then_inc(x_dve, 1)
                    if k >= 2:
                        then(k - 2)
                then(KD - 2)
                then(KD - 1)

            def scaled_low(gen, g0, k):
                dve.wait_ge(a_hi_done, gen_at(gen, k))
                V.scalar_tensor_tensor(a_lo[:, k, :], x[:, k, :], vec[:, g0 + k:g0 + k + 1], a_hi[:, k, :],
                                       ALU.mult, ALU.subtract).then_inc(a_odd if k % 2 else a_even, 1)

            def take_scale(name):
                inverse_root(name)
                link(V.tensor_copy(scale[:, :], bank[:, 7, :]))

            def normalise(gen, g0):
                def low(k):
                    dve.wait_ge(a_hi_done, gen_at(gen, k))
                    V.tensor_tensor(a_lo[:, k, :], buf(k), a_hi[:, k, :], ALU.subtract).then_inc(a_even, 1)
                for k in range(KD):
                    if k >= 4:
                        dve.wait_ge(*low_at(gen, k - 4))
                    V.scalar_tensor_tensor(buf(k), x[:, k, :], vec[:, g0 + k:g0 + k + 1], bank[:, 7, :],
                                           ALU.mult, ALU.mult).then_inc(norm_t, 1)
                    if k % 2 and k >= 1:
                        low(k - 1)

            def ln_columns(name, kv=None):
                n = LN_ENDS.index(name)
                dve.wait_ge(stats, STAT_N[name])
                link(V.tensor_scalar(stat[:, 0:8], bank[:, 6, 0:2 * NT], 1.0 / D, None, ALU.mult))
                link(V.tensor_tensor(stat[:, 8:12], stat[:, 0:4], stat[:, 0:4], ALU.mult))
                link(V.tensor_tensor(stat[:, 8:12], stat[:, 4:8], stat[:, 8:12], ALU.subtract))
                V.tensor_scalar(stat[:, 8:12], stat[:, 8:12], 0.0, None, ALU.max).then_inc(stat_v, 1)
                dve.wait_ge(stat_a, ST0[name] + 1)
                link(V.reciprocal(stat[:, 8:12], stat[:, 8:12]))
                spread(stat[:, 8:12], 0)
                link(V.scalar_tensor_tensor(stat[:, 0:4], stat[:, 0:4], -1.0, stat[:, 8:12], ALU.mult, ALU.mult))
                spread(stat[:, 0:4], 1)
                if kv:
                    split_next(kv + 1)
                elif NEXT[name]:
                    split_ahead(NEXT[name])
                dve.wait_ge(scale_bc, SC0[name] + 2)

            def ln_norm(name, k):
                if k >= 4:
                    dve.wait_ge(x_act, XACT0[name] + k - 3)
                link(V.tensor_tensor(buf(k), x[:, k, :], bank[:, 6, :], ALU.mult))
                V.tensor_tensor(buf(k), buf(k), bank[:, 7, :], ALU.add).then_inc(norm_t, 1)

            def ln_low(name, k):
                if NEXT[name] and k % 2 == 0:
                    dve.wait_ge(a_hi_done, gen_at(NEXT[name], k))
                    dve.wait_ge(x_act, XACT0[name] + k + 1)
                    V.tensor_tensor(a_lo[:, k, :], x[:, k, :], a_hi[:, k, :], ALU.subtract).then_inc(a_even, 1)

            def low_parts(gen, srcs, ks=(0, 2, 4, 6)):
                for k in ks:
                    dve.wait_ge(a_hi_done, gen_at(gen, k))
                    V.tensor_tensor(a_lo[:, k, :], srcs(k), a_hi[:, k, :], ALU.subtract).then_inc(a_even, 1)

            def mlstm_args(h):
                dve.wait_ge(SIG["mlstm_m_mm"], h + 1)
                if h:
                    dve.wait_ge(SIG["mlstm_den_mm"], h)
                for s in range(NT):
                    V.tensor_scalar(mp[:, s * T + s * P:(s + 1) * T], bank[:, 4, s * P:T],
                                    ct[:, 0, s, h:h + 1], 0.0, ALU.add, ALU.min).then_inc(SIG["mlstm_arg"], 1)

            def mlstm_probs(h):
                for i, s in enumerate((0, 1, 3, 2)):
                    b, c0 = SCORE_AT[s]
                    dve.wait_ge(SIG["mlstm_scores_mm"], 4 * h + (1, 3, 3, 4)[i])
                    dve.wait_ge(SIG["mlstm_weight"], 4 * h + s + 1)
                    V.scalar_tensor_tensor(mp[:, s * T + s * P:(s + 1) * T], bank[:, b, c0:c0 + T - s * P], 64.0 ** -0.5,
                                           mp[:, s * T + s * P:(s + 1) * T], ALU.mult, ALU.mult
                                           ).then_inc(SIG["mlstm_p"], 1)
                dve.wait_ge(SIG["mlstm_p"], 4 * h + NT)
                diags = mp[:, :].rearrange("p (s c) -> p s c", s=NT)[:, :, 0:P]
                V.tensor_tensor(diags, diags, tri[:, 0:1, :].broadcast_to([P, NT, P]),
                                ALU.mult).then_inc(SIG["mlstm_masked"], 1)

            def mlstm_scale(h):
                den, scale = mcol[:, 2, :], mcol[:, 3, :]
                dve.wait_ge(SIG["mlstm_den_mm"], h + 1)
                link(V.tensor_scalar(den, bank[:, 6, 0:NT], -1.0, None, ALU.mult))
                link(V.tensor_tensor(den, den, bank[:, 6, 0:NT], ALU.max))
                link(V.tensor_tensor(den, den, ct[:, 1, :, h], ALU.max))
                link(V.reciprocal(den, den))
                link(V.tensor_tensor(mcol[:, 1, :], den, den, ALU.mult))
                dve.wait_ge(SIG["mlstm_square"], 4 * h + 4)
                V.tensor_tensor(mcol[:, 1, :], mcol[:, 1, :], mcol[:, 0, :], ALU.mult).then_inc(SIG["mlstm_ms"], 1)
                dve.wait_ge(SIG["mlstm_rms"], h + 1)
                link(V.reciprocal(scale, mcol[:, 1, :]))
                link(V.tensor_tensor(scale, scale, den, ALU.mult))
                if h:
                    dve.wait_ge(SIG["mlstm_turned"], h)
                V.tensor_tensor(mtmp[:, 0, :].rearrange("p (n v) -> p n v", n=NT),
                                bank[:, 5, :].rearrange("p (n v) -> p n v", n=NT),
                                scale.unsqueeze(2).broadcast_to([P, NT, P]), ALU.mult).then_inc(SIG["mlstm_scaled"], 1)

            def mlstm_gated(h):
                dve.wait_ge(SIG["mlstm_turned"], h + 1)
                c0 = VCOL["mlstm_norm"] + h
                V.scalar_tensor_tensor(mgate[:, h, :], bank[:, 7, :], vec[:, c0:c0 + 1], mgate[:, h, :],
                                       ALU.mult, ALU.mult).then_inc(SIG["mlstm_y"], 1)

            V.memset(ones[:, :], 1.0)
            V.memset(eps6, 1e-6)
            V.memset(eps5, 1e-5)
            V.memset(one, 1.0).then_inc(consts_v, 1)
            dve.sem_inc(w_split, SLOTS)
            dve.sem_inc(gemm_done, 4)
            dve.sem_inc(banks_free, 2)
            dve.wait_ge(consts, 48)
            link(V.tensor_scalar(half_g[:, :], vec[:, VCOL["norm_post"]:VCOL["norm_post"] + 24], 0.5, None, ALU.mult))
            split(0, 0, FULL)
            for k in range(KD):
                if k == 2:
                    split_ahead("up0")
                scaled_low("up0", VCOL["norm_pre"], k)
            take_scale("x0")
            up(0)
            clear_acc("down0", h_done, F0[0] + KF)
            end_rms("down0")
            inverse_root("down0")
            residual("down0", y_ff)
            split_ahead("mixin")
            inverse_root("pre_mixin")
            normalise("mixin", VCOL["norm_pre"] + 8)

            mi = UNIT0["mixin"]
            dve.wait_ge(mix_in[0], 16)
            dve.wait_ge(mix_in[1], 16)
            V.tensor_tensor(lb[:, 0, :], lbt[:, 0, :], lbt[:, 1, :], ALU.subtract)
            V.tensor_tensor(lb[:, 1, :], lbt[:, 1, :], lbt[:, 0, :], ALU.subtract).then_inc(SIG["lb_diff"], 1)
            dve.wait_ge(SIG["gate_w_hi"], 1)
            V.tensor_tensor(wg_lo[:, :, :], wg_raw[:, :, :], wg_hi[:, :, :], ALU.subtract).then_inc(SIG["gate_w_lo"], 1)
            dve.wait_ge(SIG["lb_sigmoid"], 1)
            cw = VCOL["conv_w"]
            for u in range(2):
                split_next(mi + u)
                for m in range(2):
                    t = 2 * u + m
                    dve.wait_ge(SIG["mconv_start"], t + 1)
                    for tap in (1, 2, 3):
                        ins = V.scalar_tensor_tensor(mqk[:, t, tap:T], bank[:, 2 * u + m, 0:T - tap],
                                                     vec[:, cw + 4 * (3 - tap) + t:cw + 4 * (3 - tap) + t + 1],
                                                     mqk[:, t, tap:T], ALU.mult, ALU.add)
                        if tap < 3:
                            link(ins)
                        else:
                            ins.then_inc(SIG["mconv_done"], 1)
                dve.wait_ge(SIG["mconv_done"], 2 * u + 1 + 1)
                dve.sem_inc(banks_free, 1)
            def value_unit(u):
                split_next(mi + u)
                dve.wait_ge(SIG["mlstm_v"], u - 1)
                dve.sem_inc(banks_free, 1)

            def scan(op):
                for n in range(9):
                    d = 1 << n
                    src, dst = rows[:, n % 2, :], rows[:, 1 - n % 2, :]
                    link(V.tensor_tensor(dst[:, 256:256 + T], src[:, 256:256 + T], src[:, 256 - d:256 - d + T], op))

            value_unit(2)
            V.memset(rows[:, :, 0:256], 0.0)
            dve.wait_ge(SIG["f_row_log"], 1)
            link(V.scalar_tensor_tensor(rows[:, 0, 256:256 + T], row_b[:, :], 0.0, row_t[:, :], ALU.min, ALU.subtract))
            scan(ALU.add)
            link(V.tensor_copy(row_b[:, :], rows[:, 1, 256:256 + T]))
            V.tensor_tensor(row_t[:, :], row_i[:, :], row_b[:, :], ALU.subtract).then_inc(SIG["c_row"], 1)
            value_unit(3)
            dve.wait_ge(SIG["c_row"], 1)
            link(V.tensor_scalar(rows[:, 0, 256:256 + T], row_t[:, :], 0.0, None, ALU.max))
            scan(ALU.max)
            V.tensor_scalar(row_nm[:, :], rows[:, 1, 256:256 + T], -1.0, None, ALU.mult).then_inc(SIG["neg_m_row"], 1)
            dve.wait_ge(SIG["neg_m_row"], 1)
            V.tensor_tensor(row_em[:, :], row_nm[:, :], row_b[:, :], ALU.subtract).then_inc(SIG["neg_bm_row"], 1)
            for u in (4, 5):
                split_next(mi + u)
                dve.wait_ge(SIG["mlstm_gate"], u - 4 + 1)
                dve.sem_inc(banks_free, 1)
            dve.wait_ge(SIG["c_columns_mm"], 1)
            V.tensor_copy(ct[:, :, :, :], bank[:, 5, 0:2 * NT * HEADS].rearrange("p (w s h) -> p w s h", w=2, h=HEADS)
                          ).then_inc(SIG["c_columns"], 1)
            dve.wait_ge(SIG["c_columns"], 1)
            for h in range(3):
                for j in range(2):
                    u = 6 + 2 * h + j
                    split_next(mi + u)
                    dve.wait_ge(SIG["hgrn_input"], 2 * h + j + 1)
                    dve.sem_inc(banks_free, 1)
                    if h == 0:
                        cols = slice(j * 256, (j + 1) * 256)
                        s4 = sigm[:, :, :, :].rearrange("p a t c -> p (a t) c")
                        link(V.tensor_tensor(s4, s4, lb[:, 1:2, cols].broadcast_to([P, NT, 256]), ALU.mult))
                        V.tensor_tensor(logf[:, :, cols], s4, lb[:, 0:1, cols].broadcast_to([P, NT, 256]),
                                        ALU.add).then_inc(SIG["forget_ready"], 1)
                    if j == 0:
                        mlstm_args(h)
                        if h:
                            mlstm_gated(h - 1)
                        mlstm_probs(h)
                    else:
                        mlstm_scale(h)
                if h == 0:
                    dve.wait_ge(SIG["forget_ready"], 2)
                    V.tensor_scalar(k_tm[:, :, :], logf[:, :, :], -1.0, 1.0, ALU.mult, ALU.add).then_inc(SIG["keys_tm"], 1)
            mlstm_args(3)
            mlstm_gated(2)
            mlstm_probs(3)
            split_next(mi + 12)
            mlstm_scale(3)
            mlstm_gated(3)

            dve.wait_ge(SIG["rest_decay"], 1)
            dve.wait_ge(SIG["keys_tm"], 1)
            V.tensor_tensor(kdec[:, :, :], k_tm[:, :, :], lev[0][:, :, :], ALU.mult).then_inc(SIG["keys_decayed"], 1)
            dve.wait_ge(SIG["q_decay"], 1)
            link(V.tensor_tensor(q_dec[:, :, :], q_dec[:, :, :], q_fm[:, :, :], ALU.mult))
            link(V.memset(scores[:, :, :], 0.0))

            def level_mul(l):
                hs = LEVELS[l]
                d = blocks(lev[l % 3], hs)
                dve.wait_ge(SIG["level_exp"], l + 1)
                V.tensor_tensor(d[:, :, 1, :], d[:, :, 1, :], blocks(q_fm, hs)[:, :, 1, :], ALU.mult)
                V.tensor_tensor(d[:, :, 0, :], d[:, :, 0, :], blocks(k_fm, hs)[:, :, 0, :], ALU.mult).then_inc(SIG["level_ready"], 1)

            def take_scores(l):
                dve.wait_ge(SIG["level_scores_mm"], l + 1)
                if l:
                    dve.wait_ge(SIG["scores_taken"], l)
                b = 4 * (l > 0)
                V.copy_predicated(scores[:, :, :].rearrange("p h (n c) -> p (h n) c", c=P),
                                  masks[:, l:l + 1, :].broadcast_to([P, HEADS * NT, P]),
                                  bank[:, b:b + 4, :].rearrange("p h (n c) -> p (h n) c", c=P)
                                  ).then_inc(SIG["scores_taken"], 1)

            dve.wait_ge(SIG["state_add_mm"], 1)
            link(V.tensor_copy(states[:, 0, :, :], bank[:, 4, :].rearrange("p (h v) -> p h v", h=HEADS)))
            dve.wait_ge(SIG["chunk_decay"], 1)
            for n in (1, 2):
                for h in range(HEADS):
                    ins = V.scalar_tensor_tensor(states[:, n, h, :], states[:, n - 1, h, :],
                                                 g_end[:, h * NT + n:h * NT + n + 1],
                                                 bank[:, 4 + n, h * P:(h + 1) * P], ALU.mult, ALU.add)
                    if h == HEADS - 1 and n == 1:
                        link(ins)
            ins.then_inc(SIG["states_ready"], 1)
            dve.wait_ge(mask_in, 16)
            level_mul(0)
            for l in range(1, len(LEVELS)):
                take_scores(l - 1)
                level_mul(l)
                if l == 5:
                    dve.wait_ge(SIG["hgrn_input"], 7)
                    dve.sem_inc(banks_free, 1)
                    split_next(mi + 13)
            take_scores(len(LEVELS) - 1)
            take_scores(len(LEVELS))
            dve.wait_ge(SIG["hgrn_input"], 8)
            dve.sem_inc(banks_free, 1)
            for n in range(NT):
                dve.wait_ge(SIG["hgrn_square"], n + 1)
                ins = V.tensor_reduce(hcol[:, n, :], lev[1][:, n, :].rearrange("p (h v) -> p h v", h=HEADS), AX.X, ALU.add)
            ins.then_inc(SIG["hgrn_ms"], 1)
            dve.wait_ge(SIG["hgrn_rms"], 1)
            link(V.reciprocal(hcol[:, :, :], hcol[:, :, :]))
            for n in range(NT):
                V.tensor_tensor(lev[0][:, n, :].rearrange("p (h v) -> p h v", h=HEADS),
                                bank[:, n, :].rearrange("p (h v) -> p h v", h=HEADS),
                                hcol[:, n, :].unsqueeze(2).broadcast_to([P, HEADS, P]),
                                ALU.mult).then_inc(SIG["hgrn_scaled"], 1)
            low_parts("mixout", lambda k: mgate[:, k - HEADS, :], (4, 6))
            split_ahead("mixout")
            dve.wait_ge(SIG["hgrn_turned"], 1)
            for h in range(HEADS):
                c0 = VCOL["hgrn_norm"] + h
                V.scalar_tensor_tensor(hgate[:, h, :], bank[:, 4 + h, :], vec[:, c0:c0 + 1], hgate[:, h, :],
                                       ALU.mult, ALU.mult).then_inc(SIG["hgrn_y"], 1)
            low_parts("mixout", lambda k: hgate[:, k, :], (0, 2))
            clear_acc("mixout", *low_at("mixout", 2))
            end_rms("mixout")
            inverse_root("mixout")
            residual("mixout", y_mix, lambda k: scaled_low("up1", VCOL["norm_pre"] + 16, k), "up1")
            take_scale("pre_up1")
            up(1)
            clear_acc("down1", h_done, F0[1] + KF)
            end_rms("down1")
            inverse_root("down1")
            residual("down1", y_ff, lambda k: low_parts("ab", lambda k: x[:, k, :], (k,)[k % 2:]), "ab")

            ab = UNIT0["ab"]
            for u in range(2):
                split_next(ab + u)
                dve.wait_ge(SIG["sgu_v"], u + 1)
                dve.sem_inc(banks_free, 1)
            for t in range(NT):
                link(V.bn_stats(bn[:, t, :], gv[:, t, :]))
                V.bn_aggr(mv4[:, t, :], bn[:, t, :]).then_inc(SIG["sgu_stats"], 1)
            for u in (2, 3):
                split_next(ab + u)
                dve.wait_ge(SIG["pool_in"], u - 2 + 1)
                dve.sem_inc(banks_free, 1)
            for n in range(3):
                V.memset(pool[n][:, :, 0:PAD], 0.0)
            dve.wait_ge(SIG["sgu_std"], 1)
            link(V.reciprocal(rs4[:, :], rs4[:, :]))
            for t in range(NT):
                ins = V.tensor_scalar(gv[:, t, :], gv[:, t, :], mv4[:, t, 0:1], rs4[:, t:t + 1], ALU.subtract, ALU.mult)
            link(ins)
            for n in range(4):
                dve.wait_ge(ab_in[n], 16)
            link(V.tensor_tensor(gv[:, :, :], gv[:, :, :], ab_rows[:, 0:1, :].broadcast_to([P, NT, T]), ALU.mult))
            V.memset(ws_t[64:128, :, 0:64], 0.0)
            V.tensor_tensor(gv[:, :, :], gv[:, :, :], ab_rows[:, 1:2, :].broadcast_to([P, NT, T]),
                            ALU.add).then_inc(SIG["sgu_v_ready"], 1)
            split_next(ab + 4)
            for g in range(4):
                src = pool[0]
                for n in range(g + 1):
                    dst = pool[1 + n % 2]
                    link(V.tensor_tensor(dst[:, g, PAD:PAD + T], src[:, g, PAD:PAD + T],
                                         src[:, g, PAD - (1 << n):PAD - (1 << n) + T], ALU.add))
                    src = dst
                first, rest = slice(PAD, 2 * PAD), slice(2 * PAD, PAD + T)
                link(V.tensor_tensor(src[:, g, first], src[:, g, first], inv_cnt[:, g, :], ALU.mult))
                V.tensor_tensor(pool[2][:, g, first], src[:, g, first], pool[0][:, g, first], ALU.subtract)
                V.scalar_tensor_tensor(pool[2][:, g, rest], src[:, g, rest], 1.0 / (2 << g), pool[0][:, g, rest],
                                       ALU.mult, ALU.subtract).then_inc(SIG["pooled"], 1)
            dve.wait_ge(SIG["sgu_u"], 1)
            dve.sem_inc(banks_free, 1)
            for g in range(4):
                dve.wait_ge(SIG["pool_mm"], g + 1)
                c0 = VCOL["pool_scale_2"] + g
                V.tensor_scalar(pool[1][:, g, PAD:PAD + T], bank[:, 4 + g, :], vec[:, c0:c0 + 1], None,
                                ALU.mult).then_inc(SIG["ab_yb"], 1)
            dve.wait_ge(SIG["mem_hi_done"], 1)
            V.tensor_tensor(mem_lo[:, :, :], mem_raw[:, :, :], mem_hi[:, :, :], ALU.subtract).then_inc(SIG["mem_lo_done"], 1)
            split_next(ab + 5)
            dve.wait_ge(SIG["sgu_u"], 2)
            dve.sem_inc(banks_free, 1)
            low_parts("about", lambda k: pool[1][:, k - 4, PAD:PAD + T], (4, 6))
            split_ahead("about")
            for g in range(4):
                dve.wait_ge(SIG["spatial_mm"], g + 1)
                b4 = bank[:, 4 + g, :].rearrange("p (n c) -> p n c", c=P)
                gate = pool[0][:, g, PAD:PAD + T]
                o4 = gate.rearrange("p (n c) -> p n c", c=P)
                link(V.tensor_tensor(o4, b4, ab_rows[:, 2:3, g * P:(g + 1) * P].broadcast_to([P, NT, P]), ALU.add))
                V.tensor_tensor(ug[:, g, :], ug[:, g, :], gate, ALU.mult).then_inc(SIG["ab_ya"], 1)
            low_parts("about", lambda k: ug[:, k, :], (0, 2))
            for layer in range(2):
                if layer == 1:
                    ci, cw = UNIT0["cin"], VCOL["c_conv_w_2"]
                    dve.wait_ge(SIG["mem_hi_done"], 2)
                    V.tensor_tensor(mem_lo[:, :, :], mem_raw[:, :, :], mem_hi[:, :, :],
                                    ALU.subtract).then_inc(SIG["mem_lo_done"], 1)
                    for u in range(12):
                        split_next(ci + u)
                        b = 2 * (u % 2)
                        if u < 8:
                            dve.wait_ge(SIG["c_gate"], u + 1)
                            dve.wait_ge(gemm_done, gemm_at(ci + u))
                            V.tensor_tensor(ch[:, u % 2, :], cc[:, u % 2, :], bank[:, b + 1, :],
                                            ALU.mult).then_inc(SIG["c_product"], 1)
                            dve.wait_ge(SIG["c_product"], u + 1)
                            dve.sem_inc(banks_free, 1)
                            dve.wait_ge(SIG["c_conv_start"], u + 1)
                            for tap in (1, 2):
                                c0 = cw + 8 * (2 - tap) + u
                                link(V.scalar_tensor_tensor(yc[:, u, tap:T], ch[:, u % 2, 0:T - tap],
                                                            vec[:, c0:c0 + 1], yc[:, u, tap:T], ALU.mult, ALU.add))
                        else:
                            j = 2 * (u - 8)
                            dve.wait_ge(gemm_done, gemm_at(ci + u))
                            V.tensor_tensor(yc[:, j:j + 2, :], yc[:, j:j + 2, :], bank[:, b:b + 2, :],
                                            ALU.mult).then_inc(SIG["c_y"], 1)
                            dve.wait_ge(SIG["c_y"], u - 8 + 1)
                            dve.sem_inc(banks_free, 1)
                    low_parts("cout", lambda k: yc[:, k, :], (0,))
                    split_ahead("cout")
                    low_parts("cout", lambda k: yc[:, k, :], (2, 4, 6))
                end = ("about", "cout")[layer]
                clear_acc(end, *low_at(end, 2 if end == "about" else 6))
                end_ln(end)
                kv = UNIT0[f"kv{layer}"]
                split_ahead(f"kv{layer}")
                ln_columns(end, kv)
                ln_norm(end, 0)
                for k in range(KD):
                    dve.wait_ge(SIG["mem_kv"], 8 * layer + k + 1)
                    dve.sem_inc(banks_free, 1)
                    if 1 <= k < KD - 1:
                        split_next(kv + k + 1)
                    if k == KD - 1:
                        split_ahead(f"q{layer}")
                    if k + 1 < KD:
                        ln_norm(end, k + 1)
                    ln_low(end, k)
                q0 = UNIT0[f"q{layer}"]
                for u in range(4):
                    split_next(q0 + u)
                    dve.wait_ge(SIG["attn_q"], 4 * layer + u + 1)
                    dve.sem_inc(banks_free, 1)
                split_ahead(f"wo{layer}")

                def score_max(h):
                    p, b = h % 2, 2 * (h % 2)
                    dve.wait_ge(SIG["attn_scores_mm"], 4 * layer + h + 1)
                    link(V.tensor_reduce(at_s[:, p, 0, :], bank[:, b:b + 2, :].rearrange("p b (t m) -> p (b t) m", t=2),
                                         AX.X, ALU.max))
                    V.tensor_scalar(at_s[:, p, 1, :], at_s[:, p, 0, :], -(256.0 ** -0.5), None,
                                    ALU.mult).then_inc(SIG["attn_max"], 1)

                def divide(h):
                    p = h % 2
                    dve.wait_ge(SIG["attn_exp"], 16 * layer + 4 * h + 4)
                    link(V.reciprocal(at_s[:, p, 0, :], at_s[:, p, 2, :]))
                    V.tensor_tensor(pe_at[:, p, :, :], pe_at[:, p, :, :],
                                    at_s[:, p, 0, :].unsqueeze(2).broadcast_to([P, NT, MEM]),
                                    ALU.mult).then_inc(SIG["attn_probs"], 1)
                score_max(0)
                score_max(1)
                divide(0)
                divide(1)
                for g in range(HEADS):
                    if g + 2 < HEADS:
                        dve.wait_ge(SIG["attn_probs"], 4 * layer + g + 1)
                        score_max(g + 2)
                        divide(g + 2)
                    dve.wait_ge(SIG["attn_out_mm"], 4 * layer + g + 1)
                    if g:
                        dve.wait_ge(*low_at(f"wo{layer}", 2 * g - 2))
                        dve.wait_ge(*low_at(f"wo{layer}", 2 * g - 1))
                    V.tensor_copy(o32[:, :, :], bank[:, 6:8, :]).then_inc(SIG["attn_o32"], 1)
                    dve.wait_ge(a_hi_done, gen_at(f"wo{layer}", 2 * g))
                    V.tensor_tensor(a_lo[:, 2 * g, :], o32[:, 0, :], a_hi[:, 2 * g, :],
                                    ALU.subtract).then_inc(a_even, 1)
                end = f"wo{layer}"
                for end in (f"wo{layer}", f"down{2 + layer}"):
                    if end[0] == "d":
                        up(2 + layer)
                    clear_acc(end, *((h_done, F0[2 + layer] + KF) if end[0] == "d" else low_at(end, 6)))
                    end_ln(end)
                    ln_columns(end)
                    ln_norm(end, 0)
                    for k in range(KD):
                        if k + 1 < KD:
                            ln_norm(end, k + 1)
                        ln_low(end, k)


def kernel(**inputs):
    import numpy as np
    import concourse.bacc as bacc
    from concourse.bass_utils import run_bass_kernel_spmd

    def tiles(w, order):
        n = w.shape[1] // P
        w = w.reshape(KD, P, n, P).transpose(2, 1, 0, 3)[np.asarray(order)]
        return w.reshape(len(order) // 2, 2, P, KD * P).transpose(0, 2, 1, 3).reshape(-1, P, FULL)

    def columns(w, first, n):
        w = w[:, first:first + 256 * n]
        return w.reshape(KD, P, n, 256).transpose(2, 1, 0, 3).reshape(n, P, FULL)

    def down(w):
        return w.reshape(2, HALF_KF, P, KD, P).transpose(3, 0, 2, 1, 4).reshape(16, P, DOWN)

    def both(first, second):
        return [t for j in range(KF) for t in (first + j, second + j)]

    i = inputs
    mix, ab, cin = i["w_mix_in"][0], i["ab_w_in_2"][0], i["c_w_in_2"][0]
    full = [tiles(i["ffn1_w_in"][0], both(0, KF)),
            tiles(mix[:, :3584], [16, 17, 18, 19]), columns(mix, 2560, 2), tiles(mix[:, :3584], [24, 25, 26, 27]),
            columns(mix, 512, 2), columns(mix, 1024, 2),
            tiles(mix[:, :3584], [0, 1, 2, 3]), tiles(mix[:, :3584], [12, 13, 14, 15]),
            tiles(i["w_mix_out"][0], range(KD)),
            tiles(i["ffn2_w_in"][0], both(0, KF)),
            columns(ab, 512, 2), tiles(ab, [8, 9, 10, 11, 0, 1, 2, 3]), tiles(i["ab_w_out_2"][0], range(KD))]
    for layer in range(2):
        wkv = i["xa_wkv_2"][layer]
        if layer:
            full += [tiles(cin, [t for j in range(8) for t in (8 + j, 16 + j)] + list(range(8))),
                     tiles(i["c_w_out_2"][0], range(KD))]
        full += [tiles(wkv[:, :D], range(KD)), columns(wkv, D, 4), tiles(i["xa_wq_2"][layer], range(KD)),
                 tiles(i["xa_wo_2"][layer], range(KD)), tiles(i["ffn_w_up_2"][layer], both(KF, 0))]

    def vector(w):
        return np.asarray(w).reshape(-1, P).T

    steps = np.arange(P)
    s, t = steps[:, None], steps[None, :]
    masks = [s == t] + [(s // (2 * h) == t // (2 * h)) & (s // h % 2 == 0) & (t // h % 2 == 1) for h in LEVELS]
    counts = np.stack([1.0 / np.minimum(np.arange(16) + 1, 2 << g) for g in range(4)])

    def every(w):
        return np.broadcast_to(w, (P,) + w.shape)

    w_gates = np.zeros((D, P), np.float32)
    w_gates[:, 0:HEADS], w_gates[:, 32:32 + HEADS] = mix[:, 3584:3588], mix[:, 3588:3592]
    arrays = {
        "w_full": np.concatenate(full), "w_down": np.concatenate(
            [down(w) for w in (i["ffn1_w_out"][0], i["ffn2_w_out"][0], i["ffn_w_down_2"][0], i["ffn_w_down_2"][1])]),
        "vectors": np.concatenate([vector(i[n]) for n, _ in VECTORS], axis=1),
        "identity": np.eye(P, dtype=np.float32),
        "x": i["x"][0].T.reshape(KD, P, T).transpose(1, 0, 2),
        "w_gates": w_gates.reshape(KD, P, P).transpose(1, 0, 2),
        "gate_bias": i["mlstm_gate_bias"].reshape(2, HEADS).T,
        "sel": np.repeat(np.eye(HEADS, dtype=np.float32)[:, :, None], P, axis=2),
        "tri": np.stack([s <= t, s > t], axis=1).astype(np.float32),
        "masks": np.stack(masks, axis=1).astype(np.uint32),
        "lb_rows": every(i["hgrn_lb_logits"]),
        "ab_rows": every(np.stack([i["sgu_ln_g_2"][0], i["sgu_ln_b_2"][0], i["sgu_b_2"][0].reshape(-1)])),
        "ws_t": i["sgu_w_2"][0].transpose(2, 0, 1),
        "pool_w": i["pool_w_2"][0].transpose(1, 0, 2),
        "inv_cnt": every(counts.astype(np.float32)),
        "mem": i["mem_2"][0].T.reshape(KD, P, MEM).transpose(1, 0, 2),
    }
    arrays = {n: np.ascontiguousarray(v) for n, v in arrays.items()}
    nc = bacc.Bacc("TRN2", target_bir_lowering=False, num_devices=1)
    aps = {n: nc.dram_tensor(n, v.shape, mybir.dt.from_np(v.dtype), kind="ExternalInput").ap()
           for n, v in arrays.items()}
    aps["out"] = nc.dram_tensor("out", (P, KD, T), mybir.dt.float32, kind="ExternalOutput").ap()
    build(nc, aps)
    r = run_bass_kernel_spmd(nc, [arrays], core_ids=[0])
    y = r.results[0]["out"]
    return np.ascontiguousarray(y.transpose(1, 0, 2).reshape(D, T).T)[None]
```
